# Optimizing a Trainium2 kernel written in Bass

```python
import math
import jax, jax.numpy as jnp
from jax import lax
import numpy as np

D_MODEL = 1024
BATCH = 1
SEQ = 1024
DEPTH = 2

N_EVEN = (DEPTH + 1) // 2
N_ODD = DEPTH // 2

LRU_WIDTH = 512
LRU_BLOCKS = 8
LRU_BLOCK = LRU_WIDTH // LRU_BLOCKS
LRU_CONV = 4
LRU_C = 8.0

MLA_HEADS = 8
Q_LORA = 256
KV_LORA = 128
QK_NOPE = 64
QK_ROPE = 32
V_HEAD = 64
ROPE_THETA = 10000.0
Q_BLOCK = 128

EVEN_IN = 2 * LRU_WIDTH + Q_LORA + KV_LORA + QK_ROPE
EVEN_MIX = LRU_WIDTH + MLA_HEADS * V_HEAD

M_HEADS = 4
M_QK = 128
M_V = 256
M_CHUNK = 64
GATE_CAP = 15.0
ODD_IN = 2 * M_HEADS * M_QK + 2 * M_HEADS * M_V + 2 * M_HEADS
ODD_MIX = M_HEADS * M_V

D_FF = 2816
FFN_CONV = 3
EPS = 1e-6

kernel_name = "hybrid_rglru_mla_mlstm_convffn"

def rms_norm(x, g):
    xf = x.astype(jnp.float32)
    y = xf * lax.rsqrt(jnp.mean(xf * xf, axis=-1, keepdims=True) + EPS)
    return (y * g.astype(jnp.float32)).astype(x.dtype)

def causal_dwconv(x, w, b):
    k = w.shape[0]
    s = x.shape[1]
    xp = jnp.pad(x, ((0, 0), (k - 1, 0), (0, 0)))
    y = b
    for j in range(k):
        y = y + xp[:, j:j + s] * w[j]
    return y

def rope_cos_sin(positions):
    half = QK_ROPE // 2
    inv_freq = ROPE_THETA ** (-jnp.arange(half, dtype=jnp.float32) / half)
    ang = positions.astype(jnp.float32)[..., None] * inv_freq
    return jnp.cos(ang), jnp.sin(ang)

def apply_rope(x, cos, sin):
    x1, x2 = jnp.split(x.astype(jnp.float32), 2, axis=-1)
    return jnp.concatenate([x1 * cos - x2 * sin, x2 * cos + x1 * sin], axis=-1).astype(x.dtype)

def rg_lru(xr, gate, conv_w, conv_b, w_a, b_a, w_x, b_x, lam):
    bsz, s, _ = xr.shape
    xc = causal_dwconv(xr, conv_w, conv_b).astype(jnp.float32)
    xb = xc.reshape(bsz, s, LRU_BLOCKS, LRU_BLOCK)
    r = jax.nn.sigmoid(jnp.einsum("bsgi,gij->bsgj", xb, w_a.astype(jnp.float32)) + b_a).reshape(bsz, s, LRU_WIDTH)
    i = jax.nn.sigmoid(jnp.einsum("bsgi,gij->bsgj", xb, w_x.astype(jnp.float32)) + b_x).reshape(bsz, s, LRU_WIDTH)
    log_a = -LRU_C * r * jax.nn.softplus(-lam.astype(jnp.float32))
    a = jnp.exp(log_a)
    u = jnp.sqrt(-jnp.expm1(2.0 * log_a)) * (i * xc)

    def combine(left, right):
        a1, b1 = left
        a2, b2 = right
        return a1 * a2, a2 * b1 + b2

    _, h = lax.associative_scan(combine, (a, u), axis=1)
    return (h * jax.nn.gelu(gate.astype(jnp.float32))).astype(xr.dtype)

def causal_attention(q, k, v):
    bsz, s, h, dq = q.shape
    nb = s // Q_BLOCK
    qb = jnp.moveaxis(q.reshape(bsz, nb, Q_BLOCK, h, dq), 1, 0)
    key_idx = jnp.arange(s)
    neg = jnp.finfo(jnp.float32).min

    def one_block(args):
        blk, qi = args
        sc = jnp.einsum("bqhd,bkhd->bhqk", qi, k).astype(jnp.float32)
        q_idx = blk * Q_BLOCK + jnp.arange(Q_BLOCK)
        sc = jnp.where(key_idx[None, :] <= q_idx[:, None], sc, neg)
        p = jax.nn.softmax(sc, axis=-1).astype(v.dtype)
        return jnp.einsum("bhqk,bkhd->bqhd", p, v)

    out = lax.map(one_block, (jnp.arange(nb), qb))
    return jnp.moveaxis(out, 0, 1).reshape(bsz, s, h, v.shape[-1])

def mla(q_lat, kv_lat, k_rope, positions, q_norm_g, w_qb, kv_norm_g, w_kvb):
    bsz, s, _ = q_lat.shape
    q = (rms_norm(q_lat, q_norm_g) @ w_qb).reshape(bsz, s, MLA_HEADS, QK_NOPE + QK_ROPE)
    kv = (rms_norm(kv_lat, kv_norm_g) @ w_kvb).reshape(bsz, s, MLA_HEADS, QK_NOPE + V_HEAD)
    k_nope, v = kv[..., :QK_NOPE], kv[..., QK_NOPE:]
    cos, sin = rope_cos_sin(positions)
    q_pe = apply_rope(q[..., QK_NOPE:], cos[:, :, None, :], sin[:, :, None, :])
    k_pe = apply_rope(k_rope, cos, sin)
    scale = (QK_NOPE + QK_ROPE) ** -0.5
    q_full = jnp.concatenate([q[..., :QK_NOPE], q_pe], axis=-1) * scale
    k_full = jnp.concatenate([k_nope, jnp.broadcast_to(k_pe[:, :, None, :], (bsz, s, MLA_HEADS, QK_ROPE))], axis=-1)
    out = causal_attention(q_full, k_full, v)
    return out.reshape(bsz, s, MLA_HEADS * V_HEAD)

def even_mixer(h, positions, w_in, lru_conv_w, lru_conv_b, lru_w_a, lru_b_a, lru_w_x, lru_b_x, lru_lambda,
               q_norm_g, w_qb, kv_norm_g, w_kvb, w_out):
    z = h @ w_in
    c1 = LRU_WIDTH
    c2 = 2 * LRU_WIDTH
    c3 = c2 + Q_LORA
    c4 = c3 + KV_LORA
    xr, gate, q_lat, kv_lat, k_rope = jnp.split(z, [c1, c2, c3, c4], axis=-1)
    y_lru = rg_lru(xr, gate, lru_conv_w, lru_conv_b, lru_w_a, lru_b_a, lru_w_x, lru_b_x, lru_lambda)
    y_mla = mla(q_lat, kv_lat, k_rope, positions, q_norm_g, w_qb, kv_norm_g, w_kvb)
    return jnp.concatenate([y_lru, y_mla.astype(y_lru.dtype)], axis=-1) @ w_out

def chunk_view(t, nc):
    bsz, s, h = t.shape[:3]
    t = t.reshape(bsz, nc, M_CHUNK, h, *t.shape[3:])
    return jnp.moveaxis(t, (1, 3), (0, 2))

def mlstm(q, k, v, i_pre, f_pre):
    bsz, s, h, dk = q.shape
    dv = v.shape[-1]
    nc = s // M_CHUNK
    q = q * dk ** -0.5
    log_f = jax.nn.log_sigmoid(f_pre)
    causal = jnp.tril(jnp.ones((M_CHUNK, M_CHUNK), dtype=bool))

    def step(carry, inp):
        c_st, n_st, m_st = carry
        qc, kc, vc, ic, fc = inp
        b = jnp.cumsum(fc, axis=-1)
        d = jnp.where(causal, b[..., :, None] - b[..., None, :] + ic[..., None, :], -jnp.inf)
        inter = b + m_st[..., None]
        m_t = jnp.maximum(inter, jnp.max(d, axis=-1))
        w = jnp.exp(d - m_t[..., None])
        g = jnp.exp(inter - m_t)
        sc = jnp.einsum("bhtd,bhsd->bhts", qc, kc) * w
        num = g[..., None] * jnp.einsum("bhtd,bhde->bhte", qc, c_st) + jnp.einsum("bhts,bhse->bhte", sc, vc)
        den = g * jnp.einsum("bhtd,bhd->bht", qc, n_st) + jnp.sum(sc, axis=-1)
        h_out = num / jnp.maximum(jnp.abs(den), jnp.exp(-m_t))[..., None]
        b_last = b[..., -1]
        w_end = b_last[..., None] - b + ic
        m_new = jnp.maximum(b_last + m_st, jnp.max(w_end, axis=-1))
        g_end = jnp.exp(b_last + m_st - m_new)
        w_s = jnp.exp(w_end - m_new[..., None])
        c_new = g_end[..., None, None] * c_st + jnp.einsum("bhs,bhsd,bhse->bhde", w_s, kc, vc)
        n_new = g_end[..., None] * n_st + jnp.einsum("bhs,bhsd->bhd", w_s, kc)
        return (c_new, n_new, m_new), h_out

    init = (jnp.zeros((bsz, h, dk, dv), jnp.float32), jnp.zeros((bsz, h, dk), jnp.float32),
            jnp.zeros((bsz, h), jnp.float32))
    xs = (chunk_view(q, nc), chunk_view(k, nc), chunk_view(v, nc), chunk_view(i_pre, nc), chunk_view(log_f, nc))
    _, hs = lax.scan(step, init, xs)
    return jnp.moveaxis(hs, (0, 2), (1, 3)).reshape(bsz, s, h, dv)

def soft_cap(t):
    return GATE_CAP * jnp.tanh(t / GATE_CAP)

def odd_mixer(h, w_in, b_igate, b_fgate, out_norm_g, w_out):
    bsz, s, _ = h.shape
    z = (h @ w_in).astype(jnp.float32)
    c1 = M_HEADS * M_QK
    c2 = 2 * c1
    c3 = c2 + M_HEADS * M_V
    c4 = c3 + M_HEADS * M_V
    c5 = c4 + M_HEADS
    q, k, v, o, ig, fg = jnp.split(z, [c1, c2, c3, c4, c5], axis=-1)
    ig = soft_cap(ig + b_igate.astype(jnp.float32))
    fg = soft_cap(fg + b_fgate.astype(jnp.float32))
    hh = mlstm(q.reshape(bsz, s, M_HEADS, M_QK), k.reshape(bsz, s, M_HEADS, M_QK),
               v.reshape(bsz, s, M_HEADS, M_V), ig, fg)
    hh = hh * lax.rsqrt(jnp.mean(hh * hh, axis=-1, keepdims=True) + EPS)
    y = hh.reshape(bsz, s, ODD_MIX) * out_norm_g.astype(jnp.float32) * jax.nn.sigmoid(o)
    return y.astype(h.dtype) @ w_out

def conv_ffn(h, w_up, conv_w, conv_b, w_down):
    u = causal_dwconv(h @ w_up, conv_w, conv_b)
    g, val = jnp.split(u, 2, axis=-1)
    return (jax.nn.silu(g) * val) @ w_down

def setup_inputs(seed: int = 0) -> dict:
    key = jax.random.key(seed)
    ks = iter(jax.random.split(key, 40))

    def w(shape, fan_in):
        return jax.random.normal(next(ks), shape, jnp.float32) * fan_in ** -0.5

    def gain(shape):
        return 1.0 + 0.05 * jax.random.normal(next(ks), shape, jnp.float32)

    def bias(shape, scale=0.02):
        return scale * jax.random.normal(next(ks), shape, jnp.float32)

    x = jax.random.normal(next(ks), (BATCH, SEQ, D_MODEL), jnp.float32)
    positions = jnp.broadcast_to(jnp.arange(SEQ, dtype=jnp.int32)[None, :], (BATCH, SEQ))
    a_init = jax.random.uniform(next(ks), (N_EVEN, LRU_WIDTH), jnp.float32, minval=0.9, maxval=0.999)
    lru_lambda = jnp.log(a_init) - jnp.log1p(-a_init)
    return {
        "x": x,
        "positions": positions,
        "e_norm_g": gain((N_EVEN, D_MODEL)),
        "e_w_in": w((N_EVEN, D_MODEL, EVEN_IN), D_MODEL),
        "e_lru_conv_w": w((N_EVEN, LRU_CONV, LRU_WIDTH), LRU_CONV),
        "e_lru_conv_b": bias((N_EVEN, LRU_WIDTH)),
        "e_lru_w_a": w((N_EVEN, LRU_BLOCKS, LRU_BLOCK, LRU_BLOCK), LRU_BLOCK),
        "e_lru_b_a": bias((N_EVEN, LRU_BLOCKS, LRU_BLOCK)),
        "e_lru_w_x": w((N_EVEN, LRU_BLOCKS, LRU_BLOCK, LRU_BLOCK), LRU_BLOCK),
        "e_lru_b_x": bias((N_EVEN, LRU_BLOCKS, LRU_BLOCK)),
        "e_lru_lambda": lru_lambda,
        "e_q_norm_g": gain((N_EVEN, Q_LORA)),
        "e_w_qb": w((N_EVEN, Q_LORA, MLA_HEADS * (QK_NOPE + QK_ROPE)), Q_LORA),
        "e_kv_norm_g": gain((N_EVEN, KV_LORA)),
        "e_w_kvb": w((N_EVEN, KV_LORA, MLA_HEADS * (QK_NOPE + V_HEAD)), KV_LORA),
        "e_w_out": w((N_EVEN, EVEN_MIX, D_MODEL), EVEN_MIX),
        "o_norm_g": gain((N_ODD, D_MODEL)),
        "o_w_in": w((N_ODD, D_MODEL, ODD_IN), D_MODEL),
        "o_b_igate": bias((N_ODD, M_HEADS), 0.1),
        "o_b_fgate": 3.0 + 3.0 * jax.random.uniform(next(ks), (N_ODD, M_HEADS), jnp.float32),
        "o_out_norm_g": gain((N_ODD, ODD_MIX)),
        "o_w_out": w((N_ODD, ODD_MIX, D_MODEL), ODD_MIX),
        "f_norm_g": gain((DEPTH, D_MODEL)),
        "f_w_up": w((DEPTH, D_MODEL, 2 * D_FF), D_MODEL),
        "f_conv_w": w((DEPTH, FFN_CONV, 2 * D_FF), FFN_CONV),
        "f_conv_b": bias((DEPTH, 2 * D_FF)),
        "f_w_down": w((DEPTH, D_FF, D_MODEL), D_FF),
        "final_norm_g": gain((D_MODEL,)),
    }

def reference(x, positions, e_norm_g, e_w_in, e_lru_conv_w, e_lru_conv_b, e_lru_w_a, e_lru_b_a, e_lru_w_x,
              e_lru_b_x, e_lru_lambda, e_q_norm_g, e_w_qb, e_kv_norm_g, e_w_kvb, e_w_out, o_norm_g, o_w_in,
              o_b_igate, o_b_fgate, o_out_norm_g, o_w_out, f_norm_g, f_w_up, f_conv_w, f_conv_b, f_w_down,
              final_norm_g):
    h = x
    for layer in range(DEPTH):
        j = layer // 2
        if layer % 2 == 0:
            h = h + even_mixer(rms_norm(h, e_norm_g[j]), positions, e_w_in[j], e_lru_conv_w[j], e_lru_conv_b[j],
                               e_lru_w_a[j], e_lru_b_a[j], e_lru_w_x[j], e_lru_b_x[j], e_lru_lambda[j],
                               e_q_norm_g[j], e_w_qb[j], e_kv_norm_g[j], e_w_kvb[j], e_w_out[j])
        else:
            h = h + odd_mixer(rms_norm(h, o_norm_g[j]), o_w_in[j], o_b_igate[j], o_b_fgate[j],
                              o_out_norm_g[j], o_w_out[j])
        h = h + conv_ffn(rms_norm(h, f_norm_g[layer]), f_w_up[layer], f_conv_w[layer], f_conv_b[layer],
                         f_w_down[layer])
    return rms_norm(h, final_norm_g)


_drawn_inputs = setup_inputs


def setup_inputs(seed=0):
    import zlib

    import numpy as np

    out = dict(_drawn_inputs(seed))
    spreads = {}
    factors = {'e_lru_b_a': 64.0,
     'e_lru_b_x': 64.0,
     'e_q_norm_g': 7.891,
     'e_kv_norm_g': 5.581,
     'o_b_igate': 64.0,
     'e_lru_conv_b': 8.0,
     'e_lru_w_a': 3.303,
     'o_norm_g': 4.052,
     'o_out_norm_g': 8.0,
     'f_norm_g': 3.455,
     'f_conv_b': 8.0}
    for name, (base, spread) in spreads.items():
        noise = np.random.default_rng([zlib.crc32(name.encode()), seed]).standard_normal(out[name].shape)
        drawn = base * np.exp(spread * noise) if base else spread * noise
        out[name] = __import__('jax').numpy.asarray(drawn.astype(out[name].dtype))
    for name, factor in factors.items():
        out[name] = (out[name] * factor).astype(out[name].dtype)
    return out
```

```python
from contextlib import ExitStack

import numpy as np

import concourse.bass as bass
from concourse import mybir

ALU = mybir.AluOpType
ACT = mybir.ActivationFunctionType
F32 = mybir.dt.float32
F32R = mybir.dt.float32r
I32 = mybir.dt.int32
AX_X = mybir.AxisListType.X

P = 128
D = 1024
S = 1024
HALF = 512
KT = D // P
TT = S // P
EPS = 1e-6

LRU_W = 512
LRU_T = LRU_W // P
Q_LORA = 256
KV_LORA = 128
HEADS = 8
NOPE, ROPE, VH = 64, 32, 64
QK = NOPE + ROPE
QK_SCALE = float(QK) ** -0.5

MH, MQK, MV = 4, 128, 256
MVA = MV + 2
GATE_CAP = 15.0

D_FF = 2816
FT = D_FF // P
FG = FT // 2

RING = 4
STAGE = 2

T_L0_OUT = 2 * LRU_T + 4
T_FFN0 = T_L0_OUT + KT
T_L1 = T_FFN0 + 3 * FT
T_L1_V = T_L1 + 2 * MH
T_L1_O = T_L1_V + 8
T_L1_OUT = T_L1_O + KT
T_FFN1 = T_L1_OUT + KT
TILES = T_FFN1 + 3 * FT

_cols = {}
_n = 0
for _name, _w in [("e_g", KT), ("o_g", KT), ("f_g0", KT), ("f_g1", KT), ("fin_g", KT), ("q_g", Q_LORA // P),
                  ("kv_g", 1), ("lru", LRU_T * 8), ("out_g", KT), ("gate_b", TT * 8),
                  ("conv0", FT * 8), ("conv1", FT * 8)]:
    _cols[_name] = _n
    _n += _w
NPAR = _n

C_ID, C_ONE, C_TRI, C_MASKQ, C_MASKS, C_ROPE = 0, P, 2 * P, 3 * P, 4 * P, 5 * P
NCON = 5 * P + 8
TWO_PI = 2.0 * np.pi
RED1 = 6.28125
RED2 = float(np.float32(np.floor((TWO_PI - RED1) * 2 ** 18) / 2 ** 18))
RED3 = float(TWO_PI - RED1 - RED2)
MAGIC = 12582912.0
SIN_MAX = 3.1415925
BIG = 1e30


class Chain:

    def __init__(self, eng, sem):
        self.eng, self.sem, self.n, self.shift = eng, sem, 0, 0

    def link(self, ins):
        ins.then_inc(self.sem, 1)
        self.n += 1
        self.eng.wait_ge(self.sem, self.shift + self.n)

    def add(self, ins):
        ins.then_inc(self.sem, 1)
        self.n += 1
        return self.n

    def wait(self, n):
        self.eng.wait_ge(self.sem, self.shift + n)

    def enter(self, i, per):
        self.shift, self.start, self.per = i * per, self.n, per

    def leave(self, count):
        assert self.n - self.start == self.per, (self.n - self.start, self.per)
        self.n += self.per * (count - 1)
        self.shift = 0


def build(nc, wt, xt, pos, par, con, wqb, wkvb, wlru, wg, spill, out, upto=4):
    with ExitStack() as ctx:
        def psum(name, shape):
            return ctx.enter_context(nc.psum_tensor(name, shape, F32))

        sems = {}

        def sem(name):
            if name not in sems:
                sems[name] = ctx.enter_context(nc.semaphore(name))
            return sems[name]

        base = -(-nc.sbuf_base // 32) * 32
        room = (nc.sbuf_usable_end - base) // 32 * 32 - 32
        ctx.enter_context(nc.sbuf_tensor("arena", [P, room // 4], F32))
        KB = 1024

        def at(name, off, shape, dt=F32):
            size = int(np.prod(shape[1:])) * 4
            assert off + size <= room, (name, off, size, room)
            return nc.alloc_sbuf_tensor_at(name, shape, dt, offset=base + off)

        stage = at("stage", 0, [P, STAGE, 1024])
        whi = at("whi", 8 * KB, [P, RING, 1024], F32R)
        wlo = at("wlo", 24 * KB, [P, RING, 1024], F32R)
        ahi = at("ahi", 40 * KB, [P, KT, S], F32R)
        alo = at("alo", 72 * KB, [P, KT, S], F32R)
        c0 = 104 * KB
        cons = at("cons", c0, [P, NCON])
        c0 += NCON * 4
        pars = at("pars", c0, [P, NPAR])
        c0 += -(-NPAR * 4 // 32) * 32
        small = at("small", c0, [P, 96])
        c0 += 96 * 4
        nw = -(-c0 // 32) * 32
        sh = nw + 20 * KB
        sq = at("sq", nw, [P, 2, S])
        xnf = at("xnf", nw + 8 * KB, [P, 2, S])
        diag = at("diag", nw + 16 * KB, [P, S])
        sqb = at("sqb", sh, [P, 2, S])
        diagb = at("diagb", sh + 8 * KB, [P, S])
        hT = at("hT", sh, [P, KT, S])
        lr = at("lr", nw, [P, S])
        li = at("li", nw + 4 * KB, [P, S])
        lg = at("lg", nw + 8 * KB, [P, S])
        ls = at("ls", nw + 12 * KB, [P, S])
        lc = at("lc", nw + 16 * KB, [P, S])
        ylru = at("ylru", sh + 16 * KB, [P, LRU_T, S])
        xrp = at("xrp", sh + 32 * KB, [P, S + 3])
        xc = at("xc", sh + 36 * KB + 32, [P, S])
        pbuf = at("pbuf", nw, [P, 2, S])
        ptb = at("ptb", nw + 8 * KB, [P, 2, S])
        opair = at("opair", nw + 16 * KB, [P, TT, P])
        vtok = at("vtok", sh, [P, TT, HEADS * VH])
        qh = at("qh", sh + 16 * KB, [P, 2, S])
        kh = at("kh", sh + 24 * KB, [P, 2, S])
        rt1 = at("rt1", sh + 32 * KB, [P, S])
        rt2 = at("rt2", sh + 36 * KB + 32, [P, S])
        x0 = sh + 41 * KB
        lat = at("lat", x0, [P, 3, S])
        posi = at("posi", x0, [P, S], I32)
        kpe = at("kpe", x0 + 12 * KB, [P, S])
        tab = at("tab", x0 + 16 * KB, [P, S])
        wqb_s = at("wqb_s", x0 + 20 * KB, [P, 2, 1024])
        wlru_s = at("wlru_s", x0 + 20 * KB, [P, LRU_T, 2 * P])
        wlfix = at("wlfix", x0 + 24 * KB, [P, 2, 2 * P])
        wkvb_s = at("wkvb_s", x0 + 28 * KB, [P, 1024])
        wh = at("wh", x0 + 32 * KB, [P, 2, 3 * P])
        hid_hi = at("hid_hi", sh + 32 * KB, [P, 2, S], F32R)
        hid_lo = at("hid_lo", sh + 40 * KB, [P, 2, S], F32R)
        upg = at("upg", sh + 48 * KB, [P, S + 2])
        upv = at("upv", sh + 52 * KB + 32, [P, S + 2])
        cvg = at("cvg", sh + 56 * KB + 64, [P, S])
        cvv = at("cvv", sh + 60 * KB + 64, [P, S])
        vaug = at("vaug", sh, [P, TT, MH, MVA])
        q1 = sh + 33 * KB
        qT = at("qT", q1, [P, MH, S])
        kT = at("kT", q1 + 16 * KB, [P, MH, S])
        sigo = at("sigo", q1, [P, 2, HALF])
        m1 = q1 + 32 * KB
        cst = at("cst", m1, [P, MH, MVA])
        mw = at("mw", m1 + 4 * KB + 256, [P, 2, MH * P])
        ginfo = at("ginfo", m1 + 8 * KB + 256, [P, 640])
        gaT = at("gaT", m1 + 10 * KB + 768, [P, P])
        gAT = at("gAT", m1 + 11 * KB + 256, [P, P])
        gMT = at("gMT", m1 + 11 * KB + 768, [P, P])
        wghi = at("wghi", m1 + 12 * KB + 256, [P, KT * 8], F32R)
        wglo = at("wglo", m1 + 12 * KB + 512, [P, KT * 8], F32R)
        junk = at("junk", m1 + 12 * KB + 768, [P, MV])
        wgs = at("wgs", m1 + 4 * KB + 256, [P, KT * 8])
        gz, gt, gsp, ga, gnb = (ginfo[:, a:b] for a, b in ((0, 64), (64, 128), (128, 160), (160, 192), (192, 224)))
        gex = ginfo[:, 224:256]
        m_row, m_next, ml_row = ginfo[0:1, 256:288], ginfo[0:1, 260:292], ginfo[0:1, 292:324]
        g_exp = ginfo[:, 384:512]
        g_row = ginfo[0:1, 512:576]
        g_last = ginfo[0:32, 576:577]
        g_mcol = ginfo[0:32, 577:578]
        msw = at("msw", nw, [P, 2, MH * P])
        mkw = at("mkw", nw + 4 * KB, [P, 2, MH * P])
        mnum = at("mnum", nw + 8 * KB, [P, MH, MVA])
        mtx = at("mtx", nw + 12 * KB + 256, [P, MH * P])
        mtmp = at("mtmp", nw + 14 * KB + 256, [P, MVA])
        mhn = at("mhn", nw + 15 * KB + 512, [P, MH, MV])
        assert nw + 15 * KB + 512 + MH * MV * 4 <= sh

        ident = cons[:, C_ID:C_ID + P]
        ones = cons[:, C_ONE:C_ONE + P]
        tri = cons[:, C_TRI:C_TRI + P]
        maskq = cons[:, C_MASKQ:C_MASKQ + P]
        masks = cons[:, C_MASKS:C_MASKS + P]
        std, rstd = small[:, 0:8], small[:, 8:16]
        eps = small[:, 16:17]
        lcoef = small[:, 20:24]
        l0, l1, l2, l3 = small[:, 24:28], small[:, 28:32], small[:, 32:36], small[:, 36:40]
        nmax, rsum, rinv = small[:, 40:42], small[:, 42:44], small[:, 44:46]
        mss, mden, mrd, mt2, msd, mrs, msc = (small[:, 48 + 4 * n:52 + 4 * n] for n in range(7))
        one_col = ones[:, 0:1]
        groups_before = [sum(1 if q < 4 else 2 for q in range(qt)) for qt in range(TT)]
        group_parity = [g % 2 for g in groups_before]

        def pcol(name, i, n=1):
            return pars[:, _cols[name] + i:_cols[name] + i + n]

        ps = psum("ps", [P, 8, HALF])

        w_landed = [sem(f"w_landed{n}") for n in range(STAGE)]
        w_hi, w_ready, w_used = sem("w_hi"), sem("w_ready"), sem("w_used")
        x_in = [sem(f"x_in{k}") for k in range(KT)]
        half_done = sem("half_done")

        block = ctx.enter_context(nc.Block())

        @block.sync
        def _(sp):
            sp.dma_start(cons[:], con).then_inc(sem("const_in"), 16)
            sp.dma_start(pars[:], par).then_inc(sem("const_in"), 16)

            def load(t, n, round_):
                if n is not None:
                    sp.wait_ge(w_ready, n)
                sp.dma_start(stage[:, round_, :], wt[bass.ds(t * P, P), :]).then_inc(w_landed[round_], 16)

            for t in range(STAGE):
                load(t, None, t)
            with sp.Fori(1, TILES // STAGE) as i:
                for r in range(STAGE):
                    load(i * STAGE + r, (i - 1) * STAGE + r + 1, r)
            for k in range(KT):
                sp.wait_ge(sem("fin_ready"), k + 1)
                sp.dma_start(out[k * P:(k + 1) * P, :], hT[:, k, :]).then_inc(sem("out_done"), 16)
            sp.wait_ge(sem("out_done"), 16 * KT)

        @block.gpsimd
        def _(pool):
            def split(r, landed, hi_count, used):
                slot, st = r % RING, r % STAGE
                pool.wait_ge(w_landed[st], landed)
                if used is not None:
                    pool.wait_ge(w_used, used)
                nc.gpsimd.tensor_tensor(whi[:, slot, :], stage[:, st, :], one_col.to_broadcast([P, 1024]),
                                        ALU.mult).then_inc(w_hi, 1)
                pool.wait_ge(w_hi, hi_count)
                nc.gpsimd.tensor_tensor(wlo[:, slot, :], stage[:, st, :], whi[:, slot, :].bitcast(F32),
                                        ALU.subtract).then_inc(w_ready, 1)

            pool.wait_ge(sem("const_in"), 32)
            for r in range(RING):
                split(r, 16 * (r // STAGE + 1), r + 1, None)
            with pool.Fori(1, TILES // RING) as i:
                for r in range(RING):
                    split(r, (i * (RING // STAGE) + r // STAGE + 1) * 16, i * RING + r + 1,
                          (i - 1) * RING + r + 1)

        norms = [("n0", KT), ("nk", 1), ("nq", 2), ("F0n", KT), ("n1", KT), ("F1n", KT), ("nf", KT)]

        def nbase(name, kind):
            before = norms[:[n for n, _ in norms].index(name)]
            if kind in ("sq", "sum"):
                return sum(t for _, t in before)
            if kind in ("std", "diag"):
                return len(before)
            if kind == "bc":
                return 2 * len(before)
            return sum(KT for _, t in before if t == KT)

        def pe_sums(pe, name, tiles, bank, squares):
            for k in range(tiles):
                pe.wait_ge(sem("norm_sq"), nbase(name, "sq") + k + 1)
                for c in range(TT):
                    mm = nc.tensor.matmul(ps[:, bank, c:c + 1], squares[:, k % 2, c * P:(c + 1) * P], one_col,
                                          start=(k == 0 and c == 0), stop=(k == tiles - 1), skip_group_check=True)
                mm.then_inc(sem("norm_sum"), 1)

        def pe_spread(pe, name, bank, dg):
            pe.wait_ge(sem("norm_diag"), nbase(name, "diag") + 1)
            for s in range(2):
                nc.tensor.matmul(ps[:, bank + s, :], ones, dg[:, s * HALF:(s + 1) * HALF],
                                 start=True, stop=True).then_inc(sem("norm_bc"), 1)

        def pe_norm(pe, name, bank_sum, bank_bc):
            pe_sums(pe, name, KT, bank_sum, sq)
            pe_spread(pe, name, bank_bc, diag)

        def act_squares(act, name, src, tiles, squares, ready=None):
            for k in range(tiles):
                if ready is not None:
                    ready(k)
                if k >= 2:
                    act.wait_ge(sem("norm_sum"), nbase(name, "sum") + k - 1)
                nc.scalar.activation(squares[:, k % 2, :], src(k), ACT.Square).then_inc(sem("norm_sq"), 1)

        def act_std(act, name, tiles, width, bank):
            act.wait_ge(sem("norm_sum"), nbase(name, "sum") + tiles)
            nc.scalar.activation(std, ps[:, bank, 0:TT], ACT.Sqrt, bias=eps,
                                 scale=1.0 / width).then_inc(sem("norm_std"), 1)

        def act_norm(act, name, bank_sum, ready, split=True):
            act_squares(act, name, lambda k: hT[:, k, :], KT, sq, ready)
            act_std(act, name, KT, D, bank_sum)
            if split:
                for k in range(KT):
                    act.wait_ge(sem("norm_xn"), nbase(name, "xn") + k + 1)
                    nc.scalar.copy(ahi[:, k, :], xnf[:, k % 2, :]).then_inc(sem("norm_hi"), 1)

        def dve_factor(dve, ch, name, dg):
            dve.wait_ge(sem("norm_std"), nbase(name, "std") + 1)
            ch.link(nc.vector.reciprocal(rstd, std))
            for c in range(TT):
                ins = nc.vector.tensor_scalar(dg[:, c * P:(c + 1) * P], ident, rstd[:, c:c + 1], None, ALU.mult)
            ins.then_inc(sem("norm_diag"), 1)
            dve.wait_ge(sem("norm_bc"), nbase(name, "bc") + 2)

        def spread_factor(bank):
            return ps[:, bank:bank + 2, :].rearrange("p a b -> p (a b)")

        def dve_norm(dve, ch, name, gain, bank_bc):
            dve_factor(dve, ch, name, diag)

            def lo(k):
                dve.wait_ge(sem("norm_hi"), nbase(name, "hi") + k + 1)
                nc.vector.tensor_tensor(alo[:, k, :], xnf[:, k % 2, :], ahi[:, k, :].bitcast(F32),
                                        ALU.subtract).then_inc(sem("norm_ready"), 1)

            for k in range(KT):
                if k >= 2:
                    lo(k - 2)
                    dve.wait_ge(sem("norm_ready"), nbase(name, "ready") + k - 1)
                nc.vector.scalar_tensor_tensor(out=xnf[:, k % 2, :], in0=hT[:, k, :], scalar=pcol(gain, k),
                                               in1=spread_factor(bank_bc), op0=ALU.mult,
                                               op1=ALU.mult).then_inc(sem("norm_xn"), 1)
            lo(KT - 2)
            lo(KT - 1)

        def product3(bank, wcols, slot, rhs_k, k_first, k_last, tok):
            hi, lo = whi[:, slot, wcols], wlo[:, slot, wcols]
            nc.tensor.matmul(bank, hi, rhs_k[0][:, tok], start=k_first, stop=False)
            nc.tensor.matmul(bank, hi, rhs_k[1][:, tok], start=False, stop=False)
            return nc.tensor.matmul(bank, lo, rhs_k[0][:, tok], start=False, stop=k_last)

        def m_tile(pe, t, slot, banks, evac=None, xn=None):
            pe.wait_ge(w_ready, t + 1)
            for s in range(2):
                if evac is not None:
                    evac(s)
                for k in range(KT):
                    if xn is not None and s == 0:
                        xn(k)
                    mm = product3(ps[:, banks[s], :], slice(k * P, (k + 1) * P), slot,
                                  (ahi[:, k, :], alo[:, k, :]), k == 0, k == KT - 1,
                                  slice(s * HALF, (s + 1) * HALF))
                mm.then_inc(half_done if s == 0 else w_used, 1)

        def pe_mlp(pe, L, t0):
            up_read, added = sem(L + "up_read"), sem(L + "added")

            def up(t, slot, n, gv, first=False):
                def evac(s):
                    if not first:
                        pe.wait_ge(up_read, n * 4 + 2 * gv + s - 3)
                m_tile(pe, t, slot, (2 * gv, 2 * gv + 1), evac,
                       (lambda k: pe.wait_ge(sem("norm_ready"), nbase(L + "n", "ready") + k + 1)) if first and gv == 0 else None)

            def down(t, slots, g):
                pe.wait_ge(w_ready, t + 2)
                pe.wait_ge(sem(L + "hid"), g * 2 + 2)
                for m in range(KT):
                    for s in range(2):
                        n = m * 2 + s
                        pe.wait_ge(added, g * 2 * KT + (n + 1))
                        for j in range(2):
                            mm = product3(ps[:, 4 + n % 4, :], slice(m * P, (m + 1) * P), slots[j],
                                          (hid_hi[:, j, :], hid_lo[:, j, :]), j == 0, j == 1,
                                          slice(s * HALF, (s + 1) * HALF))
                            if n == 2 * KT - 1:
                                mm.then_inc(w_used, 1)
                        if n < 2 * KT - 1:
                            mm.then_inc(sem(L + "down"), 1)

            def pair(t, tm, g, last=False):
                for gv in range(2):
                    up(t + gv, (tm + gv) % RING, g * 2 + 1, gv)
                if not last:
                    for gv in range(2):
                        up(t + 2 + gv, (tm + 2 + gv) % RING, g * 2 + 2, gv)
                d = 2 if last else 4
                down(t + d, ((tm + d) % RING, (tm + d + 1) % RING), g)

            for gv in range(2):
                up(t0 + gv, (t0 + gv) % RING, 0, gv, first=True)
            with pe.Fori(0, (FG - 1) // 2) as i:
                for j in range(2):
                    pair(i * 12 + (t0 + 2 + 6 * j), (t0 + 2 + 6 * j) % RING, i * 2 + j)
            pair(t0 + 2 + 6 * (FG - 1), (t0 + 2 + 6 * (FG - 1)) % RING, FG - 1, last=True)

        def half_base(t):
            n = t
            for a, b in ((T_L1_V, T_L1_V + 8),):
                n -= max(0, min(t, b) - a)
            for f in (T_FFN0, T_FFN1):
                if t >= f + 3 * FT:
                    n -= FT
            return n

        def act_mlp(act, ch, L, t0):
            hb = half_base(t0)

            def evac(n, t, gv, first=False):
                buf = upg if gv == 0 else upv
                if not first:
                    act.wait_ge(sem(L + "conv"), n * 2 + gv - 1)
                for s in range(2):
                    if s == 0:
                        act.wait_ge(half_done, n * 2 + (hb + gv + 1))
                    else:
                        act.wait_ge(w_used, t + gv + 1)
                    nc.scalar.copy(buf[:, 2 + s * HALF:2 + (s + 1) * HALF],
                                   ps[:, 2 * gv + s, :]).then_inc(sem(L + "up_read"), 1)

            def finish(n, j, down=None):
                act.wait_ge(sem(L + "conv"), n * 2 + 2)
                nc.scalar.activation(cvg[:, :], cvg[:, :], ACT.Silu).then_inc(sem(L + "silu"), 1)
                act.wait_ge(sem(L + "prod"), n + 1)
                if down is not None:
                    act.wait_ge(w_used, down)
                nc.scalar.copy(hid_hi[:, j, :], cvv[:, :]).then_inc(sem(L + "hid_hi"), 1)

            def pair(t, g, last=False):
                for gv in range(2):
                    evac(g * 2 + 1, t, gv)
                finish(g * 2 + 1, 1)
                if not last:
                    for gv in range(2):
                        evac(g * 2 + 2, t + 2, gv)
                    finish(g * 2 + 2, 0, down=t + 6)

            for gv in range(2):
                evac(0, t0, gv, first=True)
            finish(0, 0)
            with act.Fori(0, FG - 1) as g:
                pair(g * 6 + (t0 + 2), g)
            pair(t0 + 2 + 6 * (FG - 1), FG - 1, last=True)

        def dve_mlp(dve, ch, L, t0, layer):
            col = _cols[f"conv{layer}"]

            def conv(n, gv):
                def w(i):
                    return pars[:, bass.ds(n * 8 + (col + gv * 4 + i), 1)]
                src, dst = (upg, cvg) if gv == 0 else (upv, cvv)
                dve.wait_ge(sem(L + "up_read"), n * 4 + 2 * gv + 2)
                ch.link(nc.vector.tensor_scalar(dst[:, :], src[:, 0:S], w(0), w(3), ALU.mult, ALU.add))
                ch.link(nc.vector.scalar_tensor_tensor(out=dst[:, :], in0=src[:, 1:S + 1], scalar=w(1),
                                                       in1=dst[:, :], op0=ALU.mult, op1=ALU.add))
                nc.vector.scalar_tensor_tensor(out=dst[:, :], in0=src[:, 2:S + 2], scalar=w(2), in1=dst[:, :],
                                               op0=ALU.mult, op1=ALU.add).then_inc(sem(L + "conv"), 1)

            def prod(n):
                dve.wait_ge(sem(L + "silu"), n + 1)
                nc.vector.tensor_tensor(cvv[:, :], cvg[:, :], cvv[:, :], ALU.mult).then_inc(sem(L + "prod"), 1)

            def lo(n, j):
                dve.wait_ge(sem(L + "hid_hi"), n + 1)
                nc.vector.tensor_tensor(hid_lo[:, j, :], cvv[:, :], hid_hi[:, j, :].bitcast(F32),
                                        ALU.subtract).then_inc(sem(L + "hid"), 1)
                dve.wait_ge(sem(L + "hid"), n + 1)

            def add(g, t_last):
                for m in range(KT):
                    for s in range(2):
                        n = m * 2 + s
                        if n < 2 * KT - 1:
                            dve.wait_ge(sem(L + "down"), g * (2 * KT - 1) + (n + 1))
                        else:
                            dve.wait_ge(w_used, t_last + 1)
                        h = hT[:, m, s * HALF:(s + 1) * HALF]
                        nc.vector.tensor_tensor(h, h, ps[:, 4 + n % 4, :], ALU.add).then_inc(sem(L + "added"), 1)

            def pair(t, g, last=False):
                for gv in range(2):
                    conv(g * 2 + 1, gv)
                prod(g * 2 + 1)
                lo(g * 2 + 1, 1)
                if not last:
                    for gv in range(2):
                        conv(g * 2 + 2, gv)
                    prod(g * 2 + 2)
                add(g, t + (3 if last else 5))
                if not last:
                    lo(g * 2 + 2, 0)

            dve.sem_inc(sem(L + "added"), 4)
            nc.vector.memset(upg[:, 0:2], 0.0)
            ch.link(nc.vector.memset(upv[:, 0:2], 0.0))
            for gv in range(2):
                conv(0, gv)
            prod(0)
            lo(0, 0)
            with dve.Fori(0, FG - 1) as g:
                ch.enter(g, 8)
                pair(g * 6 + (t0 + 2), g)
            ch.leave(FG - 1)
            pair(t0 + 2 + 6 * (FG - 1), FG - 1, last=True)

        def m_tiles(pe, t0, count, read, ready):
            with pe.Fori(0, count // 4) as i:
                for b in range(4):
                    m_tile(pe, i * 4 + (t0 + b), (t0 + b) % RING, (2 * (b % 2), 2 * (b % 2) + 1),
                           lambda s: pe.wait_ge(read, i * 8 + (2 * b + s + 1)),
                           ready if b == 0 else None)

        def dve_out(dve, L, t0, x_count):
            hb = half_base(t0)
            for m in range(KT):
                dve.wait_ge(x_in[m], x_count)
                for s in range(2):
                    if s == 0:
                        dve.wait_ge(half_done, hb + m + 1)
                    else:
                        dve.wait_ge(w_used, t0 + m + 1)
                    h = hT[:, m, s * HALF:(s + 1) * HALF]
                    nc.vector.tensor_tensor(h, h, ps[:, 2 * (m % 2) + s, :], ALU.add).then_inc(sem(L + "res"), 1)

        @block.tensor
        def _(pe):
            for name in ("lru_pre", "o", "yt"):
                pe.sem_inc(sem(name), 1)
            pe.wait_ge(sem("const_in"), 32)
            pe_norm(pe, "n0", 0, 6)
            with pe.Fori(0, LRU_T // 2) as i:
                for jj in range(2):
                    j = i * 2 + jj
                    t = i * 4 + 2 * jj
                    m_tile(pe, t, 2 * jj, (0, 1), lambda s: pe.wait_ge(sem("xr_read"), j * 2 + 1),
                           lambda k: pe.wait_ge(sem("norm_ready"), nbase("n0", "ready") + k + 1))
                    m_tile(pe, t + 1, 2 * jj + 1, (2, 3), lambda s: pe.wait_ge(sem("gelu"), j + 1))
                    pe.wait_ge(sem("xc_ready"), j + 1 + 1)
                    pe.wait_ge(sem("wlfix_in"), j + 1)
                    pe.wait_ge(sem("lru_r"), j + 1)
                    pe.wait_ge(sem("lru_i"), j + 1)
                    for g in range(2):
                        for s in range(2):
                            nc.tensor.matmul(ps[:, 4 + 2 * g + s, :], wlfix[:, jj, g * P:(g + 1) * P],
                                             xc[:, s * HALF:(s + 1) * HALF], start=True, stop=True
                                             ).then_inc(sem("lru_pre"), 1)
            t = 2 * LRU_T
            pe.wait_ge(sem("xr_read"), 2 * LRU_T + 1)
            m_tile(pe, t, t % RING, (0, 1))
            pe.wait_ge(sem("gelu"), LRU_T + 1)
            m_tile(pe, t + 1, (t + 1) % RING, (2, 3))
            pe_sums(pe, "nk", 1, 0, sqb)
            pe.wait_ge(sem("lru_r"), LRU_T + 1)
            m_tile(pe, t + 2, (t + 2) % RING, (4, 5))
            pe_spread(pe, "nk", 0, diagb)
            pe.wait_ge(sem("lru_i"), LRU_T + 1)
            m_tile(pe, t + 3, (t + 3) % RING, (6, 7))
            pe_sums(pe, "nq", 2, 4, sqb)
            pe_spread(pe, "nq", 4, diagb)
            pe.wait_ge(sem("wb_in"), 32)
            pe.wait_ge(sem("kv_normed"), 1)
            wv = wkvb_s[:, :].rearrange("p (h e) -> p h e", h=HEADS)[:, :, NOPE:NOPE + VH]
            for c in range(TT):
                if c >= 2:
                    pe.wait_ge(sem("v_read"), c - 1)
                nc.tensor.matmul(ps[:, 2 + c % 2, :], lat[:, 2, c * P:(c + 1) * P], wv,
                                 start=True, stop=True).then_inc(sem("v_mm"), 1)

            def project(h, par, part):
                if part == 0:
                    pe.wait_ge(sem("wh_in"), h * 3 + 3)
                pe.wait_ge(sem("proj_read"), h * 4 + part)
                s = part % 2
                tok = slice(s * HALF, (s + 1) * HALF)
                if part < 2:
                    for k in range(2):
                        mm = nc.tensor.matmul(ps[:, 0, :], wh[:, par, k * P:(k + 1) * P], lat[:, k, tok],
                                              start=(k == 0), stop=(k == 1))
                else:
                    mm = nc.tensor.matmul(ps[0:NOPE, 0, :], wh[:, par, 2 * P:2 * P + NOPE], lat[:, 2, tok],
                                          start=True, stop=True)
                mm.then_inc(sem("proj"), 1)

            def scores(h, par, qt, step):
                if qt == 0:
                    pe.wait_ge(sem("proj_read"), h * 4 + 4)
                if not isinstance(step, int) or step >= 2:
                    pe.wait_ge(sem("probs"), (step - 1) + 1)
                b = 1 + 2 * (qt % 2)
                n = (qt + 1) * P
                for a in range(0, n, HALF):
                    w = min(HALF, n - a)
                    mm = nc.tensor.matmul(ps[:, b + a // HALF, 0:w], qh[0:QK, par, qt * P:(qt + 1) * P],
                                          kh[0:QK, par, a:a + w], start=True, stop=True)
                mm.then_inc(sem("scores"), 1)

            def weigh(h, qt, step, grp):
                pe.wait_ge(sem("probs"), step + 1 + 1)
                groups = [(a, min(4, qt + 1 - a)) for a in range(0, qt + 1, 4)]
                for n, (a, w) in enumerate(groups):
                    pe.wait_ge(sem("pt_read"), grp + n + 1)
                    for kb in range(a, a + w):
                        mm = nc.tensor.transpose(ps[:, 5 + (group_parity[qt] + n) % 2, (kb - a) * P:(kb - a + 1) * P],
                                                 pbuf[:, qt % 2, kb * P:(kb + 1) * P], ident)
                    mm.then_inc(sem("pt"), 1)
                pe.wait_ge(sem("o_read"), step + 1)
                o = ps[:, 7, 0:VH]
                for n, (a, w) in enumerate(groups):
                    pe.wait_ge(sem("pt_read"), (grp + (n + 2)) + 1)
                    for kb in range(a, a + w):
                        mm = nc.tensor.matmul(o, ptb[:, qt % 2, kb * P:(kb + 1) * P],
                                              vtok[:, kb, bass.ds(h * VH, VH)], start=(kb == 0), stop=(kb == qt),
                                              skip_group_check=True)
                mm.then_inc(sem("o"), 1)

            def turn(p, m, last):
                pe.wait_ge(sem("o_read"), (p * 16 + (8 + 2 * m + 2)) + 1)
                if m == 0:
                    pe.wait_ge(sem("proj_read"), p * 8 + (8 if last else 12))
                else:
                    pe.wait_ge(sem("y_read"), p * 4 + m + 1)
                for n in range(2):
                    mm = nc.tensor.transpose(ps[:, 0, n * P:(n + 1) * P], opair[:, 2 * m + n, :], ident)
                mm.then_inc(sem("yt"), 1)

            def head_pair(p, last=False):
                for i in range(16):
                    par, qt = i // 8, i % 8
                    step = p * 16 + i
                    weigh(p * 2 + par, qt, step, p * 24 + (12 * par + groups_before[qt]))
                    if i == 0:
                        pe.wait_ge(sem("y_read"), p * 4 + 1)
                    if qt < 4 and not (last and par == 1):
                        project(p * 2 + par + 1, 1 - par, qt)
                    j = i + 2
                    if not (last and j >= 16):
                        scores(p * 2 + j // 8, (j // 8) % 2, j % 8, p * 16 + j)
                    if par == 1 and 4 <= qt < 7:
                        turn(p, qt - 4, last)
                turn(p, 3, last)

            pe.wait_ge(sem("v_read"), TT)
            pe.wait_ge(sem("q_normed"), 2)
            pe.wait_ge(sem("kpe_ready"), 1)
            for part in range(4):
                project(0, 0, part)
            for i in range(2):
                scores(0, 0, i, i)
            with pe.Fori(0, HEADS // 2 - 1) as p:
                head_pair(p)
            head_pair(HEADS // 2 - 1, last=True)
            pe.wait_ge(sem("lru_split"), LRU_T)
            pe.wait_ge(sem("y_read"), (4 * (HEADS // 2)) + 1)
            m_tiles(pe, T_L0_OUT, KT, sem("L0res"), None)
            pe_norm(pe, "F0n", 4, 6)
            pe_mlp(pe, "F0", T_FFN0)

            pe_norm(pe, "n1", 0, 6)
            pe.wait_ge(sem("wg_split"), 1)
            pe.wait_ge(sem("norm_ready"), nbase("n1", "ready") + KT)
            for c in range(TT):
                for k in range(KT):
                    tok = slice(c * P, (c + 1) * P)
                    g = ps[:, 4, c * 8:(c + 1) * 8]
                    wk = slice(k * 8, (k + 1) * 8)
                    nc.tensor.matmul(g, ahi[:, k, tok], wghi[:, wk], start=(c == 0 and k == 0), stop=False,
                                     skip_group_check=True)
                    nc.tensor.matmul(g, alo[:, k, tok], wghi[:, wk], start=False, stop=False, skip_group_check=True)
                    mm = nc.tensor.matmul(g, ahi[:, k, tok], wglo[:, wk], start=False, stop=(k == KT - 1),
                                          skip_group_check=True)
            mm.then_inc(sem("g_pre"), 1)
            for h in range(MH):
                for qk in range(2):
                    t = T_L1 + 2 * h + qk
                    m_tile(pe, t, t % RING, (2 * qk, 2 * qk + 1),
                           None if h == 0 else (lambda s: pe.wait_ge(sem("l1_read"), 4 * h + 2 * qk + s - 3)))
                if h == 0:
                    pe.wait_ge(sem("g_sp"), 1)
                    nc.tensor.matmul(ps[:, 5, 0:TT * MH], tri, gsp, start=True, stop=True
                                     ).then_inc(sem("g_cum"), 1)
                if h == 1:
                    pe.wait_ge(sem("g_a"), 2)
                    nc.tensor.transpose(ps[0:32, 6, 0:P], ga, ident)
                    nc.tensor.transpose(ps[0:32, 6, P:2 * P], gnb, ident).then_inc(sem("g_turned"), 1)
                if h == 2:
                    pe.wait_ge(sem("g_max"), 2)
                    nc.tensor.matmul(ps[0:1, 7, 0:32], gAT[0:32, P - 1:P], ident[0:32, 0:32], start=True, stop=True)
                    nc.tensor.matmul(ps[0:1, 7, 32:64], g_last, ident[0:32, 0:32], start=True, stop=True
                                     ).then_inc(sem("g_rows"), 1)
                if h == 3:
                    pe.wait_ge(sem("g_m"), 1)
                    nc.tensor.matmul(ps[0:32, 7, 64:65], m_row, ones[0:1, 0:1], start=True, stop=True)
                    nc.tensor.matmul(ps[:, 7, 128:160], ones[0:1, :], m_row, start=True, stop=True)
                    nc.tensor.matmul(ps[:, 7, 160:192], ones[0:1, :], ml_row, start=True, stop=True
                                     ).then_inc(sem("g_spread"), 1)
                    pe.wait_ge(sem("g_MT"), 1)
                    nc.tensor.transpose(ps[:, 7, 256:288], gMT[0:32, :], ident[0:32, 0:32]).then_inc(sem("g_M"), 1)

            pe.wait_ge(sem("l1_read"), 4 * MH)
            pe.wait_ge(sem("g_e"), 1)

            with pe.Fori(0, 2) as n:
                for j in range(4):
                    slot = (T_L1_V + j) % RING
                    pe.wait_ge(w_ready, n * 4 + (T_L1_V + j + 1))
                    for c in range(TT):
                        if j == 0:
                            pe.wait_ge(sem("l1_read"), n * 8 + (4 * MH + c + 1 - TT))
                        for kk in range(2):
                            k = 2 * j + kk
                            tok = slice(c * P, (c + 1) * P)
                            cols = slice(kk * HALF, (kk + 1) * HALF)
                            nc.tensor.matmul(ps[:, c, :], ahi[:, k, tok], whi[:, slot, cols], start=(k == 0),
                                             stop=False)
                            nc.tensor.matmul(ps[:, c, :], alo[:, k, tok], whi[:, slot, cols], start=False,
                                             stop=False)
                            mm = nc.tensor.matmul(ps[:, c, :], ahi[:, k, tok], wlo[:, slot, cols], start=False,
                                                  stop=(k == KT - 1))
                        if c == TT - 1:
                            mm.then_inc(w_used, 1)
                        elif j == 3:
                            mm.then_inc(sem("v1_mm"), 1)
            pe.wait_ge(sem("l1_read"), 4 * MH + 2 * TT)

            def chunk_scores(c):
                tok = slice(c * P, (c + 1) * P)
                pe.wait_ge(sem("mtx"), c + 1)
                if c >= 1:
                    pe.wait_ge(sem("mw"), 4 * c)
                nc.tensor.matmul(ps[:, 0, :], ones[0:32, :], mtx[0:32, :], start=True, stop=False,
                                 skip_group_check=True)
                for h in range(MH):
                    mm = nc.tensor.matmul(ps[:, 0, h * P:(h + 1) * P], ident, masks, start=False, stop=(h == 3),
                                          skip_group_check=True)
                mm.then_inc(sem("m_bc"), 1)
                if c >= 1:
                    pe.wait_ge(sem("msw"), c)
                    pe.wait_ge(sem("mkw"), 4 * c)
                for h in range(MH):
                    mm = nc.tensor.matmul(ps[:, 1, h * P:(h + 1) * P], kT[:, h, tok], qT[:, h, tok],
                                          start=(h == 0), stop=(h == MH - 1), skip_group_check=True)
                mm.then_inc(sem("m_qk"), 1)
                for h in range(MH):
                    mm = nc.tensor.transpose(ps[:, 2, h * P:(h + 1) * P], kT[:, h, tok], ident)
                mm.then_inc(sem("m_kt"), 1)

            def chunk_head(c, h):
                tok = slice(c * P, (c + 1) * P)
                n = 4 * c + h
                if n >= 1:
                    pe.wait_ge(sem("m_inter_read"), n)
                    if c >= 1:
                        pe.wait_ge(sem("m_state"), n - 3)
                nc.tensor.matmul(ps[:, 5, 0:MV + 1], qT[:, h, tok], cst[:, h, 0:MV + 1],
                                 start=True, stop=True).then_inc(sem("m_inter"), 1)
                if n >= 2:
                    pe.wait_ge(sem("m_num_read"), n - 1)
                pe.wait_ge(sem("msw"), c + 1)
                nc.tensor.matmul(ps[:, 3 + h % 2, 0:MV + 1], msw[:, c % 2, h * P:(h + 1) * P],
                                 vaug[:, c, h, 0:MV + 1], start=True, stop=True).then_inc(sem("m_num"), 1)
                if n >= 1:
                    pe.wait_ge(sem("m_state"), n)
                pe.wait_ge(sem("mkw"), 4 * c + h + 1)
                nc.tensor.matmul(ps[:, 6, 0:MV + 1], mkw[:, c % 2, h * P:(h + 1) * P],
                                 vaug[:, c, h, 0:MV + 1], start=True, stop=True).then_inc(sem("m_kv"), 1)

            def chunk_turn(c):
                for b in range(2):
                    n = 2 * c + b
                    pe.wait_ge(sem("m_hn"), c + 1)
                    if n >= 1:
                        pe.wait_ge(sem("m_y"), 4 * n)
                    for i in range(4):
                        h, e = 2 * b + i // 2, i % 2
                        mm = nc.tensor.transpose(ps[:, 7, i * P:(i + 1) * P], mhn[:, h, e * P:(e + 1) * P], ident)
                    mm.then_inc(sem("m_turned"), 1)

            pe.wait_ge(sem("cst0"), 1)
            chunk_scores(0)
            for c in range(TT):
                if c + 1 < TT:
                    chunk_scores(c + 1)
                for h in range(MH):
                    chunk_head(c, h)
                if c >= 1:
                    chunk_turn(c - 1)
            chunk_turn(TT - 1)

            pe.wait_ge(sem("m_y"), 8 * TT)

            m_tiles(pe, T_L1_O, KT, sem("sigo"), None)
            m_tiles(pe, T_L1_OUT, KT, sem("L1res"), lambda k: pe.wait_ge(sem("L1mix"), k + 1))
            pe_norm(pe, "F1n", 4, 6)
            pe_mlp(pe, "F1", T_FFN1)
            pe_norm(pe, "nf", 0, 6)

        @block.scalar
        def _(act):
            ch = Chain(act, sem("act_chain"))
            for name in ("xr_read", "gelu", "lru_r", "lru_i", "probs"):
                act.sem_inc(sem(name), 1)
            act.sem_inc(sem("pt_read"), 2)
            for k in range(KT):
                act.dma_start(hT[:, k, :], xt[k * P:(k + 1) * P, :]).then_inc(x_in[k], 16)
            act.dma_start(posi[64:128, :], pos[64:128, :]).then_inc(sem("pos_in"), 16)
            act.dma_start(wlru_s[:], wlru).then_inc(sem("wlru_in"), 16)
            act.dma_start(wkvb_s[:], wkvb).then_inc(sem("wb_in"), 16)
            act.wait_ge(sem("const_in"), 32)
            act.wait_ge(sem("eps_set"), 1)
            act_norm(act, "n0", 0, lambda k: act.wait_ge(x_in[k], 16))
            act.wait_ge(sem("lam_abs"), 1)
            nc.scalar.activation(l1, l0, ACT.Exp).then_inc(sem("lam_exp"), 1)
            act.wait_ge(sem("angles"), 1)
            nc.scalar.activation(tab[64:128, :], lat[64:128, 1, :], ACT.Sin,
                                 scale=cons[64:128, C_ROPE + 3:C_ROPE + 4]).then_inc(sem("tab_ready"), 1)

            def lru_par(j, n):
                return pars[:, bass.ds(j * 8 + (_cols["lru"] + n), 1)]

            act.wait_ge(sem("wlru_in"), 16)
            act.wait_ge(sem("lcoef"), 1)
            with act.Fori(0, LRU_T // 2) as i:
                for jj in range(2):
                    j = i * 2 + jj
                    t = i * 4 + 2 * jj
                    act.wait_ge(sem("lru_pre"), j * 4 + 1)
                    nc.scalar.copy(wlfix[:, jj, :], wlru_s[:, bass.ds(j, 1), :].rearrange("p a b -> p (a b)")
                                   ).then_inc(sem("wlfix_in"), 1)
                    act.wait_ge(sem("xc_ready"), j + 1)
                    act.wait_ge(half_done, t + 1)
                    nc.scalar.copy(xrp[:, 3:3 + HALF], ps[:, 0, :]).then_inc(sem("xr_read"), 1)
                    act.wait_ge(w_used, t + 1)
                    nc.scalar.copy(xrp[:, 3 + HALF:3 + S], ps[:, 1, :]).then_inc(sem("xr_read"), 1)
                    act.wait_ge(sem("ylru"), j + 1)
                    act.wait_ge(w_used, t + 2)
                    nc.scalar.activation(lg[:, :], spread_factor(2), ACT.Gelu_apprx_tanh).then_inc(sem("gelu"), 1)
                    act.wait_ge(sem("lru_pre"), j * 4 + 2 + 1)
                    nc.scalar.activation(lr[:, :], spread_factor(4), ACT.Sigmoid,
                                         bias=lru_par(j, 5)).then_inc(sem("lru_r"), 1)
                    act.wait_ge(sem("lru_pre"), j * 4 + 4 + 1)
                    nc.scalar.activation(li[:, :], spread_factor(6), ACT.Sigmoid,
                                         bias=lru_par(j, 6)).then_inc(sem("lru_i"), 1)
                    act.wait_ge(sem("lru_r"), j + 1 + 1)
                    nc.scalar.activation(lr[:, :], lr[:, :], ACT.Tanh,
                                         scale=small[:, bass.ds(j + 20, 1)]).then_inc(sem("lru_u"), 1)
                    act.wait_ge(sem("lru_u"), j + 1)
                    nc.scalar.activation(ls[:, :], lr[:, :], ACT.Sqrt).then_inc(sem("lru_sq"), 1)
            t = 2 * LRU_T
            act.wait_ge(sem("lru_pre"), 4 * LRU_T + 1)
            act.dma_start(wqb_s[:], wqb).then_inc(sem("wb_in"), 16)
            act.wait_ge(sem("tab_ready"), 1)

            def latent(n, t, banks):
                act.wait_ge(w_used, t + 1)
                nc.scalar.copy(lat[:, n, :], spread_factor(banks)).then_inc(sem("lat_in"), 1)

            latent(2, t, 0)
            act.wait_ge(sem("lat_in"), 1)
            act_squares(act, "nk", lambda k: lat[:, 2, :], 1, sqb)
            latent(0, t + 1, 2)
            act_std(act, "nk", 1, KV_LORA, 0)
            latent(1, t + 2, 4)
            act_squares(act, "nq", lambda k: lat[:, k, :], 2, sqb, lambda k: act.wait_ge(sem("lat_in"), k + 2))
            act_std(act, "nq", 2, Q_LORA, 4)
            act.wait_ge(w_used, T_L0_OUT)
            for j in range(LRU_T):
                act.wait_ge(sem("ylru"), j + 1 + 1)
                nc.scalar.copy(ahi[:, j, :], ylru[:, j, :]).then_inc(sem("lru_hi"), 1)
            for c in range(TT):
                act.wait_ge(sem("v_mm"), c + 1)
                nc.scalar.copy(vtok[:, c, :], ps[:, 2 + c % 2, :]).then_inc(sem("v_read"), 1)

            act.wait_ge(sem("wb_in"), 32)

            def head_weights(h, par):
                if not isinstance(h, int) or h >= 2:
                    act.wait_ge(sem("proj"), h * 4 - 4)
                for n in range(2):
                    nc.scalar.copy(wh[:, par, n * P:(n + 1) * P],
                                   wqb_s[:, n, bass.ds(h * P, P)]).then_inc(sem("wh_in"), 1)
                nc.scalar.copy(wh[:, par, 2 * P:3 * P], wkvb_s[:, bass.ds(h * P, P)]).then_inc(sem("wh_in"), 1)

            def nope(h, par, part):
                s = part % 2
                tok = slice(s * HALF, (s + 1) * HALF)
                act.wait_ge(sem("proj"), h * 4 + (part + 1))
                if part < 2:
                    nc.scalar.mul(qh[0:NOPE, par, tok], ps[0:NOPE, 0, :], QK_SCALE).then_inc(sem("q_nope"), 1)
                else:
                    nc.scalar.copy(kh[0:NOPE, par, tok], ps[0:NOPE, 0, :]).then_inc(sem("proj_read"), 1)

            def exps(qt, step):
                n = (qt + 1) * P
                act.wait_ge(sem("nmax"), step + 1)
                act.wait_ge(sem("o_read"), (step - 1 if not isinstance(step, int) or step >= 1 else 0) + 1)
                b = 1 + 2 * (qt % 2)
                sc = ps[:, b:b + 2, :].rearrange("p a b -> p (a b)")[:, 0:n]
                nc.scalar.activation(pbuf[:, qt % 2, 0:n], sc, ACT.Exp, bias=nmax[:, qt % 2:qt % 2 + 1],
                                     accum_out=rsum[:, qt % 2:qt % 2 + 1]).then_inc(sem("probs"), 1)

            def turned(qt, step, grp):
                act.wait_ge(sem("o"), step + 1)
                for n, a in enumerate(range(0, qt + 1, 4)):
                    w = min(4, qt + 1 - a)
                    act.wait_ge(sem("pt"), grp + (n + 1))
                    nc.scalar.copy(ptb[:, qt % 2, a * P:(a + w) * P],
                                   ps[:, 5 + (group_parity[qt] + n) % 2, 0:w * P]).then_inc(sem("pt_read"), 1)

            def y_hi(p, m):
                act.wait_ge(sem("yt"), (p * 4 + (m + 1)) + 1)
                nc.scalar.copy(ahi[:, bass.ds(p + LRU_T, 1), 2 * m * P:2 * (m + 1) * P].rearrange("p a b -> p (a b)"),
                               ps[:, 0, 0:2 * P]).then_inc(sem("y_hi"), 1)

            def head_pair(p, last=False):
                for i in range(16):
                    par, qt = i // 8, i % 8
                    turned(qt, p * 16 + i, p * 24 + (12 * par + groups_before[qt]))
                    if par == 1 and qt >= 5:
                        y_hi(p, qt - 5)
                    if not (last and i == 15):
                        exps((i + 1) % 8, p * 16 + (i + 1))
                    if qt < 4 and not (last and par == 1):
                        nope(p * 2 + par + 1, 1 - par, qt)
                    if qt == 4 and not (last and par >= 0 and i >= 4):
                        head_weights(p * 2 + par + 2, par)
                y_hi(p, 3)

            act.wait_ge(sem("kpe_in"), 2)
            act.wait_ge(sem("ylru"), LRU_T + 1)
            head_weights(0, 0)
            head_weights(1, 1)
            for part in range(4):
                nope(0, 0, part)
            exps(0, 0)
            with act.Fori(0, HEADS // 2 - 1) as p:
                head_pair(p)
            head_pair(HEADS // 2 - 1, last=True)
            act.wait_ge(sem("o"), 8 * HEADS + 1)
            for k in range(KT):
                act.dma_start(hT[:, k, :], xt[k * P:(k + 1) * P, :]).then_inc(x_in[k], 16)
            act_norm(act, "F0n", 4, lambda k: act.wait_ge(sem("L0res"), 2 * k + 6))
            act_mlp(act, ch, "F0", T_FFN0)

            last_added = 2 * KT * (FG - 1) + 4
            act_squares(act, "n1", lambda k: hT[:, k, :], KT, sq,
                        lambda k: act.wait_ge(sem("F0added"), last_added + 2 * k + 2))
            act.dma_start(spill, hT[:, :, :].rearrange("p a b -> p (a b)")).then_inc(sem("spilled"), 16)
            act.dma_start(wgs[:], wg).then_inc(sem("wg_in"), 16)
            act_std(act, "n1", KT, D, 0)
            act.wait_ge(sem("wg_in"), 16)
            nc.scalar.copy(wghi[:], wgs[:]).then_inc(sem("wg_hi"), 1)
            for k in range(KT):
                act.wait_ge(sem("norm_xn"), nbase("n1", "xn") + k + 1)
                nc.scalar.copy(ahi[:, k, :], xnf[:, k % 2, :]).then_inc(sem("norm_hi"), 1)

            tv = gt.rearrange("p (c g) -> p c g", c=TT)
            act.wait_ge(sem("g_z"), 1)
            nc.scalar.activation(gt, gz, ACT.Tanh, scale=1.0 / GATE_CAP).then_inc(sem("g_tanh"), 1)
            act.wait_ge(sem("g_tanh"), 1)
            ch.link(nc.scalar.activation(gex.rearrange("p (c g) -> p c g", c=TT), tv[:, :, MH:2 * MH], ACT.Exp,
                                         scale=-GATE_CAP))
            nc.scalar.activation(gsp, gex, ACT.Ln, bias=one_col).then_inc(sem("g_sp"), 1)

            hb = half_base(T_L1)
            for h in range(MH):
                for qk in range(2):
                    t = T_L1 + 2 * h + qk
                    for s in range(2):
                        if s == 0:
                            act.wait_ge(half_done, hb + 2 * h + qk + 1)
                        else:
                            act.wait_ge(w_used, t + 1)
                        tok = slice(s * HALF, (s + 1) * HALF)
                        if qk == 0:
                            ins = nc.scalar.mul(qT[:, h, tok], ps[:, s, :], float(MQK) ** -0.5)
                        else:
                            ins = nc.scalar.copy(kT[:, h, tok], ps[:, 2 + s, :])
                        ins.then_inc(sem("l1_read"), 1)
            act.wait_ge(sem("g_E"), 1)
            nc.scalar.activation(g_exp, g_exp, ACT.Exp).then_inc(sem("g_e"), 1)
            act.wait_ge(sem("spilled"), 16)
            with act.Fori(0, 2) as n:
                for c in range(TT):
                    if c < TT - 1:
                        act.wait_ge(sem("v1_mm"), n * (TT - 1) + (c + 1))
                    else:
                        act.wait_ge(w_used, n * 4 + (T_L1_V + 4))
                    nc.scalar.copy(vaug[:, c, bass.ds(n * 2, 2), 0:MV],
                                   ps[:, c, :].rearrange("p (h e) -> p h e", h=2)).then_inc(sem("l1_read"), 1)

            def stab(c):
                act.wait_ge(sem("m_bc"), c + 1)
                if c >= 2:
                    act.wait_ge(sem("msw"), c - 1)
                for h in range(MH):
                    nc.scalar.activation(mw[:, c % 2, h * P:(h + 1) * P], ps[:, 0, h * P:(h + 1) * P], ACT.Exp,
                                         bias=ga[:, 4 * c + h:4 * c + h + 1], scale=-1.0).then_inc(sem("mw"), 1)

            def squares(c, h):
                act.wait_ge(sem("m_num_read"), 4 * c + h + 1)
                if c + h >= 1:
                    act.wait_ge(sem("m_sq"), 4 * c + h)
                nc.scalar.activation(junk[:], mnum[:, h, 0:MV], ACT.Square,
                                     accum_out=mss[:, h:h + 1]).then_inc(sem("m_sq"), 1)

            act.wait_ge(sem("g_e"), 1)
            stab(0)
            for c in range(TT):
                if c + 1 < TT:
                    stab(c + 1)
                for h in range(MH):
                    n = 4 * c + h
                    act.wait_ge(sem("m_inter"), n + 1)
                    if n >= 1:
                        act.wait_ge(sem("m_num_read"), n)
                    nc.scalar.mul(mtmp[:, 0:MV + 1], ps[:, 5, 0:MV + 1],
                                  g_exp[:, n:n + 1]).then_inc(sem("m_inter_read"), 1)
                    if h >= 1:
                        squares(c, h - 1)
                squares(c, MH - 1)
                act.wait_ge(sem("m_v"), c + 1)
                nc.scalar.activation(msd, mt2, ACT.Sqrt, bias=eps, scale=1.0 / MV).then_inc(sem("m_sd"), 1)
            hb = half_base(T_L1_O)
            for m in range(KT):
                for s in range(2):
                    n = 2 * m + s
                    if s == 0:
                        act.wait_ge(half_done, hb + m + 1)
                    else:
                        act.wait_ge(w_used, T_L1_O + m + 1)
                    if n >= 2:
                        act.wait_ge(sem("y_gated"), n - 1)
                    nc.scalar.activation(sigo[:, s, :], ps[:, 2 * (m % 2) + s, :],
                                         ACT.Sigmoid).then_inc(sem("sigo"), 1)
            act.wait_ge(w_used, T_L1_OUT)
            for m in range(KT):
                act.wait_ge(sem("y_gated"), 2 * m + 2)
                nc.scalar.copy(ahi[:, m, :].rearrange("p (c t) -> p c t", c=TT),
                               vaug[:, :, m // 2, (m % 2) * P:(m % 2 + 1) * P]).then_inc(sem("L1hi"), 1)
            act.wait_ge(sem("L1mix"), KT)
            for k in range(KT):
                act.dma_start(hT[:, k, :], spill[:, k * S:(k + 1) * S]).then_inc(x_in[k], 16)
            act_norm(act, "F1n", 4, lambda k: act.wait_ge(sem("L1res"), 2 * k + 6))
            act_mlp(act, ch, "F1", T_FFN1)
            act_norm(act, "nf", 0, lambda k: act.wait_ge(sem("F1added"), last_added + 2 * k + 2), split=False)

        @block.vector
        def _(dve):
            ch = Chain(dve, sem("dve_chain"))
            for name in ("ylru", "xc_ready", "y_read", "o_read"):
                dve.sem_inc(sem(name), 1)
            nc.vector.memset(eps, EPS).then_inc(sem("eps_set"), 1)
            dve.sem_inc(sem("L0res"), 4)
            dve.wait_ge(sem("const_in"), 32)
            lam = pars[:, _cols["lru"]:_cols["lru"] + 8 * LRU_T].rearrange("p (j n) -> p j n", n=8)[:, :, 7]
            nc.vector.scalar_tensor_tensor(out=l0, in0=lam, scalar=-1.0, in1=lam, op0=ALU.mult,
                                           op1=ALU.min).then_inc(sem("lam_abs"), 1)
            rows = slice(64, 128)
            dve.wait_ge(sem("pos_in"), 16)
            posf, ang = lat[rows, 2, :], lat[rows, 1, :]

            def rc(n):
                return cons[rows, C_ROPE + n:C_ROPE + n + 1]

            ch.link(nc.vector.tensor_copy(posf, posi[rows, :]))
            ch.link(nc.vector.tensor_scalar(ang, posf, rc(0), None, ALU.mult))
            ch.link(nc.vector.tensor_scalar(posf, ang, 1.0 / TWO_PI, rc(1), ALU.mult, ALU.add))
            ch.link(nc.vector.tensor_scalar(posf, posf, MAGIC, MAGIC, ALU.add, ALU.subtract))
            for part in (RED1, RED2, RED3):
                ch.link(nc.vector.scalar_tensor_tensor(out=ang, in0=posf, scalar=-part, in1=ang,
                                                       op0=ALU.mult, op1=ALU.add))
            ch.link(nc.vector.tensor_scalar(ang, ang, rc(2), SIN_MAX, ALU.add, ALU.min))
            nc.vector.tensor_scalar(ang, ang, -SIN_MAX, None, ALU.max).then_inc(sem("angles"), 1)
            dve_norm(dve, ch, "n0", "e_g", 6)
            dve.wait_ge(sem("lam_exp"), 1)
            ch.link(nc.vector.tensor_scalar(l2, l1, 2.0, None, ALU.add))
            ch.link(nc.vector.reciprocal(l2, l2))
            ch.link(nc.vector.tensor_tensor(l1, l1, l2, ALU.mult))
            ch.link(nc.vector.tensor_tensor(l2, l1, l1, ALU.mult))
            ch.link(nc.vector.tensor_scalar(l3, l2, 1.0 / 17, 1.0 / 15, ALU.mult, ALU.add))
            for n in (13, 11, 9, 7, 5, 3, 1):
                ch.link(nc.vector.tensor_tensor(l3, l3, l2, ALU.mult))
                ch.link(nc.vector.tensor_scalar(l3, l3, 1.0 / n, None, ALU.add))
            ch.link(nc.vector.tensor_tensor(l3, l3, l1, ALU.mult))
            ch.link(nc.vector.tensor_scalar(l0, lam, -1.0, 0.0, ALU.mult, ALU.max))
            ch.link(nc.vector.tensor_scalar(l3, l3, 8.0, None, ALU.mult))
            nc.vector.scalar_tensor_tensor(out=lcoef, in0=l0, scalar=4.0, in1=l3, op0=ALU.mult,
                                           op1=ALU.add).then_inc(sem("lcoef"), 1)
            ch.link(nc.vector.memset(xrp[:, 0:3], 0.0))

            with dve.Fori(0, LRU_T // 2) as i:
                ch.enter(i, 2 * 9)
                for jj in range(2):
                    j = i * 2 + jj

                    def w(n):
                        return pars[:, bass.ds(j * 8 + (_cols["lru"] + n), 1)]

                    dve.wait_ge(sem("xr_read"), j * 2 + 2 + 1)
                    dve.wait_ge(sem("lru_pre"), j * 4 + 1)
                    ch.link(nc.vector.tensor_scalar(xc[:, :], xrp[:, 0:S], w(0), w(4), ALU.mult, ALU.add))
                    for n in (1, 2):
                        ch.link(nc.vector.scalar_tensor_tensor(out=xc[:, :], in0=xrp[:, n:n + S], scalar=w(n),
                                                               in1=xc[:, :], op0=ALU.mult, op1=ALU.add))
                    nc.vector.scalar_tensor_tensor(out=xc[:, :], in0=xrp[:, 3:3 + S], scalar=w(3), in1=xc[:, :],
                                                   op0=ALU.mult, op1=ALU.add).then_inc(sem("xc_ready"), 1)
                    dve.wait_ge(sem("lru_u"), j + 1)
                    ch.link(nc.vector.tensor_scalar(lc[:, :], lr[:, :], 1.0, None, ALU.add))
                    ch.link(nc.vector.reciprocal(lc[:, :], lc[:, :]))
                    dve.wait_ge(sem("lru_i"), j + 1 + 1)
                    dve.wait_ge(sem("xc_ready"), j + 1 + 1)
                    nc.vector.tensor_tensor(li[:, :], li[:, :], xc[:, :], ALU.mult)
                    dve.wait_ge(sem("lru_sq"), j + 1)
                    ch.link(nc.vector.scalar_tensor_tensor(out=ls[:, :], in0=ls[:, :], scalar=2.0, in1=lc[:, :],
                                                           op0=ALU.mult, op1=ALU.mult))
                    ch.link(nc.vector.tensor_scalar(lr[:, :], lc[:, :], 2.0, 1.0, ALU.mult, ALU.subtract))
                    ch.link(nc.vector.tensor_tensor(ls[:, :], ls[:, :], li[:, :], ALU.mult))
                    y = ylru[:, bass.ds(j, 1), :].rearrange("p a b -> p (a b)")
                    ch.link(nc.vector.tensor_tensor_scan(y, lr[:, :], ls[:, :], 0.0, ALU.mult, ALU.add))
                    dve.wait_ge(sem("gelu"), j + 1 + 1)
                    nc.vector.tensor_tensor(y, y, lg[:, :], ALU.mult).then_inc(sem("ylru"), 1)
            ch.leave(LRU_T // 2)

            dve.wait_ge(sem("lat_in"), 1)
            dve_factor(dve, ch, "nk", diagb)
            nc.vector.scalar_tensor_tensor(out=lat[:, 2, :], in0=lat[:, 2, :], scalar=pcol("kv_g", 0),
                                           in1=spread_factor(0), op0=ALU.mult, op1=ALU.mult
                                           ).then_inc(sem("kv_normed"), 1)
            dve.wait_ge(w_used, T_L0_OUT)
            dve.wait_ge(sem("tab_ready"), 1)
            a32, b32 = slice(NOPE, QK), slice(QK, P)
            kr = spread_factor(6)
            nc.vector.tensor_tensor(rt1[a32, :], kr[a32, :], tab[a32, :], ALU.mult)
            ch.link(nc.vector.tensor_tensor(rt2[a32, :], kr[b32, :], tab[b32, :], ALU.mult))
            nc.vector.tensor_tensor(kpe[a32, :], rt1[a32, :], rt2[a32, :], ALU.add).then_inc(sem("kpe_ready"), 1)
            dve_factor(dve, ch, "nq", diagb)
            for k in range(2):
                nc.vector.scalar_tensor_tensor(out=lat[:, k, :], in0=lat[:, k, :], scalar=pcol("q_g", k),
                                               in1=spread_factor(4), op0=ALU.mult, op1=ALU.mult
                                               ).then_inc(sem("q_normed"), 1)
            for j in range(LRU_T):
                dve.wait_ge(sem("lru_hi"), j + 1)
                nc.vector.tensor_tensor(alo[:, j, :], ylru[:, j, :], ahi[:, j, :].bitcast(F32),
                                        ALU.subtract).then_inc(sem("lru_split"), 1)
            dve.wait_ge(sem("kpe_ready"), 1)
            dve.wait_ge(sem("lru_split"), LRU_T)
            for par in range(2):
                nc.vector.tensor_copy(kh[a32, par, :], kpe[a32, :]).then_inc(sem("kpe_in"), 1)

            def rotate(h, par, part, per_chain):
                tok = slice(part * HALF, (part + 1) * HALF)
                dve.wait_ge(sem("q_nope"), h * 2 + (part + 1))
                nc.vector.scalar_tensor_tensor(out=rt1[a32, 0:HALF], in0=ps[a32, 0, :], scalar=QK_SCALE,
                                               in1=tab[a32, tok], op0=ALU.mult, op1=ALU.mult)
                ch.link(nc.vector.scalar_tensor_tensor(out=rt2[a32, 0:HALF], in0=ps[b32, 0, :], scalar=QK_SCALE,
                                                       in1=tab[b32, tok], op0=ALU.mult, op1=ALU.mult))
                nc.vector.tensor_tensor(qh[a32, par, tok], rt1[a32, 0:HALF], rt2[a32, 0:HALF], ALU.add
                                        ).then_inc(sem("proj_read"), 1)

            def maxima(qt, step):
                n = (qt + 1) * P
                b = 1 + 2 * (qt % 2)
                sc = ps[:, b:b + 2, :].rearrange("p a b -> p (a b)")
                dve.wait_ge(sem("scores"), step + 1)
                if not isinstance(step, int) or step >= 1:
                    dve.wait_ge(sem("probs"), (step - 1) + 1)
                ch.link(nc.vector.tensor_tensor(sc[:, n - P:n], sc[:, n - P:n], maskq, ALU.add))
                nc.vector.tensor_reduce(nmax[:, qt % 2:qt % 2 + 1], sc[:, 0:n], AX_X, ALU.max,
                                        negate=True).then_inc(sem("nmax"), 1)

            def outputs(p, par, qt, step):
                dve.wait_ge(sem("probs"), step + 1 + 1)
                ch.link(nc.vector.reciprocal(rinv[:, qt % 2:qt % 2 + 1], rsum[:, qt % 2:qt % 2 + 1]))
                dve.wait_ge(sem("o"), step + 1 + 1)
                if par == 0:
                    dve.wait_ge(sem("yt"), p * 4 + 1)
                nc.vector.tensor_scalar(opair[:, qt, par * VH:(par + 1) * VH],
                                        ps[:, 7, 0:VH],
                                        rinv[:, qt % 2:qt % 2 + 1], None, ALU.mult).then_inc(sem("o_read"), 1)

            def y_lo(p, m):
                tok = slice(2 * m * P, 2 * (m + 1) * P)
                dve.wait_ge(sem("y_hi"), p * 4 + (m + 1))
                hi = ahi[:, bass.ds(p + LRU_T, 1), tok].rearrange("p a b -> p (a b)")
                lo = alo[:, bass.ds(p + LRU_T, 1), tok].rearrange("p a b -> p (a b)")
                nc.vector.tensor_tensor(lo, ps[:, 0, 0:2 * P], hi.bitcast(F32), ALU.subtract
                                        ).then_inc(sem("y_read"), 1)

            def head_pair(p, last=False):
                for i in range(16):
                    par, qt = i // 8, i % 8
                    if not (last and i == 15):
                        maxima((i + 1) % 8, p * 16 + (i + 1))
                    if qt < 2 and not (last and par == 1):
                        rotate(p * 2 + par + 1, 1 - par, qt, None)
                    outputs(p, par, qt, p * 16 + i)
                    if par == 1 and qt >= 5:
                        y_lo(p, qt - 5)
                y_lo(p, 3)

            for part in range(2):
                rotate(0, 0, part, None)
            maxima(0, 0)
            with dve.Fori(0, HEADS // 2 - 1) as p:
                ch.enter(p, 36)
                head_pair(p)
            ch.leave(HEADS // 2 - 1)
            head_pair(HEADS // 2 - 1, last=True)
            dve_out(dve, "L0", T_L0_OUT, 32)
            dve_norm(dve, ch, "F0n", "f_g0", 6)
            dve_mlp(dve, ch, "F0", T_FFN0, 0)

            dve.sem_inc(sem("sigo"), 4)
            dve.sem_inc(sem("L1res"), 4)
            dve_norm(dve, ch, "n1", "o_g", 6)
            dve.wait_ge(sem("wg_hi"), 1)
            nc.vector.tensor_tensor(wglo[:], wgs[:], wghi[:].bitcast(F32), ALU.subtract).then_inc(sem("wg_split"), 1)
            dve.wait_ge(sem("g_pre"), 1)
            nc.vector.tensor_tensor(gz, ps[:, 4, 0:8 * TT], pcol("gate_b", 0, 8 * TT), ALU.add
                                    ).then_inc(sem("g_z"), 1)
            dve.wait_ge(sem("g_cum"), 1)
            tv = gt.rearrange("p (c g) -> p c g", c=TT)
            nc.vector.scalar_tensor_tensor(out=ga.rearrange("p (c g) -> p c g", c=TT), in0=tv[:, :, 0:MH],
                                           scalar=GATE_CAP, in1=ps[:, 5, 0:32].rearrange("p (c g) -> p c g", c=TT),
                                           op0=ALU.mult, op1=ALU.add).then_inc(sem("g_a"), 1)
            nc.vector.tensor_copy(gnb, ps[:, 5, 0:32]).then_inc(sem("g_a"), 1)
            dve.wait_ge(sem("g_turned"), 1)
            ch.link(nc.vector.tensor_copy(gaT[0:32, :], ps[0:32, 6, 0:P]))
            nc.vector.tensor_tensor_scan(gAT[0:32, :], gaT[0:32, :], gaT[0:32, :], -BIG, ALU.max, ALU.max
                                         ).then_inc(sem("g_max"), 1)
            nc.vector.tensor_copy(g_last, ps[0:32, 6, 2 * P - 1:2 * P]).then_inc(sem("g_max"), 1)
            dve.wait_ge(sem("g_rows"), 1)
            nc.vector.memset(ginfo[0:1, 256:260], 0.0)
            ch.link(nc.vector.tensor_copy(g_row, ps[0:1, 7, 0:64]))
            for h in range(MH):
                ch.add(nc.vector.tensor_tensor_scan(m_next[:, h::MH], g_row[:, h:32:MH], g_row[:, 32 + h:64:MH], 0.0,
                                                    ALU.max, ALU.subtract))
            ch.wait(ch.n)
            nc.vector.tensor_tensor(ml_row, m_row, g_row[:, 0:32], ALU.max).then_inc(sem("g_m"), 1)
            dve.wait_ge(sem("g_spread"), 1)
            ch.link(nc.vector.tensor_copy(g_mcol, ps[0:32, 7, 64:65]))
            ch.link(nc.vector.tensor_copy(gz, ps[:, 7, 128:192]))
            nc.vector.tensor_scalar(gMT[0:32, :], gAT[0:32, :], g_mcol, None, ALU.max).then_inc(sem("g_MT"), 1)
            dve.wait_ge(sem("g_M"), 1)
            m_tok = ps[:, 7, 256:288]
            nc.vector.tensor_tensor(g_exp[:, 0:32], gz[:, 0:32], m_tok, ALU.subtract)
            nc.vector.tensor_tensor(g_exp[:, 32:64], gnb, m_tok, ALU.subtract)
            nc.vector.tensor_tensor(g_exp[:, 64:96], ga, gz[:, 32:64], ALU.subtract)
            nc.vector.tensor_tensor(g_exp[:, 96:128], gz[:, 0:32], gz[:, 32:64], ALU.subtract
                                    ).then_inc(sem("g_E"), 1)
            dve.wait_ge(sem("spilled"), 16)
            ch.link(nc.vector.memset(vaug[:, :, :, MV:MVA], 1.0))
            nc.vector.memset(cst[:, :, :], 0.0).then_inc(sem("cst0"), 1)

            def stab_rows(c):
                if c == 0:
                    dve.wait_ge(sem("g_MT"), 1)
                else:
                    dve.wait_ge(sem("m_bc"), c)
                for h in range(MH):
                    ins = nc.vector.tensor_scalar(mtx[0:32, h * P:(h + 1) * P], gMT[0:32, :],
                                                  ident[0:32, 4 * c + h:4 * c + h + 1], None, ALU.mult)
                ins.then_inc(sem("mtx"), 1)

            def weights(c):
                dve.wait_ge(sem("mw"), 4 * c + 4)
                dve.wait_ge(sem("m_qk"), c + 1)
                if c >= 2:
                    dve.wait_ge(sem("m_kv"), 4 * c - 4)
                nc.vector.tensor_tensor(msw[:, c % 2, :], ps[:, 1, :], mw[:, c % 2, :], ALU.mult
                                        ).then_inc(sem("msw"), 1)
                dve.wait_ge(sem("m_kt"), c + 1)
                for h in range(MH):
                    n = 4 * c + h
                    nc.vector.tensor_scalar(mkw[:, c % 2, h * P:(h + 1) * P], ps[:, 2, h * P:(h + 1) * P],
                                            g_exp[:, 64 + n:65 + n], None, ALU.mult).then_inc(sem("mkw"), 1)

            def gather(c):
                for b in range(2):
                    dve.wait_ge(sem("m_turned"), 2 * c + b + 1)
                    for i in range(4):
                        h, e = 2 * b + i // 2, i % 2
                        nc.vector.tensor_scalar(vaug[:, c, h, e * P:(e + 1) * P], ps[:, 7, i * P:(i + 1) * P],
                                                pcol("out_g", 2 * h + e), None, ALU.mult).then_inc(sem("m_y"), 1)

            stab_rows(0)
            dve.wait_ge(sem("g_e"), 1)
            weights(0)
            stab_rows(1)
            for c in range(TT):
                if c + 1 < TT:
                    weights(c + 1)
                if c + 2 < TT:
                    stab_rows(c + 2)
                if c >= 1:
                    dve.wait_ge(sem("m_hn"), c)
                for h in range(MH):
                    n = 4 * c + h
                    dve.wait_ge(sem("m_inter_read"), n + 1)
                    dve.wait_ge(sem("m_num"), n + 1)
                    nc.vector.tensor_tensor(mnum[:, h, 0:MV + 1], ps[:, 3 + h % 2, 0:MV + 1], mtmp[:, 0:MV + 1],
                                            ALU.add).then_inc(sem("m_num_read"), 1)
                    dve.wait_ge(sem("m_kv"), n + 1)
                    nc.vector.scalar_tensor_tensor(out=cst[:, h, 0:MV + 1], in0=cst[:, h, 0:MV + 1],
                                                   scalar=g_exp[:, 96 + n:97 + n], in1=ps[:, 6, 0:MV + 1],
                                                   op0=ALU.mult, op1=ALU.add).then_inc(sem("m_state"), 1)
                if c >= 1:
                    gather(c - 1)
                dve.wait_ge(sem("m_num_read"), 4 * c + 4)
                ch.link(nc.vector.scalar_tensor_tensor(out=mden, in0=mnum[:, :, MV], scalar=-1.0,
                                                       in1=mnum[:, :, MV], op0=ALU.mult, op1=ALU.max))
                ch.link(nc.vector.tensor_tensor(mden, mden, g_exp[:, 32 + 4 * c:36 + 4 * c], ALU.max))
                ch.link(nc.vector.reciprocal(mrd, mden))
                ch.link(nc.vector.tensor_tensor(mt2, mrd, mrd, ALU.mult))
                dve.wait_ge(sem("m_sq"), 4 * c + 4)
                nc.vector.tensor_tensor(mt2, mt2, mss, ALU.mult).then_inc(sem("m_v"), 1)
                dve.wait_ge(sem("m_sd"), c + 1)
                ch.link(nc.vector.reciprocal(mrs, msd))
                ch.link(nc.vector.tensor_tensor(msc, mrs, mrd, ALU.mult))
                if c >= 1:
                    dve.wait_ge(sem("m_turned"), 2 * c)
                for h in range(MH):
                    ins = nc.vector.tensor_scalar(mhn[:, h, :], mnum[:, h, 0:MV], msc[:, h:h + 1], None, ALU.mult)
                ins.then_inc(sem("m_hn"), 1)
            gather(TT - 1)
            for m in range(KT):
                for s in range(2):
                    n = 2 * m + s
                    dve.wait_ge(sem("sigo"), n + 5)
                    y = vaug[:, 4 * s:4 * s + 4, m // 2, (m % 2) * P:(m % 2 + 1) * P]
                    nc.vector.tensor_tensor(y, y, sigo[:, s, :].rearrange("p (c t) -> p c t", c=4), ALU.mult
                                            ).then_inc(sem("y_gated"), 1)
            for m in range(KT):
                dve.wait_ge(sem("L1hi"), m + 1)
                nc.vector.tensor_tensor(alo[:, m, :].rearrange("p (c t) -> p c t", c=TT),
                                        vaug[:, :, m // 2, (m % 2) * P:(m % 2 + 1) * P],
                                        ahi[:, m, :].bitcast(F32).rearrange("p (c t) -> p c t", c=TT),
                                        ALU.subtract).then_inc(sem("L1mix"), 1)
            dve_out(dve, "L1", T_L1_OUT, 48)
            dve_norm(dve, ch, "F1n", "f_g1", 6)
            dve_mlp(dve, ch, "F1", T_FFN1, 1)
            dve_factor(dve, ch, "nf", diag)
            for k in range(KT):
                nc.vector.scalar_tensor_tensor(out=hT[:, k, :], in0=hT[:, k, :], scalar=pcol("fin_g", k),
                                               in1=spread_factor(6), op0=ALU.mult, op1=ALU.mult
                                               ).then_inc(sem("fin_ready"), 1)


def _m_tile(w, cols):
    k = w.shape[0] // P
    return w[:, cols].reshape(k, P, P).transpose(1, 0, 2).reshape(P, k * P)


def _mlp_tiles(up, down):
    def ups(f):
        return [_m_tile(up, slice(f * P, (f + 1) * P)), _m_tile(up, slice(D_FF + f * P, D_FF + (f + 1) * P))]

    tiles = ups(0)
    for g in range(FG):
        tiles += ups(2 * g + 1)
        if g < FG - 1:
            tiles += ups(2 * g + 2)
        tiles += [down[(2 * g + j) * P:(2 * g + j + 1) * P, :] for j in range(2)]
    return tiles


def kernel(**inputs):
    import concourse.bacc as bacc
    from concourse.bass_utils import run_bass_kernel_spmd

    a = {k: np.asarray(v) for k, v in inputs.items()}
    w0, w1 = a["e_w_in"][0], a["o_w_in"][0]
    tiles = []
    for j in range(LRU_T):
        tiles += [_m_tile(w0, slice(j * P, (j + 1) * P)), _m_tile(w0, slice(LRU_W + j * P, LRU_W + (j + 1) * P))]
    q0 = 2 * LRU_W
    kv0 = q0 + Q_LORA
    r0 = kv0 + KV_LORA
    half = ROPE // 2
    tiles += [_m_tile(w0, slice(kv0, kv0 + P)), _m_tile(w0, slice(q0, q0 + P)), _m_tile(w0, slice(q0 + P, q0 + 2 * P))]
    rot = np.concatenate([np.zeros((D, NOPE), np.float32), w0[:, r0:r0 + ROPE], w0[:, r0 + half:r0 + ROPE],
                          w0[:, r0:r0 + half]], axis=1)
    tiles.append(_m_tile(rot, slice(0, P)))
    tiles += [_m_tile(a["e_w_out"][0], slice(m * P, (m + 1) * P)) for m in range(KT)]
    tiles += _mlp_tiles(a["f_w_up"][0], a["f_w_down"][0])
    c1 = MH * MQK
    for h in range(MH):
        tiles += [_m_tile(w1, slice(h * P, (h + 1) * P)), _m_tile(w1, slice(c1 + h * P, c1 + (h + 1) * P))]
    for n in range(2):
        for j in range(4):
            v = w1[2 * j * P:(2 * j + 2) * P, 2 * c1 + n * HALF:2 * c1 + (n + 1) * HALF]
            tiles.append(v.reshape(2, P, HALF).transpose(1, 0, 2).reshape(P, 2 * HALF))
    o0 = 2 * c1 + MH * MV
    tiles += [_m_tile(w1, slice(o0 + m * P, o0 + (m + 1) * P)) for m in range(KT)]
    tiles += [_m_tile(a["o_w_out"][0], slice(m * P, (m + 1) * P)) for m in range(KT)]
    tiles += _mlp_tiles(a["f_w_up"][1], a["f_w_down"][1])
    assert len(tiles) == TILES, (len(tiles), TILES)
    wt = np.ascontiguousarray(np.concatenate(tiles, axis=0))

    wg = np.ascontiguousarray(w1[:, o0 + MH * MV:].reshape(KT, P, 8).transpose(1, 0, 2).reshape(P, KT * 8))
    qb = a["e_w_qb"][0].reshape(Q_LORA, HEADS, QK)
    qb = np.concatenate([qb, qb[:, :, NOPE + half:], qb[:, :, NOPE:NOPE + half]], axis=2)
    wqb = np.ascontiguousarray(qb.reshape(2, P, HEADS * P).transpose(1, 0, 2))
    wkvb = np.ascontiguousarray(a["e_w_kvb"][0])
    wlru = np.zeros((P, LRU_T, 2, P), np.float32)
    for g, name in enumerate(("e_lru_w_a", "e_lru_w_x")):
        for j in range(LRU_T):
            for b in range(2):
                wlru[64 * b:64 * (b + 1), j, g, 64 * b:64 * (b + 1)] = a[name][0, 2 * j + b]
    wlru = wlru.reshape(P, LRU_T, 2 * P)

    def columns(v):
        return v.reshape(-1, P).T

    par = np.zeros((P, NPAR), np.float32)

    def put(name, v):
        par[:, _cols[name]:_cols[name] + v.shape[1]] = v

    put("e_g", columns(a["e_norm_g"][0]))
    put("o_g", columns(a["o_norm_g"][0]))
    put("f_g0", columns(a["f_norm_g"][0]))
    put("f_g1", columns(a["f_norm_g"][1]))
    put("fin_g", columns(a["final_norm_g"]))
    put("q_g", columns(a["e_q_norm_g"][0]))
    put("kv_g", columns(a["e_kv_norm_g"][0]))
    put("out_g", columns(a["o_out_norm_g"][0]))
    lru = [a["e_lru_conv_w"][0, n] for n in range(4)] + [a["e_lru_conv_b"][0], a["e_lru_b_a"][0].reshape(-1),
                                                        a["e_lru_b_x"][0].reshape(-1), a["e_lru_lambda"][0]]
    put("lru", np.stack([columns(v) for v in lru], axis=2).reshape(P, -1))
    put("gate_b", np.broadcast_to(np.tile(np.concatenate([a["o_b_igate"][0], a["o_b_fgate"][0]]), TT), (P, 8 * TT)))
    for l in range(2):
        rows = [a["f_conv_w"][l, n] for n in range(3)] + [a["f_conv_b"][l]]
        parts = [columns(r[g * D_FF:(g + 1) * D_FF]) for g in range(2) for r in rows]
        put(f"conv{l}", np.stack(parts, axis=2).reshape(P, -1))

    con = np.zeros((P, NCON), np.float32)
    i = np.arange(P)
    con[:, C_ID:C_ID + P] = np.eye(P)
    con[:, C_ONE:C_ONE + P] = 1.0
    con[:, C_TRI:C_TRI + P] = i[:, None] <= i[None, :]
    con[:, C_MASKQ:C_MASKQ + P] = -BIG * (i[:, None] < i[None, :])
    con[:, C_MASKS:C_MASKS + P] = BIG * (i[:, None] > i[None, :])
    freq = (10000.0 ** (-np.arange(half) / half)).astype(np.float32)
    con[NOPE:, C_ROPE] = np.tile(freq, 4)
    con[NOPE:QK, C_ROPE + 1] = 0.25
    con[NOPE:QK, C_ROPE + 2] = np.pi / 2
    con[NOPE:, C_ROPE + 3] = 1.0
    con[QK:QK + half, C_ROPE + 3] = -1.0

    xt = np.ascontiguousarray(a["x"][0].T)
    pos = np.ascontiguousarray(np.broadcast_to(a["positions"][0][None, :].astype(np.int32), (P, S)))

    nc = bacc.Bacc("TRN2", target_bir_lowering=False, num_devices=1)
    arrays = {"wt": wt, "xt": xt, "pos": pos, "par": par, "con": con, "wqb": wqb, "wkvb": wkvb, "wlru": wlru,
              "wg": wg}
    aps = {n: nc.dram_tensor("in_" + n, v.shape, mybir.dt.from_np(v.dtype), kind="ExternalInput").ap()
           for n, v in arrays.items()}
    spill = nc.dram_tensor("spill", (P, KT * S), F32, kind="Internal").ap()
    out = nc.dram_tensor("out_0", (D, S), F32, kind="ExternalOutput").ap()
    build(nc, spill=spill, out=out, **aps)
    r = run_bass_kernel_spmd(nc, [{"in_" + n: v for n, v in arrays.items()}], core_ids=[0])
    return np.ascontiguousarray(r.results[0]["out_0"].T)[None]
```

```python
from contextlib import ExitStack

import numpy as np

import concourse.bass as bass
from concourse import mybir

ALU = mybir.AluOpType
ACT = mybir.ActivationFunctionType
F32 = mybir.dt.float32
F32R = mybir.dt.float32r
I32 = mybir.dt.int32
AX_X = mybir.AxisListType.X

P = 128
D = 1024
S = 1024
HALF = 512
KT = D // P
TT = S // P
EPS = 1e-6

LRU_W = 512
LRU_T = LRU_W // P
Q_LORA = 256
KV_LORA = 128
HEADS = 8
NOPE, ROPE, VH = 64, 32, 64
QK = NOPE + ROPE
QK_SCALE = float(QK) ** -0.5

MH, MQK, MV = 4, 128, 256
MVA = MV + 2
GATE_CAP = 15.0

D_FF = 2816
FT = D_FF // P
FG = FT // 2

RING = 4
STAGE = 2

T_L0_OUT = 2 * LRU_T + 4
T_FFN0 = T_L0_OUT + KT
T_L1 = T_FFN0 + 3 * FT
T_L1_V = T_L1 + 2 * MH
T_L1_O = T_L1_V + 8
T_L1_OUT = T_L1_O + KT
T_FFN1 = T_L1_OUT + KT
TILES = T_FFN1 + 3 * FT

_cols = {}
_n = 0
for _name, _w in [("e_g", KT), ("o_g", KT), ("f_g0", KT), ("f_g1", KT), ("fin_g", KT), ("q_g", Q_LORA // P),
                  ("kv_g", 1), ("lru", LRU_T * 8), ("out_g", KT), ("gate_b", TT * 8),
                  ("conv0", FT * 8), ("conv1", FT * 8)]:
    _cols[_name] = _n
    _n += _w
NPAR = _n

C_ID, C_ONE, C_TRI, C_MASKQ, C_MASKS, C_ROPE = 0, P, 2 * P, 3 * P, 4 * P, 5 * P
NCON = 5 * P + 8
TWO_PI = 2.0 * np.pi
RED1 = 6.28125
RED2 = float(np.float32(np.floor((TWO_PI - RED1) * 2 ** 18) / 2 ** 18))
RED3 = float(TWO_PI - RED1 - RED2)
MAGIC = 12582912.0
SIN_MAX = 3.1415925
BIG = 1e30


class Chain:

    def __init__(self, eng, sem):
        self.eng, self.sem, self.n, self.shift = eng, sem, 0, 0

    def link(self, ins):
        ins.then_inc(self.sem, 1)
        self.n += 1
        self.eng.wait_ge(self.sem, self.shift + self.n)

    def add(self, ins):
        ins.then_inc(self.sem, 1)
        self.n += 1
        return self.n

    def wait(self, n):
        self.eng.wait_ge(self.sem, self.shift + n)

    def enter(self, i, per):
        self.shift, self.start, self.per = i * per, self.n, per

    def leave(self, count):
        assert self.n - self.start == self.per, (self.n - self.start, self.per)
        self.n += self.per * (count - 1)
        self.shift = 0


def build(nc, wt, xt, pos, par, con, wqb, wkvb, wlru, wg, spill, out, upto=4):
    with ExitStack() as ctx:
        def psum(name, shape):
            return ctx.enter_context(nc.psum_tensor(name, shape, F32))

        sems = {}

        def sem(name):
            if name not in sems:
                sems[name] = ctx.enter_context(nc.semaphore(name))
            return sems[name]

        base = -(-nc.sbuf_base // 32) * 32
        room = (nc.sbuf_usable_end - base) // 32 * 32 - 32
        ctx.enter_context(nc.sbuf_tensor("arena", [P, room // 4], F32))
        KB = 1024

        def at(name, off, shape, dt=F32):
            size = int(np.prod(shape[1:])) * 4
            assert off + size <= room, (name, off, size, room)
            return nc.alloc_sbuf_tensor_at(name, shape, dt, offset=base + off)

        stage = at("stage", 0, [P, STAGE, 1024])
        whi = at("whi", 8 * KB, [P, RING, 1024], F32R)
        wlo = at("wlo", 24 * KB, [P, RING, 1024], F32R)
        ahi = at("ahi", 40 * KB, [P, KT, S], F32R)
        alo = at("alo", 72 * KB, [P, KT, S], F32R)
        c0 = 104 * KB
        cons = at("cons", c0, [P, NCON])
        c0 += NCON * 4
        pars = at("pars", c0, [P, NPAR])
        c0 += -(-NPAR * 4 // 32) * 32
        small = at("small", c0, [P, 96])
        c0 += 96 * 4
        nw = -(-c0 // 32) * 32
        sh = nw + 20 * KB
        sq = at("sq", nw, [P, 2, S])
        xnf = at("xnf", nw + 8 * KB, [P, 2, S])
        acc = at("acc", nw + 16 * KB, [P, S])
        diag = at("diag", nw + 16 * KB, [P, S])
        sqb = at("sqb", sh, [P, 2, S])
        diagb = at("diagb", sh + 8 * KB, [P, S])
        hT = at("hT", sh, [P, KT, S])
        lr = at("lr", nw, [P, S])
        li = at("li", nw + 4 * KB, [P, S])
        lg = at("lg", nw + 8 * KB, [P, S])
        ls = at("ls", nw + 12 * KB, [P, S])
        lc = at("lc", nw + 16 * KB, [P, S])
        ylru = at("ylru", sh + 16 * KB, [P, LRU_T, S])
        xrp = at("xrp", sh + 32 * KB, [P, S + 3])
        xc = at("xc", sh + 36 * KB + 32, [P, S])
        pbuf = at("pbuf", nw, [P, 2, S])
        ptb = at("ptb", nw + 8 * KB, [P, 2, S])
        opair = at("opair", nw + 16 * KB, [P, TT, P])
        vtok = at("vtok", sh, [P, TT, HEADS * VH])
        qh = at("qh", sh + 16 * KB, [P, 2, S])
        kh = at("kh", sh + 24 * KB, [P, 2, S])
        rt1 = at("rt1", sh + 32 * KB, [P, S])
        rt2 = at("rt2", sh + 36 * KB + 32, [P, S])
        x0 = sh + 41 * KB
        lat = at("lat", x0, [P, 3, S])
        posi = at("posi", x0, [P, S], I32)
        kpe = at("kpe", x0 + 12 * KB, [P, S])
        tab = at("tab", x0 + 16 * KB, [P, S])
        wqb_s = at("wqb_s", x0 + 20 * KB, [P, 2, 1024])
        wlru_s = at("wlru_s", x0 + 20 * KB, [P, LRU_T, 2 * P])
        wlfix = at("wlfix", x0 + 24 * KB, [P, 2, 2 * P])
        wkvb_s = at("wkvb_s", x0 + 28 * KB, [P, 1024])
        wh = at("wh", x0 + 32 * KB, [P, 2, 3 * P])
        hid_hi = at("hid_hi", sh + 32 * KB, [P, 2, S], F32R)
        hid_lo = at("hid_lo", sh + 40 * KB, [P, 2, S], F32R)
        upg = at("upg", sh + 48 * KB, [P, S + 2])
        upv = at("upv", sh + 52 * KB + 32, [P, S + 2])
        cvg = at("cvg", sh + 56 * KB + 64, [P, S])
        cvv = at("cvv", sh + 60 * KB + 64, [P, S])
        vaug = at("vaug", sh, [P, TT, MH, MVA])
        q1 = sh + 33 * KB
        qT = at("qT", q1, [P, MH, S])
        kT = at("kT", q1 + 16 * KB, [P, MH, S])
        sigo = at("sigo", q1, [P, 2, HALF])
        m1 = q1 + 32 * KB
        cst = at("cst", m1, [P, MH, MVA])
        mw = at("mw", m1 + 4 * KB + 256, [P, 2, MH * P])
        ginfo = at("ginfo", m1 + 8 * KB + 256, [P, 640])
        gaT = at("gaT", m1 + 10 * KB + 768, [P, P])
        gAT = at("gAT", m1 + 11 * KB + 256, [P, P])
        gMT = at("gMT", m1 + 11 * KB + 768, [P, P])
        wgs = at("wgs", q1 + 20 * KB, [P, KT * P])
        wghi = at("wghi", q1 + 24 * KB, [P, KT * P], F32R)
        wglo = at("wglo", q1 + 28 * KB, [P, KT * P], F32R)
        grow = xnf[0:8, 1, :]
        junk = at("junk", m1 + 12 * KB + 768, [P, MV])
        gz, gt, gsp, ga, gnb = (ginfo[:, a:b] for a, b in ((0, 64), (64, 128), (128, 160), (160, 192), (192, 224)))
        gex = ginfo[:, 224:256]
        m_row, m_next, ml_row = ginfo[0:1, 256:288], ginfo[0:1, 260:292], ginfo[0:1, 292:324]
        g_exp = ginfo[:, 384:512]
        g_row = ginfo[0:1, 512:576]
        g_last = ginfo[0:32, 576:577]
        g_mcol = ginfo[0:32, 577:578]
        msw = at("msw", nw, [P, 2, MH * P])
        mkw = at("mkw", nw + 4 * KB, [P, 2, MH * P])
        mnum = at("mnum", nw + 8 * KB, [P, MH, MVA])
        mtx = at("mtx", nw + 12 * KB + 256, [P, MH * P])
        mtmp = at("mtmp", nw + 14 * KB + 256, [P, MVA])
        mhn = at("mhn", nw + 15 * KB + 512, [P, MH, MV])
        assert nw + 15 * KB + 512 + MH * MV * 4 <= sh

        ident = cons[:, C_ID:C_ID + P]
        ones = cons[:, C_ONE:C_ONE + P]
        tri = cons[:, C_TRI:C_TRI + P]
        maskq = cons[:, C_MASKQ:C_MASKQ + P]
        masks = cons[:, C_MASKS:C_MASKS + P]
        std, rstd = small[:, 0:8], small[:, 8:16]
        eps = small[:, 16:17]
        lcoef, lexp = small[:, 20:24], small[:, 80:84]
        l0, l1, l2, l3 = small[:, 24:28], small[:, 28:32], small[:, 32:36], small[:, 36:40]
        nmax, rsum, rinv = small[:, 40:42], small[:, 84:88], small[:, 44:46]
        mss, mden, mrd, mt2, msd, mrs, msc = (small[:, 48 + 4 * n:52 + 4 * n] for n in range(7))
        one_col = ones[:, 0:1]
        order = [6, 7, 0, 1, 4, 5, 2, 3]
        turns = [(4, 6, 2), (5, 0, 2), (7, 2, 4)]
        groups_before = [sum(1 if q < 4 else 2 for q in order[:k]) for k in range(TT)]
        group_parity = [g % 2 for g in groups_before]

        def groups_of(qt):
            return [(a, min(4, qt + 1 - a)) for a in range(0, qt + 1, 4)]

        def pcol(name, i, n=1):
            return pars[:, _cols[name] + i:_cols[name] + i + n]

        ps = psum("ps", [P, 8, HALF])

        w_landed = [sem(f"w_landed{n}") for n in range(STAGE)]
        w_hi, w_ready, w_used = sem("w_hi"), sem("w_ready"), sem("w_used")
        x_in = [sem(f"x_in{k}") for k in range(KT)]
        half_done = sem("half_done")

        block = ctx.enter_context(nc.Block())

        @block.sync
        def _(sp):
            sp.dma_start(cons[:], con).then_inc(sem("const_in"), 16)
            sp.dma_start(pars[:], par).then_inc(sem("const_in"), 16)

            def load(t, n, round_):
                if n is not None:
                    sp.wait_ge(w_ready, n)
                sp.dma_start(stage[:, round_, :], wt[bass.ds(t * P, P), :]).then_inc(w_landed[round_], 16)

            for t in range(STAGE):
                load(t, None, t)
            with sp.Fori(1, TILES // STAGE) as i:
                for r in range(STAGE):
                    load(i * STAGE + r, (i - 1) * STAGE + r + 1, r)
            for k in range(KT):
                sp.wait_ge(sem("fin_ready"), k + 1)
                sp.dma_start(out[k * P:(k + 1) * P, :], hT[:, k, :]).then_inc(sem("out_done"), 16)
            sp.wait_ge(sem("out_done"), 16 * KT)

        @block.gpsimd
        def _(pool):
            def split(r, landed, hi_count, used):
                slot, st = r % RING, r % STAGE
                pool.wait_ge(w_landed[st], landed)
                if used is not None:
                    pool.wait_ge(w_used, used)
                nc.gpsimd.tensor_tensor(whi[:, slot, :], stage[:, st, :], one_col.to_broadcast([P, 1024]),
                                        ALU.mult).then_inc(w_hi, 1)
                pool.wait_ge(w_hi, hi_count)
                nc.gpsimd.tensor_tensor(wlo[:, slot, :], stage[:, st, :], whi[:, slot, :].bitcast(F32),
                                        ALU.subtract).then_inc(w_ready, 1)

            pool.wait_ge(sem("const_in"), 32)
            for r in range(RING):
                split(r, 16 * (r // STAGE + 1), r + 1, None)
            with pool.Fori(1, TILES // RING) as i:
                for r in range(RING):
                    split(r, (i * (RING // STAGE) + r // STAGE + 1) * 16, i * RING + r + 1,
                          (i - 1) * RING + r + 1)

        norms = ["n0", "nk", "nq", "F0n", "n1", "F1n", "nf"]
        small_norms = {"nk": 1, "nq": 2}
        halves_first = ("n0",)

        def pieces(name):
            if name in halves_first:
                return [(k, slice(s * HALF, (s + 1) * HALF)) for s in range(2) for k in range(KT)]
            return [(k, slice(0, S)) for k in range(KT)]

        def nbase(name, kind):
            before = norms[:norms.index(name)]
            wide = [n for n in before if n not in small_norms]
            if kind == "sq":
                return sum(small_norms.get(n, KT + 1) for n in before)
            if kind == "acc":
                return (KT - 2) * len(wide)
            if kind == "mean":
                return len(before)
            if kind in ("diag", "bc"):
                return 2 * len(before)
            return sum(len(pieces(n)) for n in wide)

        def pe_mean(pe, name, bank, squares, dg):
            tiles = small_norms.get(name)

            def add(src, first, last, c):
                return nc.tensor.matmul(ps[:, bank, c:c + 1], src[:, c * P:(c + 1) * P], one_col,
                                        start=first and c == 0, stop=last, skip_group_check=True)

            if tiles is None:
                pe.wait_ge(sem("norm_acc"), nbase(name, "acc") + KT - 2)
                for c in range(TT):
                    add(acc, True, False, c)
                for s in range(2):
                    pe.wait_ge(sem("norm_sq"), nbase(name, "sq") + KT + s)
                    for c in range(4 * s, 4 * s + 4):
                        mm = add(squares[:, 1, :], False, True, c)
            else:
                for k in range(tiles):
                    pe.wait_ge(sem("norm_sq"), nbase(name, "sq") + k + 1)
                    for c in range(TT):
                        mm = add(squares[:, k, :], k == 0, k == tiles - 1, c)
            mm.then_inc(sem("norm_mean"), 1)
            for s in range(2):
                pe.wait_ge(sem("norm_diag"), nbase(name, "diag") + s + 1)
                nc.tensor.matmul(ps[:, bank + s, :], ones, dg[:, s * HALF:(s + 1) * HALF],
                                 start=True, stop=True).then_inc(sem("norm_bc"), 1)

        def act_squares(act, name, src, squares, ready=None):
            tiles = small_norms.get(name)
            scale = float(tiles or KT) ** -0.5 * float(P) ** -0.5
            for k in range(tiles or KT):
                if ready is not None:
                    ready(k)
                if k >= 2:
                    act.wait_ge(sem("norm_acc"), nbase(name, "acc") + max(1, k - 2))
                parts = 2 if tiles is None and k == KT - 1 else 1
                for s in range(parts):
                    tok = slice(s * S // parts, (s + 1) * S // parts)
                    nc.scalar.activation(squares[:, k % 2, tok], src(k)[:, tok], ACT.Square,
                                         scale=scale).then_inc(sem("norm_sq"), 1)

        def act_std(act, name, bank):
            act.wait_ge(sem("norm_mean"), nbase(name, "mean") + 1)
            nc.scalar.activation(std, ps[:, bank, 0:TT], ACT.Sqrt, bias=eps).then_inc(sem("norm_std"), 1)

        def act_round(act, name):
            for n, (k, tok) in enumerate(pieces(name)):
                act.wait_ge(sem("norm_xn"), nbase(name, "xn") + n + 1)
                nc.scalar.copy(ahi[:, k, tok], xnf[:, n % 2, 0:tok.stop - tok.start]).then_inc(sem("norm_hi"), 1)

        def dve_accumulate(dve, name, k):
            dve.wait_ge(sem("norm_sq"), nbase(name, "sq") + k + 1)
            if k >= 2:
                dve.wait_ge(sem("norm_acc"), nbase(name, "acc") + k - 1)
            nc.vector.tensor_tensor(acc[:, :], sq[:, 0, :] if k == 1 else acc[:, :], sq[:, k % 2, :],
                                    ALU.add).then_inc(sem("norm_acc"), 1)

        def dve_factor(dve, ch, name, dg):
            dve.wait_ge(sem("norm_std"), nbase(name, "mean") + 1)
            ch.link(nc.vector.reciprocal(rstd, std))
            for s in range(2):
                nc.vector.tensor_tensor(dg[:, s * HALF:(s + 1) * HALF].rearrange("p (c t) -> p c t", c=4),
                                        ident.unsqueeze(1).to_broadcast([P, 4, P]),
                                        rstd[:, 4 * s:4 * s + 4].unsqueeze(2).to_broadcast([P, 4, P]),
                                        ALU.mult).then_inc(sem("norm_diag"), 1)
            dve.wait_ge(sem("norm_bc"), nbase(name, "bc") + 2)

        def dve_norm(dve, ch, name, gain, bank):
            dve_factor(dve, ch, name, diag)
            work = pieces(name)

            def lo(n):
                k, tok = work[n]
                dve.wait_ge(sem("norm_hi"), nbase(name, "hi") + n + 1)
                nc.vector.tensor_tensor(alo[:, k, tok], xnf[:, n % 2, 0:tok.stop - tok.start],
                                        ahi[:, k, tok].bitcast(F32), ALU.subtract).then_inc(sem("norm_ready"), 1)

            for n, (k, tok) in enumerate(work):
                if n >= 2:
                    lo(n - 2)
                    dve.wait_ge(sem("norm_ready"), nbase(name, "ready") + n - 1)
                nc.vector.scalar_tensor_tensor(out=xnf[:, n % 2, 0:tok.stop - tok.start], in0=hT[:, k, tok],
                                               scalar=pcol(gain, k), in1=spread_banks(bank)[:, tok], op0=ALU.mult,
                                               op1=ALU.mult).then_inc(sem("norm_xn"), 1)
            lo(len(work) - 2)
            lo(len(work) - 1)

        def spread_banks(bank):
            return ps[:, bank:bank + 2, :].rearrange("p a b -> p (a b)")

        def product3(bank, wcols, slot, rhs_k, k_first, k_last, tok):
            hi, lo = whi[:, slot, wcols], wlo[:, slot, wcols]
            nc.tensor.matmul(bank, hi, rhs_k[0][:, tok], start=k_first, stop=False)
            nc.tensor.matmul(bank, hi, rhs_k[1][:, tok], start=False, stop=False)
            return nc.tensor.matmul(bank, lo, rhs_k[0][:, tok], start=False, stop=k_last)

        def m_tile(pe, t, slot, banks, evac=None, xn=None):
            pe.wait_ge(w_ready, t + 1)
            for s in range(2):
                if evac is not None:
                    evac(s)
                for k in range(KT):
                    if xn is not None:
                        xn(k, s)
                    mm = product3(ps[:, banks[s], :], slice(k * P, (k + 1) * P), slot,
                                  (ahi[:, k, :], alo[:, k, :]), k == 0, k == KT - 1,
                                  slice(s * HALF, (s + 1) * HALF))
                mm.then_inc(half_done if s == 0 else w_used, 1)

        def two_m_tiles(pe, t, ready):
            pe.wait_ge(w_ready, t + 2)
            for k in range(KT):
                ready(k)
                for n in range(2):
                    for s in range(2):
                        mm = product3(ps[:, 2 * n + s, :], slice(k * P, (k + 1) * P), (t + n) % RING,
                                      (ahi[:, k, :], alo[:, k, :]), k == 0, k == KT - 1,
                                      slice(s * HALF, (s + 1) * HALF))
                        if k == KT - 1:
                            mm.then_inc(half_done if s == 0 else w_used, 1)

        def pe_mlp(pe, L, t0):
            up_read, added = sem(L + "up_read"), sem(L + "added")

            def up(t, slot, n, gv):
                m_tile(pe, t, slot, (2 * gv, 2 * gv + 1),
                       lambda s: pe.wait_ge(up_read, n * 4 + 2 * gv + s - 3))

            def down(t, slots, g):
                pe.wait_ge(w_ready, t + 2)
                pe.wait_ge(sem(L + "hid"), g * 2 + 2)
                for m in range(KT):
                    for s in range(2):
                        n = m * 2 + s
                        pe.wait_ge(added, g * 2 * KT + (n + 1))
                        for j in range(2):
                            mm = product3(ps[:, 4 + n % 4, :], slice(m * P, (m + 1) * P), slots[j],
                                          (hid_hi[:, j, :], hid_lo[:, j, :]), j == 0, j == 1,
                                          slice(s * HALF, (s + 1) * HALF))
                            if n == 2 * KT - 1:
                                mm.then_inc(w_used, 1)
                        if n < 2 * KT - 1:
                            mm.then_inc(sem(L + "down"), 1)

            def pair(t, tm, g, last=False):
                for gv in range(2):
                    up(t + gv, (tm + gv) % RING, g * 2 + 1, gv)
                if not last:
                    for gv in range(2):
                        up(t + 2 + gv, (tm + 2 + gv) % RING, g * 2 + 2, gv)
                d = 2 if last else 4
                down(t + d, ((tm + d) % RING, (tm + d + 1) % RING), g)

            two_m_tiles(pe, t0, lambda k: pe.wait_ge(sem("norm_ready"), nbase(L + "n", "ready") + k + 1))
            with pe.Fori(0, (FG - 1) // 2) as i:
                for j in range(2):
                    pair(i * 12 + (t0 + 2 + 6 * j), (t0 + 2 + 6 * j) % RING, i * 2 + j)
            pair(t0 + 2 + 6 * (FG - 1), (t0 + 2 + 6 * (FG - 1)) % RING, FG - 1, last=True)

        def half_base(t):
            n = t
            for a, b in ((T_L1_V, T_L1_V + 8),):
                n -= max(0, min(t, b) - a)
            for f in (T_FFN0, T_FFN1):
                if t >= f + 3 * FT:
                    n -= FT
            return n

        def act_mlp(act, ch, L, t0):
            hb = half_base(t0)

            def evac(n, t, gv, first=False):
                buf = upg if gv == 0 else upv
                if not first:
                    act.wait_ge(sem(L + "conv"), n * 2 + gv - 1)
                for s in range(2):
                    if s == 0:
                        act.wait_ge(half_done, n * 2 + (hb + gv + 1))
                    else:
                        act.wait_ge(w_used, t + gv + 1)
                    nc.scalar.copy(buf[:, 2 + s * HALF:2 + (s + 1) * HALF],
                                   ps[:, 2 * gv + s, :]).then_inc(sem(L + "up_read"), 1)

            def finish(n, j, down=None):
                act.wait_ge(sem(L + "conv"), n * 2 + 2)
                nc.scalar.activation(cvg[:, :], cvg[:, :], ACT.Silu).then_inc(sem(L + "silu"), 1)
                act.wait_ge(sem(L + "prod"), n + 1)
                if down is not None:
                    act.wait_ge(w_used, down)
                nc.scalar.copy(hid_hi[:, j, :], cvv[:, :]).then_inc(sem(L + "hid_hi"), 1)

            def pair(t, g, last=False):
                for gv in range(2):
                    evac(g * 2 + 1, t, gv)
                finish(g * 2 + 1, 1)
                if not last:
                    for gv in range(2):
                        evac(g * 2 + 2, t + 2, gv)
                    finish(g * 2 + 2, 0, down=t + 6)

            for gv in range(2):
                evac(0, t0, gv, first=True)
            finish(0, 0)
            with act.Fori(0, FG - 1) as g:
                pair(g * 6 + (t0 + 2), g)
            pair(t0 + 2 + 6 * (FG - 1), FG - 1, last=True)

        def dve_mlp(dve, ch, L, t0, layer, next_norm):
            col = _cols[f"conv{layer}"]

            def conv_step(n, gv, i):
                def w(i):
                    return pars[:, bass.ds(n * 8 + (col + gv * 4 + i), 1)]
                src, dst = (upg, cvg) if gv == 0 else (upv, cvv)
                if i == 0:
                    dve.wait_ge(sem(L + "up_read"), n * 4 + 2 * gv + 2)
                    ch.link(nc.vector.tensor_scalar(dst[:, :], src[:, 0:S], w(0), w(3), ALU.mult, ALU.add))
                elif i == 1:
                    ch.link(nc.vector.scalar_tensor_tensor(out=dst[:, :], in0=src[:, 1:S + 1], scalar=w(1),
                                                           in1=dst[:, :], op0=ALU.mult, op1=ALU.add))
                else:
                    nc.vector.scalar_tensor_tensor(out=dst[:, :], in0=src[:, 2:S + 2], scalar=w(2), in1=dst[:, :],
                                                   op0=ALU.mult, op1=ALU.add).then_inc(sem(L + "conv"), 1)

            def conv(n, gv):
                for i in range(3):
                    conv_step(n, gv, i)

            def prod(n):
                dve.wait_ge(sem(L + "silu"), n + 1)
                nc.vector.tensor_tensor(cvv[:, :], cvg[:, :], cvv[:, :], ALU.mult).then_inc(sem(L + "prod"), 1)

            def lo(n, j):
                dve.wait_ge(sem(L + "hid_hi"), n + 1)
                nc.vector.tensor_tensor(hid_lo[:, j, :], cvv[:, :], hid_hi[:, j, :].bitcast(F32),
                                        ALU.subtract).then_inc(sem(L + "hid"), 1)
                dve.wait_ge(sem(L + "hid"), n + 1)

            def add(g, t_last, last, between):
                for m in range(KT):
                    for s in range(2):
                        n = m * 2 + s
                        if n < 2 * KT - 1:
                            dve.wait_ge(sem(L + "down"), g * (2 * KT - 1) + (n + 1))
                        else:
                            dve.wait_ge(w_used, t_last + 1)
                        h = hT[:, m, s * HALF:(s + 1) * HALF]
                        nc.vector.tensor_tensor(h, h, ps[:, 4 + n % 4, :], ALU.add).then_inc(sem(L + "added"), 1)
                        if n in between:
                            between[n]()
                    if last and m >= 2:
                        dve_accumulate(dve, next_norm, m - 1)

            def pair(t, g, last=False):
                for gv in range(2):
                    conv(g * 2 + 1, gv)
                prod(g * 2 + 1)
                lo(g * 2 + 1, 1)
                between = {}
                if not last:
                    conv(g * 2 + 2, 0)
                    between = {n + 1: lambda n=n: conv_step(g * 2 + 2, 1, n) for n in range(3)}
                    between[7] = lambda: prod(g * 2 + 2)
                add(g, t + (3 if last else 5), last, between)
                if not last:
                    lo(g * 2 + 2, 0)

            dve.sem_inc(sem(L + "added"), 4)
            nc.vector.memset(upg[:, 0:2], 0.0)
            ch.link(nc.vector.memset(upv[:, 0:2], 0.0))
            for gv in range(2):
                conv(0, gv)
            prod(0)
            lo(0, 0)
            with dve.Fori(0, FG - 1) as g:
                ch.enter(g, 8)
                pair(g * 6 + (t0 + 2), g)
            ch.leave(FG - 1)
            pair(t0 + 2 + 6 * (FG - 1), FG - 1, last=True)

        def m_tiles(pe, t0, count, read, ready):
            with pe.Fori(0, count // 4) as i:
                for b in range(4):
                    m_tile(pe, i * 4 + (t0 + b), (t0 + b) % RING, (2 * (b % 2), 2 * (b % 2) + 1),
                           lambda s: pe.wait_ge(read, i * 8 + (2 * b + s + 1)),
                           ready if b == 0 else None)

        def dve_out(dve, L, t0, x_count, next_norm):
            hb = half_base(t0)
            for m in range(KT):
                dve.wait_ge(x_in[m], x_count)
                for s in range(2):
                    if s == 0:
                        dve.wait_ge(half_done, hb + m + 1)
                    else:
                        dve.wait_ge(w_used, t0 + m + 1)
                    h = hT[:, m, s * HALF:(s + 1) * HALF]
                    nc.vector.tensor_tensor(h, h, ps[:, 2 * (m % 2) + s, :], ALU.add).then_inc(sem(L + "res"), 1)
                if m >= 2:
                    dve_accumulate(dve, next_norm, m - 1)

        @block.tensor
        def _(pe):
            for name in ("lru_pre", "yt"):
                pe.sem_inc(sem(name), 1)
            pe.sem_inc(sem("o"), 2)
            pe.wait_ge(sem("const_in"), 32)
            pe_mean(pe, "n0", 6, sq, diag)
            with pe.Fori(0, LRU_T // 2) as i:
                for jj in range(2):
                    j = i * 2 + jj
                    t = i * 4 + 2 * jj
                    m_tile(pe, t, 2 * jj, (0, 1), lambda s: pe.wait_ge(sem("xr_read"), j * 2 + 1),
                           lambda k, s: pe.wait_ge(sem("norm_ready"), s * KT + k + 1))
                    m_tile(pe, t + 1, 2 * jj + 1, (2, 3), lambda s: pe.wait_ge(sem("gelu"), j + 1))
                    pe.wait_ge(sem("xc_ready"), j + 1 + 1)
                    pe.wait_ge(sem("wlfix_in"), j + 1)
                    pe.wait_ge(sem("lru_r"), j + 1)
                    pe.wait_ge(sem("lru_i"), j + 1)
                    for g in range(2):
                        for s in range(2):
                            nc.tensor.matmul(ps[:, 4 + 2 * g + s, :], wlfix[:, jj, g * P:(g + 1) * P],
                                             xc[:, s * HALF:(s + 1) * HALF], start=True, stop=True
                                             ).then_inc(sem("lru_pre"), 1)
            t = 2 * LRU_T
            pe.wait_ge(sem("xr_read"), 2 * LRU_T + 1)
            m_tile(pe, t, t % RING, (0, 1))
            pe.wait_ge(sem("gelu"), LRU_T + 1)
            m_tile(pe, t + 1, (t + 1) % RING, (2, 3))
            pe_mean(pe, "nk", 0, sqb, diagb)
            pe.wait_ge(sem("lru_r"), LRU_T + 1)
            m_tile(pe, t + 2, (t + 2) % RING, (4, 5))
            pe.wait_ge(sem("lru_i"), LRU_T + 1)
            m_tile(pe, t + 3, (t + 3) % RING, (6, 7))
            pe_mean(pe, "nq", 4, sqb, diagb)
            pe.wait_ge(sem("wb_in"), 32)
            pe.wait_ge(sem("kv_normed"), 1)
            wv = wkvb_s[:, :].rearrange("p (h e) -> p h e", h=HEADS)[:, :, NOPE:NOPE + VH]
            for c in range(TT):
                if c >= 2:
                    pe.wait_ge(sem("v_read"), c - 1)
                nc.tensor.matmul(ps[:, 2 + c % 2, :], lat[:, 2, c * P:(c + 1) * P], wv,
                                 start=True, stop=True).then_inc(sem("v_mm"), 1)

            def project(h, par, part):
                if part == 0:
                    pe.wait_ge(sem("wh_in"), h * 3 + 3)
                pe.wait_ge(sem("proj_read"), h * 4 + part)
                s = part % 2
                tok = slice(s * HALF, (s + 1) * HALF)
                if part < 2:
                    for k in range(2):
                        mm = nc.tensor.matmul(ps[:, 0, :], wh[:, par, k * P:(k + 1) * P], lat[:, k, tok],
                                              start=(k == 0), stop=(k == 1))
                else:
                    mm = nc.tensor.matmul(ps[0:NOPE, 0, :], wh[:, par, 2 * P:2 * P + NOPE], lat[:, 2, tok],
                                          start=True, stop=True)
                mm.then_inc(sem("proj"), 1)

            def scores(h, par, k, step):
                qt = order[k]
                if k == 0:
                    pe.wait_ge(sem("proj_read"), h * 4 + 4)
                if not isinstance(step, int) or step >= 2:
                    pe.wait_ge(sem("probs"), (step - 1) + 1)
                b = 1 + 2 * (k % 2)
                n = (qt + 1) * P
                for a in range(0, n, HALF):
                    w = min(HALF, n - a)
                    mm = nc.tensor.matmul(ps[:, b + a // HALF, 0:w], qh[0:QK, par, qt * P:(qt + 1) * P],
                                          kh[0:QK, par, a:a + w], start=True, stop=True)
                mm.then_inc(sem("scores"), 1)

            def transpose(k, step, grp):
                pe.wait_ge(sem("probs"), step + 1 + 1)
                for n, (a, w) in enumerate(groups_of(order[k])):
                    pe.wait_ge(sem("pt_read"), grp + n + 1)
                    for kb in range(a, a + w):
                        mm = nc.tensor.transpose(ps[:, 5 + (group_parity[k] + n) % 2, (kb - a) * P:(kb - a + 1) * P],
                                                 pbuf[:, k % 2, kb * P:(kb + 1) * P], ident)
                    mm.then_inc(sem("pt"), 1)

            def weigh(h, k, step, grp):
                pe.wait_ge(sem("o_read"), step + 1)
                qt = order[k]
                o = ps[:, 7, 0:VH]
                for n, (a, w) in enumerate(groups_of(qt)):
                    pe.wait_ge(sem("pt_read"), (grp + (n + 2)) + 1)
                    for kb in range(a, a + w):
                        mm = nc.tensor.matmul(o, ptb[:, k % 2, kb * P:(kb + 1) * P],
                                              vtok[:, kb, bass.ds(h * VH, VH)], start=(kb == 0), stop=(kb == qt),
                                              skip_group_check=True)
                mm.then_inc(sem("o"), 1)

            def turn(p, n, last):
                _, first, blocks = turns[n]
                done = max(order.index(b) for b in range(first, first + blocks))
                pe.wait_ge(sem("o_read"), (p * 16 + (8 + done + 1)) + 1)
                if n == 0:
                    pe.wait_ge(sem("proj_read"), p * 8 + (8 if last else 12))
                else:
                    pe.wait_ge(sem("y_read"), p * 3 + n + 1)
                for b in range(blocks):
                    mm = nc.tensor.transpose(ps[:, 0, b * P:(b + 1) * P], opair[:, first + b, :], ident)
                mm.then_inc(sem("yt"), 1)

            def head_pair(p, last=False):
                for i in range(16):
                    par, k = i // 8, i % 8
                    step = p * 16 + i
                    grp = p * 24 + (12 * par + groups_before[k])
                    transpose(k, step, grp)
                    j = i + 2
                    if not (last and j >= 16):
                        scores(p * 2 + j // 8, (j // 8) % 2, j % 8, p * 16 + j)
                    if i == 0:
                        pe.wait_ge(sem("y_read"), p * 3 + 1)
                    if k < 4 and not (last and par == 1):
                        project(p * 2 + par + 1, 1 - par, k)
                    weigh(p * 2 + par, k, step, grp)
                    for n, (slot, _, _) in enumerate(turns):
                        if par == 1 and slot == k:
                            turn(p, n, last)

            pe.wait_ge(sem("v_read"), TT)
            pe.wait_ge(sem("q_normed"), 2)
            pe.wait_ge(sem("kpe_ready"), 1)
            for part in range(4):
                project(0, 0, part)
            for i in range(2):
                scores(0, 0, i, i)
            with pe.Fori(0, HEADS // 2 - 1) as p:
                head_pair(p)
            head_pair(HEADS // 2 - 1, last=True)
            pe.wait_ge(sem("lru_split"), LRU_T)
            pe.wait_ge(sem("y_read"), len(turns) * (HEADS // 2) + 1)
            m_tiles(pe, T_L0_OUT, KT, sem("L0res"), None)
            pe_mean(pe, "F0n", 6, sq, diag)
            pe_mlp(pe, "F0", T_FFN0)

            pe_mean(pe, "n1", 4, sq, diag)

            def gate_product():
                pe.wait_ge(sem("wg_split"), 1)
                for s in range(2):
                    for k in range(KT):
                        wk, tok = slice(k * P, (k + 1) * P), slice(s * HALF, (s + 1) * HALF)
                        nc.tensor.matmul(ps[:, 4 + s, :], wghi[:, wk], ahi[:, k, tok], start=(k == 0), stop=False)
                        nc.tensor.matmul(ps[:, 4 + s, :], wghi[:, wk], alo[:, k, tok], start=False, stop=False)
                        mm = nc.tensor.matmul(ps[:, 4 + s, :], wglo[:, wk], ahi[:, k, tok], start=False,
                                              stop=(k == KT - 1))
                    mm.then_inc(sem("g_mm"), 1)

            def gates_turn():
                pe.wait_ge(sem("g_in"), 1)
                for c in range(TT):
                    mm = nc.tensor.transpose(ps[:, 6, c * 8:(c + 1) * 8], grow[:, c * P:(c + 1) * P], ident[0:8, 0:8])
                mm.then_inc(sem("g_pre"), 1)

            def gates_sum():
                pe.wait_ge(sem("g_sp"), 1)
                nc.tensor.matmul(ps[:, 5, 0:TT * MH], tri, gsp, start=True, stop=True
                                 ).then_inc(sem("g_cum"), 1)

            def gates_rows():
                pe.wait_ge(sem("g_a"), 2)
                nc.tensor.transpose(ps[0:32, 6, 0:P], ga, ident)
                nc.tensor.transpose(ps[0:32, 6, P:2 * P], gnb, ident).then_inc(sem("g_turned"), 1)

            def gates_ends():
                pe.wait_ge(sem("g_max"), 2)
                nc.tensor.matmul(ps[0:1, 7, 0:32], gAT[0:32, P - 1:P], ident[0:32, 0:32], start=True, stop=True)
                nc.tensor.matmul(ps[0:1, 7, 32:64], g_last, ident[0:32, 0:32], start=True, stop=True
                                 ).then_inc(sem("g_rows"), 1)

            def gates_spread():
                pe.wait_ge(sem("g_m"), 1)
                nc.tensor.matmul(ps[0:32, 7, 64:65], m_row, ones[0:1, 0:1], start=True, stop=True)
                nc.tensor.matmul(ps[:, 7, 128:160], ones[0:1, :], m_row, start=True, stop=True)
                nc.tensor.matmul(ps[:, 7, 160:192], ones[0:1, :], ml_row, start=True, stop=True
                                 ).then_inc(sem("g_spread"), 1)

            def gates_stabilisers():
                pe.wait_ge(sem("g_MT"), 1)
                nc.tensor.transpose(ps[:, 7, 256:288], gMT[0:32, :], ident[0:32, 0:32]).then_inc(sem("g_M"), 1)

            behind = [None, None, gates_turn, gates_sum, gates_rows, gates_ends, gates_spread,
                      gates_stabilisers]
            two_m_tiles(pe, T_L1, lambda k: pe.wait_ge(sem("norm_ready"), nbase("n1", "ready") + k + 1))
            gate_product()
            for h in range(1, MH):
                for qk in range(2):
                    t = T_L1 + 2 * h + qk
                    m_tile(pe, t, t % RING, (2 * qk, 2 * qk + 1),
                           lambda s: pe.wait_ge(sem("l1_read"), 4 * h + 2 * qk + s - 3))
                    behind[2 * h + qk]()

            pe.wait_ge(sem("l1_read"), 4 * MH)
            pe.wait_ge(sem("g_e"), 1)

            with pe.Fori(0, 2) as n:
                for j in range(4):
                    slot = (T_L1_V + j) % RING
                    pe.wait_ge(w_ready, n * 4 + (T_L1_V + j + 1))
                    for c in range(TT):
                        if j == 0:
                            pe.wait_ge(sem("l1_read"), n * 8 + (4 * MH + c + 1 - TT))
                        for kk in range(2):
                            k = 2 * j + kk
                            tok = slice(c * P, (c + 1) * P)
                            cols = slice(kk * HALF, (kk + 1) * HALF)
                            nc.tensor.matmul(ps[:, c, :], ahi[:, k, tok], whi[:, slot, cols], start=(k == 0),
                                             stop=False)
                            nc.tensor.matmul(ps[:, c, :], alo[:, k, tok], whi[:, slot, cols], start=False,
                                             stop=False)
                            mm = nc.tensor.matmul(ps[:, c, :], ahi[:, k, tok], wlo[:, slot, cols], start=False,
                                                  stop=(k == KT - 1))
                        if c == TT - 1:
                            mm.then_inc(w_used, 1)
                        elif j == 3:
                            mm.then_inc(sem("v1_mm"), 1)
            pe.wait_ge(sem("l1_read"), 4 * MH + 2 * TT)

            def chunk_scores(c):
                tok = slice(c * P, (c + 1) * P)
                pe.wait_ge(sem("mtx"), c + 1)
                if c >= 1:
                    pe.wait_ge(sem("mw"), 4 * c)
                nc.tensor.matmul(ps[:, 0, :], ones[0:32, :], mtx[0:32, :], start=True, stop=False,
                                 skip_group_check=True)
                for h in range(MH):
                    mm = nc.tensor.matmul(ps[:, 0, h * P:(h + 1) * P], ident, masks, start=False, stop=(h == 3),
                                          skip_group_check=True)
                mm.then_inc(sem("m_bc"), 1)
                if c >= 1:
                    pe.wait_ge(sem("msw"), c)
                    pe.wait_ge(sem("mkw"), 4 * c)
                for h in range(MH):
                    mm = nc.tensor.matmul(ps[:, 1, h * P:(h + 1) * P], kT[:, h, tok], qT[:, h, tok],
                                          start=(h == 0), stop=(h == MH - 1), skip_group_check=True)
                mm.then_inc(sem("m_qk"), 1)
                for h in range(MH):
                    mm = nc.tensor.transpose(ps[:, 2, h * P:(h + 1) * P], kT[:, h, tok], ident)
                mm.then_inc(sem("m_kt"), 1)

            def chunk_head(c, h):
                tok = slice(c * P, (c + 1) * P)
                n = 4 * c + h
                if n >= 1:
                    pe.wait_ge(sem("m_inter_read"), n)
                    if c >= 1:
                        pe.wait_ge(sem("m_state"), n - 3)
                nc.tensor.matmul(ps[:, 5, 0:MV + 1], qT[:, h, tok], cst[:, h, 0:MV + 1],
                                 start=True, stop=True).then_inc(sem("m_inter"), 1)
                if n >= 2:
                    pe.wait_ge(sem("m_num_read"), n - 1)
                pe.wait_ge(sem("msw"), c + 1)
                nc.tensor.matmul(ps[:, 3 + h % 2, 0:MV + 1], msw[:, c % 2, h * P:(h + 1) * P],
                                 vaug[:, c, h, 0:MV + 1], start=True, stop=True).then_inc(sem("m_num"), 1)
                if n >= 1:
                    pe.wait_ge(sem("m_state"), n)
                pe.wait_ge(sem("mkw"), 4 * c + h + 1)
                nc.tensor.matmul(ps[:, 6, 0:MV + 1], mkw[:, c % 2, h * P:(h + 1) * P],
                                 vaug[:, c, h, 0:MV + 1], start=True, stop=True).then_inc(sem("m_kv"), 1)

            def chunk_turn(c):
                for b in range(2):
                    n = 2 * c + b
                    pe.wait_ge(sem("m_hn"), c + 1)
                    if n >= 1:
                        pe.wait_ge(sem("m_y"), 4 * n)
                    for i in range(4):
                        h, e = 2 * b + i // 2, i % 2
                        mm = nc.tensor.transpose(ps[:, 7, i * P:(i + 1) * P], mhn[:, h, e * P:(e + 1) * P], ident)
                    mm.then_inc(sem("m_turned"), 1)

            pe.wait_ge(sem("cst0"), 1)
            chunk_scores(0)
            for c in range(TT):
                if c + 1 < TT:
                    chunk_scores(c + 1)
                for h in range(MH):
                    chunk_head(c, h)
                if c >= 1:
                    chunk_turn(c - 1)
            chunk_turn(TT - 1)

            pe.wait_ge(sem("m_y"), 8 * TT)

            m_tiles(pe, T_L1_O, KT, sem("sigo"), None)
            m_tiles(pe, T_L1_OUT, KT, sem("L1res"), lambda k, s: pe.wait_ge(sem("L1mix"), k + 1))
            pe_mean(pe, "F1n", 6, sq, diag)
            pe_mlp(pe, "F1", T_FFN1)
            pe_mean(pe, "nf", 0, sq, diag)

        @block.scalar
        def _(act):
            ch = Chain(act, sem("act_chain"))
            for name in ("xr_read", "gelu", "lru_r", "lru_i", "probs"):
                act.sem_inc(sem(name), 1)
            act.sem_inc(sem("pt_read"), 2)
            act.dma_start(posi[64:128, :], pos[64:128, :]).then_inc(sem("pos_in"), 16)
            for k in range(KT):
                act.dma_start(hT[:, k, :], xt[k * P:(k + 1) * P, :]).then_inc(x_in[k], 16)
            act.dma_start(wlru_s[:], wlru).then_inc(sem("wlru_in"), 16)
            act.dma_start(wkvb_s[:], wkvb).then_inc(sem("wb_in"), 16)
            act.wait_ge(sem("const_in"), 32)
            act.wait_ge(sem("eps_set"), 1)
            act_squares(act, "n0", lambda k: hT[:, k, :], sq, lambda k: act.wait_ge(x_in[k], 16))
            act_std(act, "n0", 6)
            act_round(act, "n0")
            act.wait_ge(sem("lam_abs"), 1)
            nc.scalar.activation(l1, l0, ACT.Exp).then_inc(sem("lam_exp"), 1)
            def lru_par(j, n):
                return pars[:, bass.ds(j * 8 + (_cols["lru"] + n), 1)]

            act.wait_ge(sem("wlru_in"), 16)
            act.wait_ge(sem("lcoef"), 1)
            act.wait_ge(sem("angles"), 1)
            nc.scalar.activation(tab[64:128, :], lat[64:128, 1, :], ACT.Sin,
                                 scale=cons[64:128, C_ROPE + 3:C_ROPE + 4]).then_inc(sem("tab_ready"), 1)
            with act.Fori(0, LRU_T // 2) as i:
                for jj in range(2):
                    j = i * 2 + jj
                    t = i * 4 + 2 * jj
                    act.wait_ge(sem("lru_pre"), j * 4 + 1)
                    nc.scalar.copy(wlfix[:, jj, :], wlru_s[:, bass.ds(j, 1), :].rearrange("p a b -> p (a b)")
                                   ).then_inc(sem("wlfix_in"), 1)
                    act.wait_ge(sem("xc_ready"), j + 1)
                    act.wait_ge(half_done, t + 1)
                    nc.scalar.copy(xrp[:, 3:3 + HALF], ps[:, 0, :]).then_inc(sem("xr_read"), 1)
                    act.wait_ge(w_used, t + 1)
                    nc.scalar.copy(xrp[:, 3 + HALF:3 + S], ps[:, 1, :]).then_inc(sem("xr_read"), 1)
                    act.wait_ge(sem("ylru"), j + 1)
                    act.wait_ge(w_used, t + 2)
                    nc.scalar.activation(lg[:, :], spread_banks(2), ACT.Gelu_apprx_tanh).then_inc(sem("gelu"), 1)
                    act.wait_ge(sem("lru_pre"), j * 4 + 2 + 1)
                    nc.scalar.activation(lr[:, :], spread_banks(4), ACT.Sigmoid,
                                         bias=lru_par(j, 5)).then_inc(sem("lru_r"), 1)
                    act.wait_ge(sem("lru_pre"), j * 4 + 4 + 1)
                    nc.scalar.activation(li[:, :], spread_banks(6), ACT.Sigmoid,
                                         bias=lru_par(j, 6)).then_inc(sem("lru_i"), 1)
                    act.wait_ge(sem("lru_r"), j + 1 + 1)
                    nc.scalar.activation(lc[:, :], lr[:, :], ACT.Exp,
                                         scale=small[:, bass.ds(j + 80, 1)]).then_inc(sem("lru_a"), 1)
                    act.wait_ge(sem("lru_a"), j + 1)
                    nc.scalar.activation(lr[:, :], lr[:, :], ACT.Tanh,
                                         scale=small[:, bass.ds(j + 20, 1)]).then_inc(sem("lru_u"), 1)
                    act.wait_ge(sem("lru_u"), j + 1)
                    nc.scalar.activation(ls[:, :], lr[:, :], ACT.Sqrt).then_inc(sem("lru_sq"), 1)
            t = 2 * LRU_T
            act.wait_ge(sem("lru_pre"), 4 * LRU_T + 1)
            act.dma_start(wqb_s[:], wqb).then_inc(sem("wb_in"), 16)
            act.wait_ge(sem("tab_ready"), 1)

            def latent(n, t, banks):
                act.wait_ge(w_used, t + 1)
                nc.scalar.copy(lat[:, n, :], spread_banks(banks)).then_inc(sem("lat_in"), 1)

            latent(2, t, 0)
            act.wait_ge(sem("lat_in"), 1)
            act_squares(act, "nk", lambda k: lat[:, 2, :], sqb)
            latent(0, t + 1, 2)
            act_std(act, "nk", 0)
            latent(1, t + 2, 4)
            act_squares(act, "nq", lambda k: lat[:, k, :], sqb, lambda k: act.wait_ge(sem("lat_in"), k + 2))
            act_std(act, "nq", 4)
            act.wait_ge(w_used, T_L0_OUT)
            for j in range(LRU_T):
                act.wait_ge(sem("ylru"), j + 1 + 1)
                nc.scalar.copy(ahi[:, j, :], ylru[:, j, :]).then_inc(sem("lru_hi"), 1)
            for c in range(TT):
                act.wait_ge(sem("v_mm"), c + 1)
                nc.scalar.copy(vtok[:, c, :], ps[:, 2 + c % 2, :]).then_inc(sem("v_read"), 1)

            act.wait_ge(sem("wb_in"), 32)

            def head_weights(h, par):
                if not isinstance(h, int) or h >= 2:
                    act.wait_ge(sem("proj"), h * 4 - 4)
                for n in range(2):
                    nc.scalar.copy(wh[:, par, n * P:(n + 1) * P],
                                   wqb_s[:, n, bass.ds(h * P, P)]).then_inc(sem("wh_in"), 1)
                nc.scalar.copy(wh[:, par, 2 * P:3 * P], wkvb_s[:, bass.ds(h * P, P)]).then_inc(sem("wh_in"), 1)

            def nope(h, par, part):
                s = part % 2
                tok = slice(s * HALF, (s + 1) * HALF)
                act.wait_ge(sem("proj"), h * 4 + (part + 1))
                if part < 2:
                    nc.scalar.mul(qh[0:NOPE, par, tok], ps[0:NOPE, 0, :], QK_SCALE).then_inc(sem("q_nope"), 1)
                else:
                    nc.scalar.copy(kh[0:NOPE, par, tok], ps[0:NOPE, 0, :]).then_inc(sem("proj_read"), 1)

            def exps(k, step):
                n = (order[k] + 1) * P
                act.wait_ge(sem("nmax"), step + 1)
                b = 1 + 2 * (k % 2)
                sc = ps[:, b:b + 2, :].rearrange("p a b -> p (a b)")[:, 0:n]
                nc.scalar.activation(pbuf[:, k % 2, 0:n], sc, ACT.Exp, bias=nmax[:, k % 2:k % 2 + 1],
                                     accum_out=rsum[:, k % 4:k % 4 + 1]).then_inc(sem("probs"), 1)

            def turned(k, step, grp):
                act.wait_ge(sem("o"), step + 1)
                for n, (a, w) in enumerate(groups_of(order[k])):
                    act.wait_ge(sem("pt"), grp + (n + 1))
                    nc.scalar.copy(ptb[:, k % 2, a * P:(a + w) * P],
                                   ps[:, 5 + (group_parity[k] + n) % 2, 0:w * P]).then_inc(sem("pt_read"), 1)

            def y_hi(p, n):
                _, first, blocks = turns[n]
                act.wait_ge(sem("yt"), (p * 3 + (n + 1)) + 1)
                nc.scalar.copy(ahi[:, bass.ds(p + LRU_T, 1), first * P:(first + blocks) * P].rearrange("p a b -> p (a b)"),
                               ps[:, 0, 0:blocks * P]).then_inc(sem("y_hi"), 1)

            def head_pair(p, last=False):
                for i in range(16):
                    par, k = i // 8, i % 8
                    if not (last and i == 15):
                        exps((i + 1) % 8, p * 16 + (i + 1))
                    turned(k, p * 16 + i, p * 24 + (12 * par + groups_before[k]))
                    for n, (slot, _, _) in enumerate(turns):
                        if par == 1 and k == min(slot + 1, 7):
                            y_hi(p, n)
                    if k < 4 and not (last and par == 1):
                        nope(p * 2 + par + 1, 1 - par, k)
                    if k == 4 and not last:
                        head_weights(p * 2 + par + 2, par)

            act.wait_ge(sem("kpe_in"), 2)
            act.wait_ge(sem("ylru"), LRU_T + 1)
            head_weights(0, 0)
            head_weights(1, 1)
            for part in range(4):
                nope(0, 0, part)
            exps(0, 0)
            with act.Fori(0, HEADS // 2 - 1) as p:
                head_pair(p)
            head_pair(HEADS // 2 - 1, last=True)
            act.wait_ge(sem("o"), 8 * HEADS + 2)
            for k in range(KT):
                act.dma_start(hT[:, k, :], xt[k * P:(k + 1) * P, :]).then_inc(x_in[k], 16)
            act_squares(act, "F0n", lambda k: hT[:, k, :], sq, lambda k: act.wait_ge(sem("L0res"), 2 * k + 6))
            act_std(act, "F0n", 6)
            act_round(act, "F0n")
            act_mlp(act, ch, "F0", T_FFN0)

            last_added = 2 * KT * (FG - 1) + 4
            act_squares(act, "n1", lambda k: hT[:, k, :], sq,
                        lambda k: act.wait_ge(sem("F0added"), last_added + 2 * k + 2))
            act.dma_start(spill, hT[:, :, :].rearrange("p a b -> p (a b)")).then_inc(sem("spilled"), 16)
            act.dma_start(wgs[:], wg).then_inc(sem("wg_in"), 16)
            act_std(act, "n1", 4)
            act_round(act, "n1")
            act.wait_ge(sem("wg_in"), 16)
            nc.scalar.copy(wghi[:], wgs[:]).then_inc(sem("wg_hi"), 1)

            hb = half_base(T_L1)

            def head_part(h, qk):
                for s in range(2):
                    if s == 0:
                        act.wait_ge(half_done, hb + 2 * h + qk + 1)
                    else:
                        act.wait_ge(w_used, T_L1 + 2 * h + qk + 1)
                    tok = slice(s * HALF, (s + 1) * HALF)
                    if qk == 0:
                        ins = nc.scalar.mul(qT[:, h, tok], ps[:, s, :], float(MQK) ** -0.5)
                    else:
                        ins = nc.scalar.copy(kT[:, h, tok], ps[:, 2 + s, :])
                    ins.then_inc(sem("l1_read"), 1)

            head_part(0, 0)
            head_part(0, 1)
            act.wait_ge(sem("g_mm"), 2)
            nc.scalar.copy(grow, spread_banks(4)[0:8, :]).then_inc(sem("g_in"), 1)
            head_part(1, 0)
            tv = gt.rearrange("p (c g) -> p c g", c=TT)
            act.wait_ge(sem("g_z"), 1)
            nc.scalar.activation(gt, gz, ACT.Tanh, scale=1.0 / GATE_CAP).then_inc(sem("g_tanh"), 1)
            act.wait_ge(sem("g_tanh"), 1)
            ch.link(nc.scalar.activation(gex.rearrange("p (c g) -> p c g", c=TT), tv[:, :, MH:2 * MH], ACT.Exp,
                                         scale=-GATE_CAP))
            nc.scalar.activation(gsp, gex, ACT.Ln, bias=one_col).then_inc(sem("g_sp"), 1)
            head_part(1, 1)
            for h in range(2, MH):
                head_part(h, 0)
                head_part(h, 1)
            act.wait_ge(sem("g_E"), 1)
            nc.scalar.activation(g_exp, g_exp, ACT.Exp).then_inc(sem("g_e"), 1)
            act.wait_ge(sem("spilled"), 16)
            with act.Fori(0, 2) as n:
                for c in range(TT):
                    if c < TT - 1:
                        act.wait_ge(sem("v1_mm"), n * (TT - 1) + (c + 1))
                    else:
                        act.wait_ge(w_used, n * 4 + (T_L1_V + 4))
                    nc.scalar.copy(vaug[:, c, bass.ds(n * 2, 2), 0:MV],
                                   ps[:, c, :].rearrange("p (h e) -> p h e", h=2)).then_inc(sem("l1_read"), 1)

            def stab(c):
                act.wait_ge(sem("m_bc"), c + 1)
                if c >= 2:
                    act.wait_ge(sem("msw"), c - 1)
                for h in range(MH):
                    nc.scalar.activation(mw[:, c % 2, h * P:(h + 1) * P], ps[:, 0, h * P:(h + 1) * P], ACT.Exp,
                                         bias=ga[:, 4 * c + h:4 * c + h + 1], scale=-1.0).then_inc(sem("mw"), 1)

            def squares(c, h):
                act.wait_ge(sem("m_num_read"), 4 * c + h + 1)
                if c + h >= 1:
                    act.wait_ge(sem("m_sq"), 4 * c + h)
                nc.scalar.activation(junk[:], mnum[:, h, 0:MV], ACT.Square,
                                     accum_out=mss[:, h:h + 1]).then_inc(sem("m_sq"), 1)

            act.wait_ge(sem("g_e"), 1)
            stab(0)
            for c in range(TT):
                if c + 1 < TT:
                    stab(c + 1)
                for h in range(MH):
                    n = 4 * c + h
                    act.wait_ge(sem("m_inter"), n + 1)
                    if n >= 1:
                        act.wait_ge(sem("m_num_read"), n)
                    nc.scalar.mul(mtmp[:, 0:MV + 1], ps[:, 5, 0:MV + 1],
                                  g_exp[:, n:n + 1]).then_inc(sem("m_inter_read"), 1)
                    if h >= 1:
                        squares(c, h - 1)
                squares(c, MH - 1)
                act.wait_ge(sem("m_v"), c + 1)
                nc.scalar.activation(msd, mt2, ACT.Sqrt, bias=eps, scale=1.0 / MV).then_inc(sem("m_sd"), 1)
            hb = half_base(T_L1_O)
            for m in range(KT):
                for s in range(2):
                    n = 2 * m + s
                    if s == 0:
                        act.wait_ge(half_done, hb + m + 1)
                    else:
                        act.wait_ge(w_used, T_L1_O + m + 1)
                    if n >= 2:
                        act.wait_ge(sem("y_gated"), n - 1)
                    nc.scalar.activation(sigo[:, s, :], ps[:, 2 * (m % 2) + s, :],
                                         ACT.Sigmoid).then_inc(sem("sigo"), 1)
            act.wait_ge(w_used, T_L1_OUT)
            for m in range(KT):
                act.wait_ge(sem("y_gated"), 2 * m + 2)
                nc.scalar.copy(ahi[:, m, :].rearrange("p (c t) -> p c t", c=TT),
                               vaug[:, :, m // 2, (m % 2) * P:(m % 2 + 1) * P]).then_inc(sem("L1hi"), 1)
            act.wait_ge(sem("L1mix"), KT)
            for k in range(KT):
                act.dma_start(hT[:, k, :], spill[:, k * S:(k + 1) * S]).then_inc(x_in[k], 16)
            act_squares(act, "F1n", lambda k: hT[:, k, :], sq, lambda k: act.wait_ge(sem("L1res"), 2 * k + 6))
            act_std(act, "F1n", 6)
            act_round(act, "F1n")
            act_mlp(act, ch, "F1", T_FFN1)
            act_squares(act, "nf", lambda k: hT[:, k, :], sq,
                        lambda k: act.wait_ge(sem("F1added"), last_added + 2 * k + 2))
            act_std(act, "nf", 0)

        @block.vector
        def _(dve):
            ch = Chain(dve, sem("dve_chain"))
            for name in ("ylru", "xc_ready", "y_read", "o_read"):
                dve.sem_inc(sem(name), 1)
            nc.vector.memset(eps, EPS).then_inc(sem("eps_set"), 1)
            dve.sem_inc(sem("L0res"), 4)
            dve.wait_ge(sem("const_in"), 32)
            lam = pars[:, _cols["lru"]:_cols["lru"] + 8 * LRU_T].rearrange("p (j n) -> p j n", n=8)[:, :, 7]
            nc.vector.scalar_tensor_tensor(out=l0, in0=lam, scalar=-1.0, in1=lam, op0=ALU.mult,
                                           op1=ALU.min).then_inc(sem("lam_abs"), 1)
            rows = slice(64, 128)
            dve.wait_ge(sem("pos_in"), 16)
            posf, ang = lat[rows, 2, :], lat[rows, 1, :]

            def rc(n):
                return cons[rows, C_ROPE + n:C_ROPE + n + 1]

            ch.link(nc.vector.tensor_copy(posf, posi[rows, :]))
            ch.link(nc.vector.tensor_scalar(ang, posf, rc(0), None, ALU.mult))
            ch.link(nc.vector.tensor_scalar(posf, ang, 1.0 / TWO_PI, rc(1), ALU.mult, ALU.add))
            ch.link(nc.vector.tensor_scalar(posf, posf, MAGIC, MAGIC, ALU.add, ALU.subtract))
            for k in range(1, KT - 1):
                dve_accumulate(dve, "n0", k)
                if k <= 3:
                    ch.link(nc.vector.scalar_tensor_tensor(out=ang, in0=posf, scalar=-(RED1, RED2, RED3)[k - 1],
                                                           in1=ang, op0=ALU.mult, op1=ALU.add))
                elif k == 4:
                    ch.link(nc.vector.tensor_scalar(ang, ang, rc(2), SIN_MAX, ALU.add, ALU.min))
                elif k == 5:
                    nc.vector.tensor_scalar(ang, ang, -SIN_MAX, None, ALU.max).then_inc(sem("angles"), 1)
            dve_norm(dve, ch, "n0", "e_g", 6)
            dve.wait_ge(sem("lam_exp"), 1)
            ch.link(nc.vector.tensor_scalar(l2, l1, 2.0, None, ALU.add))
            ch.link(nc.vector.reciprocal(l2, l2))
            ch.link(nc.vector.tensor_tensor(l1, l1, l2, ALU.mult))
            ch.link(nc.vector.tensor_tensor(l2, l1, l1, ALU.mult))
            ch.link(nc.vector.tensor_scalar(l3, l2, 1.0 / 17, 1.0 / 15, ALU.mult, ALU.add))
            for n in (13, 11, 9, 7, 5, 3, 1):
                ch.link(nc.vector.tensor_tensor(l3, l3, l2, ALU.mult))
                ch.link(nc.vector.tensor_scalar(l3, l3, 1.0 / n, None, ALU.add))
            ch.link(nc.vector.tensor_tensor(l3, l3, l1, ALU.mult))
            ch.link(nc.vector.tensor_scalar(l0, lam, -1.0, 0.0, ALU.mult, ALU.max))
            ch.link(nc.vector.tensor_scalar(l3, l3, 8.0, None, ALU.mult))
            ch.link(nc.vector.scalar_tensor_tensor(out=lcoef, in0=l0, scalar=4.0, in1=l3, op0=ALU.mult,
                                                   op1=ALU.add))
            nc.vector.tensor_scalar(lexp, lcoef, -2.0, None, ALU.mult).then_inc(sem("lcoef"), 1)
            ch.link(nc.vector.memset(xrp[:, 0:3], 0.0))
            with dve.Fori(0, LRU_T // 2) as i:
                ch.enter(i, 2 * 7)
                for jj in range(2):
                    j = i * 2 + jj

                    def w(n):
                        return pars[:, bass.ds(j * 8 + (_cols["lru"] + n), 1)]

                    dve.wait_ge(sem("xr_read"), j * 2 + 2 + 1)
                    dve.wait_ge(sem("lru_pre"), j * 4 + 1)
                    ch.link(nc.vector.tensor_scalar(xc[:, :], xrp[:, 0:S], w(0), w(4), ALU.mult, ALU.add))
                    for n in (1, 2):
                        ch.link(nc.vector.scalar_tensor_tensor(out=xc[:, :], in0=xrp[:, n:n + S], scalar=w(n),
                                                               in1=xc[:, :], op0=ALU.mult, op1=ALU.add))
                    nc.vector.scalar_tensor_tensor(out=xc[:, :], in0=xrp[:, 3:3 + S], scalar=w(3), in1=xc[:, :],
                                                   op0=ALU.mult, op1=ALU.add).then_inc(sem("xc_ready"), 1)
                    dve.wait_ge(sem("lru_i"), j + 1 + 1)
                    dve.wait_ge(sem("xc_ready"), j + 1 + 1)
                    ch.link(nc.vector.tensor_tensor(li[:, :], li[:, :], xc[:, :], ALU.mult))
                    dve.wait_ge(sem("lru_sq"), j + 1)
                    ch.link(nc.vector.scalar_tensor_tensor(out=ls[:, :], in0=lc[:, :], scalar=1.0, in1=ls[:, :],
                                                           op0=ALU.add, op1=ALU.mult))
                    ch.link(nc.vector.tensor_tensor(ls[:, :], ls[:, :], li[:, :], ALU.mult))
                    y = ylru[:, bass.ds(j, 1), :].rearrange("p a b -> p (a b)")
                    ch.link(nc.vector.tensor_tensor_scan(y, lc[:, :], ls[:, :], 0.0, ALU.mult, ALU.add))
                    dve.wait_ge(sem("gelu"), j + 1 + 1)
                    nc.vector.tensor_tensor(y, y, lg[:, :], ALU.mult).then_inc(sem("ylru"), 1)
            ch.leave(LRU_T // 2)

            dve.wait_ge(sem("lat_in"), 1)
            dve_factor(dve, ch, "nk", diagb)
            nc.vector.scalar_tensor_tensor(out=lat[:, 2, :], in0=lat[:, 2, :], scalar=pcol("kv_g", 0),
                                           in1=spread_banks(0), op0=ALU.mult, op1=ALU.mult
                                           ).then_inc(sem("kv_normed"), 1)
            dve.wait_ge(w_used, T_L0_OUT)
            dve.wait_ge(sem("tab_ready"), 1)
            a32, b32 = slice(NOPE, QK), slice(QK, P)
            kr = spread_banks(6)
            nc.vector.tensor_tensor(rt1[a32, :], kr[a32, :], tab[a32, :], ALU.mult)
            ch.link(nc.vector.tensor_tensor(rt2[a32, :], kr[b32, :], tab[b32, :], ALU.mult))
            nc.vector.tensor_tensor(kpe[a32, :], rt1[a32, :], rt2[a32, :], ALU.add).then_inc(sem("kpe_ready"), 1)
            dve_factor(dve, ch, "nq", diagb)
            for k in range(2):
                nc.vector.scalar_tensor_tensor(out=lat[:, k, :], in0=lat[:, k, :], scalar=pcol("q_g", k),
                                               in1=spread_banks(4), op0=ALU.mult, op1=ALU.mult
                                               ).then_inc(sem("q_normed"), 1)
            for j in range(LRU_T):
                dve.wait_ge(sem("lru_hi"), j + 1)
                nc.vector.tensor_tensor(alo[:, j, :], ylru[:, j, :], ahi[:, j, :].bitcast(F32),
                                        ALU.subtract).then_inc(sem("lru_split"), 1)
            dve.wait_ge(sem("kpe_ready"), 1)
            dve.wait_ge(sem("lru_split"), LRU_T)
            for par in range(2):
                nc.vector.tensor_copy(kh[a32, par, :], kpe[a32, :]).then_inc(sem("kpe_in"), 1)

            def rotate(h, par, part, per_chain):
                tok = slice(part * HALF, (part + 1) * HALF)
                dve.wait_ge(sem("q_nope"), h * 2 + (part + 1))
                nc.vector.scalar_tensor_tensor(out=rt1[a32, 0:HALF], in0=ps[a32, 0, :], scalar=QK_SCALE,
                                               in1=tab[a32, tok], op0=ALU.mult, op1=ALU.mult)
                ch.link(nc.vector.scalar_tensor_tensor(out=rt2[a32, 0:HALF], in0=ps[b32, 0, :], scalar=QK_SCALE,
                                                       in1=tab[b32, tok], op0=ALU.mult, op1=ALU.mult))
                nc.vector.tensor_tensor(qh[a32, par, tok], rt1[a32, 0:HALF], rt2[a32, 0:HALF], ALU.add
                                        ).then_inc(sem("proj_read"), 1)

            def maxima(k, step):
                n = (order[k] + 1) * P
                b = 1 + 2 * (k % 2)
                sc = ps[:, b:b + 2, :].rearrange("p a b -> p (a b)")
                dve.wait_ge(sem("scores"), step + 1)
                if not isinstance(step, int) or step >= 1:
                    dve.wait_ge(sem("probs"), (step - 1) + 1)
                ch.link(nc.vector.tensor_tensor(sc[:, n - P:n], sc[:, n - P:n], maskq, ALU.add))
                nc.vector.tensor_reduce(nmax[:, k % 2:k % 2 + 1], sc[:, 0:n], AX_X, ALU.max,
                                        negate=True).then_inc(sem("nmax"), 1)

            def outputs(p, par, k, step):
                dve.wait_ge(sem("probs"), step + 1 + 1)
                ch.link(nc.vector.reciprocal(rinv[:, k % 2:k % 2 + 1], rsum[:, k % 4:k % 4 + 1]))
                dve.wait_ge(sem("o"), step + 3)
                if par == 0:
                    dve.wait_ge(sem("yt"), p * 3 + 1)
                nc.vector.tensor_scalar(opair[:, order[k], par * VH:(par + 1) * VH],
                                        ps[:, 7, 0:VH],
                                        rinv[:, k % 2:k % 2 + 1], None, ALU.mult).then_inc(sem("o_read"), 1)

            def y_lo(p, n):
                _, first, blocks = turns[n]
                tok = slice(first * P, (first + blocks) * P)
                dve.wait_ge(sem("y_hi"), p * 3 + (n + 1))
                hi = ahi[:, bass.ds(p + LRU_T, 1), tok].rearrange("p a b -> p (a b)")
                lo = alo[:, bass.ds(p + LRU_T, 1), tok].rearrange("p a b -> p (a b)")
                nc.vector.tensor_tensor(lo, ps[:, 0, 0:blocks * P], hi.bitcast(F32), ALU.subtract
                                        ).then_inc(sem("y_read"), 1)

            def head_pair(p, last=False):
                for i in range(16):
                    par, k = i // 8, i % 8
                    if not (last and i >= 14):
                        maxima((i + 2) % 8, p * 16 + (i + 2))
                    if k < 2 and not (last and par == 1):
                        rotate(p * 2 + par + 1, 1 - par, k, None)
                    outputs(p, par, k, p * 16 + i)
                    for n, (slot, _, _) in enumerate(turns):
                        if par == 1 and k == min(slot + 1, 7):
                            y_lo(p, n)

            for part in range(2):
                rotate(0, 0, part, None)
            for i in range(2):
                maxima(i, i)
            with dve.Fori(0, HEADS // 2 - 1) as p:
                ch.enter(p, 36)
                head_pair(p)
            ch.leave(HEADS // 2 - 1)
            head_pair(HEADS // 2 - 1, last=True)
            dve_out(dve, "L0", T_L0_OUT, 32, "F0n")
            dve_norm(dve, ch, "F0n", "f_g0", 6)
            dve_mlp(dve, ch, "F0", T_FFN0, 0, "n1")

            dve.sem_inc(sem("sigo"), 4)
            dve.sem_inc(sem("L1res"), 4)
            dve_norm(dve, ch, "n1", "o_g", 4)
            dve.wait_ge(sem("wg_hi"), 1)
            nc.vector.tensor_tensor(wglo[:], wgs[:], wghi[:].bitcast(F32), ALU.subtract).then_inc(sem("wg_split"), 1)
            dve.wait_ge(sem("g_pre"), 1)
            nc.vector.tensor_tensor(gz, ps[:, 6, 0:8 * TT], pcol("gate_b", 0, 8 * TT), ALU.add
                                    ).then_inc(sem("g_z"), 1)
            dve.wait_ge(sem("g_cum"), 1)
            tv = gt.rearrange("p (c g) -> p c g", c=TT)
            nc.vector.scalar_tensor_tensor(out=ga.rearrange("p (c g) -> p c g", c=TT), in0=tv[:, :, 0:MH],
                                           scalar=GATE_CAP, in1=ps[:, 5, 0:32].rearrange("p (c g) -> p c g", c=TT),
                                           op0=ALU.mult, op1=ALU.add).then_inc(sem("g_a"), 1)
            nc.vector.tensor_copy(gnb, ps[:, 5, 0:32]).then_inc(sem("g_a"), 1)
            dve.wait_ge(sem("g_turned"), 1)
            ch.link(nc.vector.tensor_copy(gaT[0:32, :], ps[0:32, 6, 0:P]))
            nc.vector.tensor_tensor_scan(gAT[0:32, :], gaT[0:32, :], gaT[0:32, :], -BIG, ALU.max, ALU.max
                                         ).then_inc(sem("g_max"), 1)
            nc.vector.tensor_copy(g_last, ps[0:32, 6, 2 * P - 1:2 * P]).then_inc(sem("g_max"), 1)
            dve.wait_ge(sem("g_rows"), 1)
            nc.vector.memset(ginfo[0:1, 256:260], 0.0)
            ch.link(nc.vector.tensor_copy(g_row, ps[0:1, 7, 0:64]))
            for h in range(MH):
                ch.add(nc.vector.tensor_tensor_scan(m_next[:, h::MH], g_row[:, h:32:MH], g_row[:, 32 + h:64:MH], 0.0,
                                                    ALU.max, ALU.subtract))
            ch.wait(ch.n)
            nc.vector.tensor_tensor(ml_row, m_row, g_row[:, 0:32], ALU.max).then_inc(sem("g_m"), 1)
            dve.wait_ge(sem("g_spread"), 1)
            ch.link(nc.vector.tensor_copy(g_mcol, ps[0:32, 7, 64:65]))
            ch.link(nc.vector.tensor_copy(gz, ps[:, 7, 128:192]))
            nc.vector.tensor_scalar(gMT[0:32, :], gAT[0:32, :], g_mcol, None, ALU.max).then_inc(sem("g_MT"), 1)
            dve.wait_ge(sem("g_M"), 1)
            m_tok = ps[:, 7, 256:288]
            nc.vector.tensor_tensor(g_exp[:, 0:32], gz[:, 0:32], m_tok, ALU.subtract)
            nc.vector.tensor_tensor(g_exp[:, 32:64], gnb, m_tok, ALU.subtract)
            nc.vector.tensor_tensor(g_exp[:, 64:96], ga, gz[:, 32:64], ALU.subtract)
            nc.vector.tensor_tensor(g_exp[:, 96:128], gz[:, 0:32], gz[:, 32:64], ALU.subtract
                                    ).then_inc(sem("g_E"), 1)
            dve.wait_ge(sem("spilled"), 16)
            ch.link(nc.vector.memset(vaug[:, :, :, MV:MVA], 1.0))
            nc.vector.memset(cst[:, :, :], 0.0).then_inc(sem("cst0"), 1)

            def stab_rows(c):
                if c == 0:
                    dve.wait_ge(sem("g_MT"), 1)
                else:
                    dve.wait_ge(sem("m_bc"), c)
                for h in range(MH):
                    ins = nc.vector.tensor_scalar(mtx[0:32, h * P:(h + 1) * P], gMT[0:32, :],
                                                  ident[0:32, 4 * c + h:4 * c + h + 1], None, ALU.mult)
                ins.then_inc(sem("mtx"), 1)

            def weights(c):
                dve.wait_ge(sem("mw"), 4 * c + 4)
                dve.wait_ge(sem("m_qk"), c + 1)
                if c >= 2:
                    dve.wait_ge(sem("m_kv"), 4 * c - 4)
                nc.vector.tensor_tensor(msw[:, c % 2, :], ps[:, 1, :], mw[:, c % 2, :], ALU.mult
                                        ).then_inc(sem("msw"), 1)
                dve.wait_ge(sem("m_kt"), c + 1)
                for h in range(MH):
                    n = 4 * c + h
                    nc.vector.tensor_scalar(mkw[:, c % 2, h * P:(h + 1) * P], ps[:, 2, h * P:(h + 1) * P],
                                            g_exp[:, 64 + n:65 + n], None, ALU.mult).then_inc(sem("mkw"), 1)

            def gather(c):
                for b in range(2):
                    dve.wait_ge(sem("m_turned"), 2 * c + b + 1)
                    for i in range(4):
                        h, e = 2 * b + i // 2, i % 2
                        nc.vector.tensor_scalar(vaug[:, c, h, e * P:(e + 1) * P], ps[:, 7, i * P:(i + 1) * P],
                                                pcol("out_g", 2 * h + e), None, ALU.mult).then_inc(sem("m_y"), 1)

            stab_rows(0)
            dve.wait_ge(sem("g_e"), 1)
            weights(0)
            stab_rows(1)
            for c in range(TT):
                if c + 1 < TT:
                    weights(c + 1)
                if c + 2 < TT:
                    stab_rows(c + 2)
                if c >= 1:
                    dve.wait_ge(sem("m_hn"), c)
                for h in range(MH):
                    n = 4 * c + h
                    dve.wait_ge(sem("m_inter_read"), n + 1)
                    dve.wait_ge(sem("m_num"), n + 1)
                    nc.vector.tensor_tensor(mnum[:, h, 0:MV + 1], ps[:, 3 + h % 2, 0:MV + 1], mtmp[:, 0:MV + 1],
                                            ALU.add).then_inc(sem("m_num_read"), 1)
                    dve.wait_ge(sem("m_kv"), n + 1)
                    nc.vector.scalar_tensor_tensor(out=cst[:, h, 0:MV + 1], in0=cst[:, h, 0:MV + 1],
                                                   scalar=g_exp[:, 96 + n:97 + n], in1=ps[:, 6, 0:MV + 1],
                                                   op0=ALU.mult, op1=ALU.add).then_inc(sem("m_state"), 1)
                if c >= 1:
                    gather(c - 1)
                dve.wait_ge(sem("m_num_read"), 4 * c + 4)
                ch.link(nc.vector.scalar_tensor_tensor(out=mden, in0=mnum[:, :, MV], scalar=-1.0,
                                                       in1=mnum[:, :, MV], op0=ALU.mult, op1=ALU.max))
                ch.link(nc.vector.tensor_tensor(mden, mden, g_exp[:, 32 + 4 * c:36 + 4 * c], ALU.max))
                ch.link(nc.vector.reciprocal(mrd, mden))
                ch.link(nc.vector.tensor_tensor(mt2, mrd, mrd, ALU.mult))
                dve.wait_ge(sem("m_sq"), 4 * c + 4)
                nc.vector.tensor_tensor(mt2, mt2, mss, ALU.mult).then_inc(sem("m_v"), 1)
                dve.wait_ge(sem("m_sd"), c + 1)
                ch.link(nc.vector.reciprocal(mrs, msd))
                ch.link(nc.vector.tensor_tensor(msc, mrs, mrd, ALU.mult))
                if c >= 1:
                    dve.wait_ge(sem("m_turned"), 2 * c)
                for h in range(MH):
                    ins = nc.vector.tensor_scalar(mhn[:, h, :], mnum[:, h, 0:MV], msc[:, h:h + 1], None, ALU.mult)
                ins.then_inc(sem("m_hn"), 1)
            gather(TT - 1)
            for m in range(KT):
                for s in range(2):
                    n = 2 * m + s
                    dve.wait_ge(sem("sigo"), n + 5)
                    y = vaug[:, 4 * s:4 * s + 4, m // 2, (m % 2) * P:(m % 2 + 1) * P]
                    nc.vector.tensor_tensor(y, y, sigo[:, s, :].rearrange("p (c t) -> p c t", c=4), ALU.mult
                                            ).then_inc(sem("y_gated"), 1)
            for m in range(KT):
                dve.wait_ge(sem("L1hi"), m + 1)
                nc.vector.tensor_tensor(alo[:, m, :].rearrange("p (c t) -> p c t", c=TT),
                                        vaug[:, :, m // 2, (m % 2) * P:(m % 2 + 1) * P],
                                        ahi[:, m, :].bitcast(F32).rearrange("p (c t) -> p c t", c=TT),
                                        ALU.subtract).then_inc(sem("L1mix"), 1)
            dve_out(dve, "L1", T_L1_OUT, 48, "F1n")
            dve_norm(dve, ch, "F1n", "f_g1", 6)
            dve_mlp(dve, ch, "F1", T_FFN1, 1, "nf")
            dve_factor(dve, ch, "nf", diag)
            for k in range(KT):
                nc.vector.scalar_tensor_tensor(out=hT[:, k, :], in0=hT[:, k, :], scalar=pcol("fin_g", k),
                                               in1=spread_banks(0), op0=ALU.mult, op1=ALU.mult
                                               ).then_inc(sem("fin_ready"), 1)


def _m_tile(w, cols):
    k = w.shape[0] // P
    return w[:, cols].reshape(k, P, P).transpose(1, 0, 2).reshape(P, k * P)


def _mlp_tiles(up, down):
    def ups(f):
        return [_m_tile(up, slice(f * P, (f + 1) * P)), _m_tile(up, slice(D_FF + f * P, D_FF + (f + 1) * P))]

    tiles = ups(0)
    for g in range(FG):
        tiles += ups(2 * g + 1)
        if g < FG - 1:
            tiles += ups(2 * g + 2)
        tiles += [down[(2 * g + j) * P:(2 * g + j + 1) * P, :] for j in range(2)]
    return tiles


def kernel(**inputs):
    import concourse.bacc as bacc
    from concourse.bass_utils import run_bass_kernel_spmd

    a = {k: np.asarray(v) for k, v in inputs.items()}
    w0, w1 = a["e_w_in"][0], a["o_w_in"][0]
    tiles = []
    for j in range(LRU_T):
        tiles += [_m_tile(w0, slice(j * P, (j + 1) * P)), _m_tile(w0, slice(LRU_W + j * P, LRU_W + (j + 1) * P))]
    q0 = 2 * LRU_W
    kv0 = q0 + Q_LORA
    r0 = kv0 + KV_LORA
    half = ROPE // 2
    tiles += [_m_tile(w0, slice(kv0, kv0 + P)), _m_tile(w0, slice(q0, q0 + P)), _m_tile(w0, slice(q0 + P, q0 + 2 * P))]
    rot = np.concatenate([np.zeros((D, NOPE), np.float32), w0[:, r0:r0 + ROPE], w0[:, r0 + half:r0 + ROPE],
                          w0[:, r0:r0 + half]], axis=1)
    tiles.append(_m_tile(rot, slice(0, P)))
    tiles += [_m_tile(a["e_w_out"][0], slice(m * P, (m + 1) * P)) for m in range(KT)]
    tiles += _mlp_tiles(a["f_w_up"][0], a["f_w_down"][0])
    c1 = MH * MQK
    for h in range(MH):
        tiles += [_m_tile(w1, slice(h * P, (h + 1) * P)), _m_tile(w1, slice(c1 + h * P, c1 + (h + 1) * P))]
    for n in range(2):
        for j in range(4):
            v = w1[2 * j * P:(2 * j + 2) * P, 2 * c1 + n * HALF:2 * c1 + (n + 1) * HALF]
            tiles.append(v.reshape(2, P, HALF).transpose(1, 0, 2).reshape(P, 2 * HALF))
    o0 = 2 * c1 + MH * MV
    tiles += [_m_tile(w1, slice(o0 + m * P, o0 + (m + 1) * P)) for m in range(KT)]
    tiles += [_m_tile(a["o_w_out"][0], slice(m * P, (m + 1) * P)) for m in range(KT)]
    tiles += _mlp_tiles(a["f_w_up"][1], a["f_w_down"][1])
    assert len(tiles) == TILES, (len(tiles), TILES)
    wt = np.ascontiguousarray(np.concatenate(tiles, axis=0))

    wg = np.zeros((P, KT, P), np.float32)
    wg[:, :, 0:8] = w1[:, o0 + MH * MV:].reshape(KT, P, 8).transpose(1, 0, 2)
    wg = wg.reshape(P, KT * P)
    qb = a["e_w_qb"][0].reshape(Q_LORA, HEADS, QK)
    qb = np.concatenate([qb, qb[:, :, NOPE + half:], qb[:, :, NOPE:NOPE + half]], axis=2)
    wqb = np.ascontiguousarray(qb.reshape(2, P, HEADS * P).transpose(1, 0, 2))
    wkvb = np.ascontiguousarray(a["e_w_kvb"][0])
    wlru = np.zeros((P, LRU_T, 2, P), np.float32)
    for g, name in enumerate(("e_lru_w_a", "e_lru_w_x")):
        for j in range(LRU_T):
            for b in range(2):
                wlru[64 * b:64 * (b + 1), j, g, 64 * b:64 * (b + 1)] = a[name][0, 2 * j + b]
    wlru = wlru.reshape(P, LRU_T, 2 * P)

    def columns(v):
        return v.reshape(-1, P).T

    par = np.zeros((P, NPAR), np.float32)

    def put(name, v):
        par[:, _cols[name]:_cols[name] + v.shape[1]] = v

    put("e_g", columns(a["e_norm_g"][0]))
    put("o_g", columns(a["o_norm_g"][0]))
    put("f_g0", columns(a["f_norm_g"][0]))
    put("f_g1", columns(a["f_norm_g"][1]))
    put("fin_g", columns(a["final_norm_g"]))
    put("q_g", columns(a["e_q_norm_g"][0]))
    put("kv_g", columns(a["e_kv_norm_g"][0]))
    put("out_g", columns(a["o_out_norm_g"][0]))
    lru = [a["e_lru_conv_w"][0, n] for n in range(4)] + [a["e_lru_conv_b"][0], a["e_lru_b_a"][0].reshape(-1),
                                                        a["e_lru_b_x"][0].reshape(-1), a["e_lru_lambda"][0]]
    put("lru", np.stack([columns(v) for v in lru], axis=2).reshape(P, -1))
    put("gate_b", np.broadcast_to(np.tile(np.concatenate([a["o_b_igate"][0], a["o_b_fgate"][0]]), TT), (P, 8 * TT)))
    for l in range(2):
        rows = [a["f_conv_w"][l, n] for n in range(3)] + [a["f_conv_b"][l]]
        parts = [columns(r[g * D_FF:(g + 1) * D_FF]) for g in range(2) for r in rows]
        put(f"conv{l}", np.stack(parts, axis=2).reshape(P, -1))

    con = np.zeros((P, NCON), np.float32)
    i = np.arange(P)
    con[:, C_ID:C_ID + P] = np.eye(P)
    con[:, C_ONE:C_ONE + P] = 1.0
    con[:, C_TRI:C_TRI + P] = i[:, None] <= i[None, :]
    con[:, C_MASKQ:C_MASKQ + P] = -BIG * (i[:, None] < i[None, :])
    con[:, C_MASKS:C_MASKS + P] = BIG * (i[:, None] > i[None, :])
    freq = (10000.0 ** (-np.arange(half) / half)).astype(np.float32)
    con[NOPE:, C_ROPE] = np.tile(freq, 4)
    con[NOPE:QK, C_ROPE + 1] = 0.25
    con[NOPE:QK, C_ROPE + 2] = np.pi / 2
    con[NOPE:, C_ROPE + 3] = 1.0
    con[QK:QK + half, C_ROPE + 3] = -1.0

    xt = np.ascontiguousarray(a["x"][0].T)
    pos = np.ascontiguousarray(np.broadcast_to(a["positions"][0][None, :].astype(np.int32), (P, S)))

    nc = bacc.Bacc("TRN2", target_bir_lowering=False, num_devices=1)
    arrays = {"wt": wt, "xt": xt, "pos": pos, "par": par, "con": con, "wqb": wqb, "wkvb": wkvb, "wlru": wlru,
              "wg": wg}
    aps = {n: nc.dram_tensor("in_" + n, v.shape, mybir.dt.from_np(v.dtype), kind="ExternalInput").ap()
           for n, v in arrays.items()}
    spill = nc.dram_tensor("spill", (P, KT * S), F32, kind="Internal").ap()
    out = nc.dram_tensor("out_0", (D, S), F32, kind="ExternalOutput").ap()
    build(nc, spill=spill, out=out, **aps)
    r = run_bass_kernel_spmd(nc, [{"in_" + n: v for n, v in arrays.items()}], core_ids=[0])
    return np.ascontiguousarray(r.results[0]["out_0"].T)[None]
```

```python
from contextlib import ExitStack

import numpy as np

import concourse.bass as bass
from concourse import mybir

ALU = mybir.AluOpType
ACT = mybir.ActivationFunctionType
F32 = mybir.dt.float32
F32R = mybir.dt.float32r
I32 = mybir.dt.int32
AX_X = mybir.AxisListType.X

P = 128
D = 1024
S = 1024
HALF = 512
KT = D // P
TT = S // P
EPS = 1e-6

LRU_W = 512
LRU_T = LRU_W // P
Q_LORA = 256
KV_LORA = 128
HEADS = 8
NOPE, ROPE, VH = 64, 32, 64
QK = NOPE + ROPE
QK_SCALE = float(QK) ** -0.5

MH, MQK, MV = 4, 128, 256
MVA = MV + 2
GATE_CAP = 15.0

D_FF = 2816
FT = D_FF // P
FG = FT // 2

RING = 4
STAGE = 2

T_L0_OUT = 2 * LRU_T + 4
T_FFN0 = T_L0_OUT + KT
T_L1 = T_FFN0 + 3 * FT
T_L1_V = T_L1 + 2 * MH
T_L1_O = T_L1_V + 8
T_L1_OUT = T_L1_O + KT
T_FFN1 = T_L1_OUT + KT
TILES = T_FFN1 + 3 * FT

_cols = {}
_n = 0
for _name, _w in [("e_g", KT), ("o_g", KT), ("f_g0", KT), ("f_g1", KT), ("fin_g", KT), ("q_g", Q_LORA // P),
                  ("kv_g", 1), ("lru", LRU_T * 8), ("out_g", KT), ("gate_b", TT * 8),
                  ("conv0", FT * 8), ("conv1", FT * 8)]:
    _cols[_name] = _n
    _n += _w
NPAR = _n

C_ID, C_ONE, C_TRI, C_MASKQ, C_MASKS, C_ROPE = 0, P, 2 * P, 3 * P, 4 * P, 5 * P
NCON = 5 * P + 8
TWO_PI = 2.0 * np.pi
RED1 = 6.28125
RED2 = float(np.float32(np.floor((TWO_PI - RED1) * 2 ** 18) / 2 ** 18))
RED3 = float(TWO_PI - RED1 - RED2)
MAGIC = 12582912.0
SIN_MAX = 3.1415925
BIG = 1e30


class Chain:

    def __init__(self, eng, sem):
        self.eng, self.sem, self.n, self.shift = eng, sem, 0, 0

    def link(self, ins):
        ins.then_inc(self.sem, 1)
        self.n += 1
        self.eng.wait_ge(self.sem, self.shift + self.n)

    def add(self, ins):
        ins.then_inc(self.sem, 1)
        self.n += 1
        return self.n

    def wait(self, n):
        self.eng.wait_ge(self.sem, self.shift + n)

    def enter(self, i, per):
        self.shift, self.start, self.per = i * per, self.n, per

    def leave(self, count):
        assert self.n - self.start == self.per, (self.n - self.start, self.per)
        self.n += self.per * (count - 1)
        self.shift = 0


def build(nc, wt, xt, pos, par, con, wqb, wkvb, wlru, wg, spill, out):
    with ExitStack() as ctx:
        def psum(name, shape):
            return ctx.enter_context(nc.psum_tensor(name, shape, F32))

        sems = {}

        def sem(name):
            if name not in sems:
                sems[name] = ctx.enter_context(nc.semaphore(name))
            return sems[name]

        base = -(-nc.sbuf_base // 32) * 32
        room = (nc.sbuf_usable_end - base) // 32 * 32 - 32
        ctx.enter_context(nc.sbuf_tensor("arena", [P, room // 4], F32))
        KB = 1024

        def at(name, off, shape, dt=F32):
            size = int(np.prod(shape[1:])) * 4
            assert off + size <= room, (name, off, size, room)
            return nc.alloc_sbuf_tensor_at(name, shape, dt, offset=base + off)

        stage = at("stage", 0, [P, STAGE, 1024])
        whi = at("whi", 8 * KB, [P, RING, 1024], F32R)
        wlo = at("wlo", 24 * KB, [P, RING, 1024], F32R)
        ahi = at("ahi", 40 * KB, [P, KT, S], F32R)
        alo = at("alo", 72 * KB, [P, KT, S], F32R)
        c0 = 104 * KB
        cons = at("cons", c0, [P, NCON])
        c0 += NCON * 4
        pars = at("pars", c0, [P, NPAR])
        c0 += -(-NPAR * 4 // 32) * 32
        small = at("small", c0, [P, 96])
        c0 += 96 * 4
        nw = -(-c0 // 32) * 32
        sh = nw + 20 * KB
        sq = at("sq", nw, [P, 2, S])
        xnf = at("xnf", nw + 8 * KB, [P, 2, S])
        acc = at("acc", nw + 16 * KB, [P, S])
        diag = at("diag", nw + 16 * KB, [P, S])
        sqb = at("sqb", sh, [P, 2, S])
        diagb = at("diagb", sh + 8 * KB, [P, S])
        hT = at("hT", sh, [P, KT, S])
        lr = at("lr", nw, [P, S])
        li = at("li", nw + 4 * KB, [P, S])
        lg = at("lg", nw + 8 * KB, [P, S])
        ls = at("ls", nw + 12 * KB, [P, S])
        lc = at("lc", nw + 16 * KB, [P, S])
        ylru = at("ylru", sh + 16 * KB, [P, LRU_T, S])
        xrp = at("xrp", sh + 32 * KB, [P, S + 3])
        xc = at("xc", sh + 36 * KB + 32, [P, S])
        pbuf = at("pbuf", nw, [P, 2, S])
        ptb = at("ptb", nw + 8 * KB, [P, 2, S])
        opair = at("opair", nw + 16 * KB, [P, TT, P])
        vtok = at("vtok", sh, [P, TT, HEADS * VH])
        qh = at("qh", sh + 16 * KB, [P, 2, S])
        kh = at("kh", sh + 24 * KB, [P, 2, S])
        rt1 = at("rt1", sh + 32 * KB, [P, S])
        rt2 = at("rt2", sh + 36 * KB + 32, [P, S])
        x0 = sh + 41 * KB
        lat = at("lat", x0, [P, 3, S])
        posi = at("posi", x0, [P, S], I32)
        kpe = at("kpe", x0 + 12 * KB, [P, S])
        tab = at("tab", x0 + 16 * KB, [P, S])
        wqb_s = at("wqb_s", x0 + 20 * KB, [P, 2, 1024])
        wlru_s = at("wlru_s", x0 + 20 * KB, [P, LRU_T, 2 * P])
        wlfix = at("wlfix", x0 + 24 * KB, [P, 2, 2 * P])
        wkvb_s = at("wkvb_s", x0 + 28 * KB, [P, 1024])
        wh = at("wh", x0 + 32 * KB, [P, 2, 3 * P])
        hid_hi = at("hid_hi", sh + 32 * KB, [P, 2, S], F32R)
        hid_lo = at("hid_lo", sh + 40 * KB, [P, 2, S], F32R)
        upg = at("upg", sh + 48 * KB, [P, S + 2])
        upv = at("upv", sh + 52 * KB + 32, [P, S + 2])
        cvg = at("cvg", sh + 56 * KB + 64, [P, S])
        cvv = at("cvv", sh + 60 * KB + 64, [P, S])
        vaug = at("vaug", sh, [P, TT, MH, MVA])
        q1 = sh + 33 * KB
        qT = at("qT", q1, [P, MH, S])
        kT = at("kT", q1 + 16 * KB, [P, MH, S])
        sigo = at("sigo", q1, [P, 2, HALF])
        m1 = q1 + 32 * KB
        cst = at("cst", m1, [P, MH, MVA])
        mw = at("mw", m1 + 4 * KB + 256, [P, 2, MH * P])
        ginfo = at("ginfo", m1 + 8 * KB + 256, [P, 640])
        gaT = at("gaT", m1 + 10 * KB + 768, [P, P])
        gAT = at("gAT", m1 + 11 * KB + 256, [P, P])
        gMT = at("gMT", m1 + 11 * KB + 768, [P, P])
        wgs = at("wgs", q1 + 20 * KB, [P, KT * P])
        wghi = at("wghi", q1 + 24 * KB, [P, KT * P], F32R)
        wglo = at("wglo", q1 + 28 * KB, [P, KT * P], F32R)
        grow = xnf[0:8, 1, :]
        junk = at("junk", m1 + 12 * KB + 768, [P, MV])
        gz, gt, gsp, ga, gnb = (ginfo[:, a:b] for a, b in ((0, 64), (64, 128), (128, 160), (160, 192), (192, 224)))
        gex = ginfo[:, 224:256]
        m_row, m_next, ml_row = ginfo[0:1, 256:288], ginfo[0:1, 260:292], ginfo[0:1, 292:324]
        g_exp = ginfo[:, 384:512]
        g_row = ginfo[0:1, 512:576]
        g_last = ginfo[0:32, 576:577]
        g_mcol = ginfo[0:32, 577:578]
        msw = at("msw", nw, [P, 2, MH * P])
        mkw = at("mkw", nw + 4 * KB, [P, 2, MH * P])
        mnum = at("mnum", nw + 8 * KB, [P, MH, MVA])
        mtx = at("mtx", nw + 12 * KB + 256, [P, MH * P])
        mtmp = at("mtmp", nw + 14 * KB + 256, [P, MVA])
        mhn = at("mhn", nw + 15 * KB + 512, [P, MH, MV])
        assert nw + 15 * KB + 512 + MH * MV * 4 <= sh

        ident = cons[:, C_ID:C_ID + P]
        ones = cons[:, C_ONE:C_ONE + P]
        tri = cons[:, C_TRI:C_TRI + P]
        maskq = cons[:, C_MASKQ:C_MASKQ + P]
        masks = cons[:, C_MASKS:C_MASKS + P]
        std, rstd = small[:, 0:8], small[:, 8:16]
        eps = small[:, 16:17]
        lcoef, lexp = small[:, 20:24], small[:, 80:84]
        l0, l1, l2, l3 = small[:, 24:28], small[:, 28:32], small[:, 32:36], small[:, 36:40]
        nmax, rsum, rinv = small[:, 40:42], small[:, 84:88], small[:, 44:46]
        mss, mden, mrd, mt2, msd, mrs, msc = (small[:, 48 + 4 * n:52 + 4 * n] for n in range(7))
        one_col = ones[:, 0:1]
        order = [6, 7, 0, 1, 4, 5, 2, 3]
        turns = [(4, 6, 2), (5, 0, 2), (7, 2, 4)]
        groups_before = [sum(1 if q < 4 else 2 for q in order[:k]) for k in range(TT)]
        group_parity = [g % 2 for g in groups_before]

        first_banks = (0, 5, 6, 7)

        def groups_of(qt):
            return [(a, min(4, qt + 1 - a)) for a in range(0, qt + 1, 4)]

        def pcol(name, i, n=1):
            return pars[:, _cols[name] + i:_cols[name] + i + n]

        ps = psum("ps", [P, 8, HALF])

        halves = [slice(s * HALF, (s + 1) * HALF) for s in range(2)]

        w_landed = [sem(f"w_landed{n}") for n in range(STAGE)]
        w_hi, w_ready, w_used = sem("w_hi"), sem("w_ready"), sem("w_used")
        x_in = [sem(f"x_in{k}") for k in range(KT)]
        x_second = [sem(f"x_second{k}") for k in range(KT)]
        half_done = sem("half_done")

        block = ctx.enter_context(nc.Block())

        @block.sync
        def _(sp):
            sp.dma_start(cons[:], con).then_inc(sem("const_in"), 16)
            sp.dma_start(pars[:], par).then_inc(sem("const_in"), 16)

            def load(t, n, round_):
                if n is not None:
                    sp.wait_ge(w_ready, n)
                sp.dma_start(stage[:, round_, :], wt[bass.ds(t * P, P), :]).then_inc(w_landed[round_], 16)

            for s in range(2):
                for k in range(KT):
                    sp.dma_start(hT[:, k, halves[s]], xt[k * P:(k + 1) * P, halves[s]]
                                 ).then_inc((x_in, x_second)[s][k], 16)
                if s == 0:
                    for t in range(STAGE):
                        load(t, None, t)
                    sp.dma_start(posi[64:128, :], pos[64:128, :]).then_inc(sem("pos_in"), 16)
            with sp.Fori(1, TILES // STAGE) as i:
                for r in range(STAGE):
                    load(i * STAGE + r, (i - 1) * STAGE + r + 1, r)
            for s in range(2):
                for k in range(KT):
                    sp.wait_ge(sem("fin_ready"), s * KT + k + 1)
                    sp.dma_start(out[k * P:(k + 1) * P, halves[s]], hT[:, k, halves[s]]
                                 ).then_inc(sem("out_done"), 16)
            sp.wait_ge(sem("out_done"), 16 * 2 * KT)

        @block.gpsimd
        def _(pool):
            def split(r, landed, hi_count, used):
                slot, st = r % RING, r % STAGE
                pool.wait_ge(w_landed[st], landed)
                if used is not None:
                    pool.wait_ge(w_used, used)
                nc.gpsimd.tensor_tensor(whi[:, slot, :], stage[:, st, :], one_col.to_broadcast([P, 1024]),
                                        ALU.mult).then_inc(w_hi, 1)
                pool.wait_ge(w_hi, hi_count)
                nc.gpsimd.tensor_tensor(wlo[:, slot, :], stage[:, st, :], whi[:, slot, :].bitcast(F32),
                                        ALU.subtract).then_inc(w_ready, 1)

            pool.wait_ge(sem("const_in"), 32)
            for r in range(RING):
                split(r, 16 * (r // STAGE + 1), r + 1, None)
            ch = Chain(pool, sem("pool_chain"))
            rows = slice(64, 128)
            pool.wait_ge(w_ready, RING)
            pool.wait_ge(sem("pos_in"), 16)
            posf, ang, turns_part = lat[rows, 2, :], lat[rows, 1, :], lat[rows, 0, :]

            def rc(n):
                return cons[rows, C_ROPE + n:C_ROPE + n + 1]

            ch.link(nc.gpsimd.tensor_copy(posf, posi[rows, :]))
            ch.link(nc.gpsimd.tensor_scalar(ang, posf, rc(0), None, ALU.mult))
            ch.link(nc.gpsimd.tensor_scalar(posf, ang, 1.0 / TWO_PI, rc(1), ALU.mult, ALU.add))
            ch.link(nc.gpsimd.tensor_scalar(posf, posf, MAGIC, MAGIC, ALU.add, ALU.subtract))
            for part in (RED1, RED2, RED3):
                ch.link(nc.gpsimd.tensor_scalar(turns_part, posf, -part, None, ALU.mult))
                ch.link(nc.gpsimd.tensor_tensor(ang, ang, turns_part, ALU.add))
            ch.link(nc.gpsimd.tensor_scalar(ang, ang, rc(2), SIN_MAX, ALU.add, ALU.min))
            nc.gpsimd.tensor_scalar(ang, ang, -SIN_MAX, None, ALU.max).then_inc(sem("angles"), 1)
            pool.wait_ge(sem("angles"), 1)
            with pool.Fori(1, TILES // RING) as i:
                for r in range(RING):
                    split(r, (i * (RING // STAGE) + r // STAGE + 1) * 16, i * RING + r + 1,
                          (i - 1) * RING + r + 1)

        norms = ["n0", "nk", "nq", "F0n", "n1", "F1n", "nf"]
        small_norms = {"nk": 1, "nq": 2}
        norm_banks = {"n0": (6, 7), "nk": (0, 1), "nq": (4, 5), "F0n": (6, 7), "n1": (1, 4), "F1n": (6, 7),
                      "nf": (1, 4)}
        tile_by_tile = ("nk", "nq", "F0n", "F1n")

        def units(name):
            tiles = small_norms.get(name, KT)
            if name in tile_by_tile:
                return [(k, s) for k in range(tiles) for s in range(2)]
            return [(k, s) for s in range(2) for k in range(tiles)]

        def nbase(name, kind):
            before = norms[:norms.index(name)]
            wide = [n for n in before if n not in small_norms]
            return {"sq": sum(len(units(n)) for n in before), "acc": 2 * (KT - 2) * len(wide),
                    "half": 2 * len(before), "piece": 2 * KT * len(wide)}[kind]

        def sq_count(name, k, s):
            return nbase(name, "sq") + units(name).index((k, s)) + 1

        def acc_count(name, k, s):
            return nbase(name, "acc") + [u for u in units(name) if 1 <= u[0] <= KT - 2].index((k, s)) + 1

        def pe_sums(pe, name, s, squares):
            bank = norm_banks[name][s]

            def add(src, first, last):
                for c in range(4):
                    mm = nc.tensor.matmul(ps[:, bank, c:c + 1], src[:, (4 * s + c) * P:(4 * s + c + 1) * P], one_col,
                                          start=first and c == 0, stop=last, skip_group_check=True)
                return mm

            if name in small_norms:
                for k in range(small_norms[name]):
                    pe.wait_ge(sem("norm_sq"), sq_count(name, k, s))
                    mm = add(squares[:, k, :], k == 0, k == small_norms[name] - 1)
            else:
                pe.wait_ge(sem("norm_acc"), acc_count(name, KT - 2, s))
                add(acc, True, False)
                pe.wait_ge(sem("norm_sq"), sq_count(name, KT - 1, s))
                mm = add(squares[:, (KT - 1) % 2, :], False, True)
            mm.then_inc(sem("norm_mean"), 1)

        def pe_spread(pe, name, s, dg):
            pe.wait_ge(sem("norm_diag"), nbase(name, "half") + s + 1)
            nc.tensor.matmul(ps[:, norm_banks[name][s], :], ones, dg[:, halves[s]],
                             start=True, stop=True).then_inc(sem("norm_bc"), 1)

        def act_square(act, name, k, s, src, squares):
            scale = float(small_norms.get(name, KT)) ** -0.5 * float(P) ** -0.5
            if k >= 2:
                act.wait_ge(sem("norm_acc"), acc_count(name, max(1, k - 2), s))
            nc.scalar.activation(squares[:, k % 2, halves[s]], src[:, halves[s]], ACT.Square,
                                 scale=scale).then_inc(sem("norm_sq"), 1)

        def act_std(act, name, s):
            act.wait_ge(sem("norm_mean"), nbase(name, "half") + s + 1)
            nc.scalar.activation(std[:, 4 * s:4 * s + 4], ps[:, norm_banks[name][s], 0:4], ACT.Sqrt,
                                 bias=eps).then_inc(sem("norm_std"), 1)

        def act_squares(act, name, ready, std_at=None):
            for n, (k, s) in enumerate(units(name)):
                ready(k, s)
                act_square(act, name, k, s, hT[:, k, :], sq)
                if n == std_at:
                    act_std(act, name, 0)

        def act_round(act, name, std_0=False):
            if std_0:
                act_std(act, name, 0)
            for n in range(2 * KT):
                if n == 1:
                    act_std(act, name, 1)
                act.wait_ge(sem("norm_xn"), nbase(name, "piece") + n + 1)
                nc.scalar.copy(ahi[:, n % KT, halves[n // KT]], xnf[:, n % 2, 0:HALF]
                               ).then_inc(sem("norm_hi"), 1)

        def dve_accumulate(dve, name, k, s):
            dve.wait_ge(sem("norm_sq"), sq_count(name, k, s))
            if k >= 2:
                dve.wait_ge(sem("norm_acc"), acc_count(name, k - 1, s))
            nc.vector.tensor_tensor(acc[:, halves[s]], (sq[:, 0, :] if k == 1 else acc)[:, halves[s]],
                                    sq[:, k % 2, halves[s]], ALU.add).then_inc(sem("norm_acc"), 1)

        def dve_diagonal(dve, ch, name, s, dg):
            dve.wait_ge(sem("norm_std"), nbase(name, "half") + s + 1)
            ch.link(nc.vector.reciprocal(rstd[:, 4 * s:4 * s + 4], std[:, 4 * s:4 * s + 4]))
            nc.vector.tensor_tensor(dg[:, halves[s]].rearrange("p (c t) -> p c t", c=4),
                                    ident.unsqueeze(1).to_broadcast([P, 4, P]),
                                    rstd[:, 4 * s:4 * s + 4].unsqueeze(2).to_broadcast([P, 4, P]),
                                    ALU.mult).then_inc(sem("norm_diag"), 1)

        def dve_norm(dve, ch, name, gain):
            work = [(n % KT, halves[n // KT]) for n in range(2 * KT)]

            def lo(n):
                k, tok = work[n]
                dve.wait_ge(sem("norm_hi"), nbase(name, "piece") + n + 1)
                nc.vector.tensor_tensor(alo[:, k, tok], xnf[:, n % 2, 0:HALF], ahi[:, k, tok].bitcast(F32),
                                        ALU.subtract).then_inc(sem("norm_ready"), 1)

            for n, (k, tok) in enumerate(work):
                if n % KT == 0:
                    dve.wait_ge(sem("norm_bc"), nbase(name, "half") + n // KT + 1)
                if n >= 2:
                    lo(n - 2)
                    dve.wait_ge(sem("norm_ready"), nbase(name, "piece") + n - 1)
                nc.vector.scalar_tensor_tensor(out=xnf[:, n % 2, 0:HALF], in0=hT[:, k, tok], scalar=pcol(gain, k),
                                               in1=ps[:, norm_banks[name][n // KT], :], op0=ALU.mult,
                                               op1=ALU.mult).then_inc(sem("norm_xn"), 1)
                if n == 2:
                    dve_diagonal(dve, ch, name, 1, diag)
            lo(len(work) - 2)
            lo(len(work) - 1)

        def spread_banks(bank):
            return ps[:, bank:bank + 2, :].rearrange("p a b -> p (a b)")

        def product3(bank, wcols, slot, rhs_k, k_first, k_last, tok):
            hi, lo = whi[:, slot, wcols], wlo[:, slot, wcols]
            nc.tensor.matmul(bank, hi, rhs_k[0][:, tok], start=k_first, stop=False)
            nc.tensor.matmul(bank, hi, rhs_k[1][:, tok], start=False, stop=False)
            return nc.tensor.matmul(bank, lo, rhs_k[0][:, tok], start=False, stop=k_last)

        def m_tile(pe, t, slot, banks, evac=None, xn=None):
            pe.wait_ge(w_ready, t + 1)
            for s in range(2):
                if evac is not None:
                    evac(s)
                for k in range(KT):
                    if xn is not None:
                        xn(k, s)
                    mm = product3(ps[:, banks[s], :], slice(k * P, (k + 1) * P), slot,
                                  (ahi[:, k, :], alo[:, k, :]), k == 0, k == KT - 1,
                                  halves[s])
                mm.then_inc(half_done if s == 0 else w_used, 1)

        def normed_tiles(pe, t, name, count=2):
            pe.wait_ge(w_ready, t + count)
            for s in range(2):
                for k in range(KT):
                    if s == 0 and k == 4:
                        pe_spread(pe, name, 1, diag)
                    pe.wait_ge(sem("norm_ready"), nbase(name, "piece") + s * KT + k + 1)
                    for n in range(count):
                        mm = product3(ps[:, 2 * n + s, :], slice(k * P, (k + 1) * P), (t + n) % RING,
                                      (ahi[:, k, :], alo[:, k, :]), k == 0, k == KT - 1, halves[s])
                        if k == KT - 1:
                            mm.then_inc(half_done if s == 0 else w_used, 1)

        def pe_mlp(pe, L, t0, next_norm):
            up_read, added = sem(L + "up_read"), sem(L + "added")

            def up(t, slot, n, gv):
                m_tile(pe, t, slot, (2 * gv, 2 * gv + 1),
                       lambda s: pe.wait_ge(up_read, n * 4 + 2 * gv + s - 3))

            def down(t, slots, g, last):
                pe.wait_ge(w_ready, t + 2)
                if not last:
                    pe.wait_ge(sem(L + "hid"), g * 2 + 2)
                for n in range(2 * KT):
                    m, s = (n % KT, n // KT) if last else (n // 2, n % 2)
                    if last and m == 0:
                        pe.wait_ge(sem(L + "hid"), g * 2 + 2 + s)
                    pe.wait_ge(added, g * 2 * KT + (n + 1))
                    for j in range(2):
                        mm = product3(ps[:, 4 + n % 4, :], slice(m * P, (m + 1) * P), slots[j],
                                      (hid_hi[:, j, :], hid_lo[:, j, :]), j == 0, j == 1, halves[s])
                        if n == 2 * KT - 1:
                            mm.then_inc(w_used, 1)
                    if n < 2 * KT - 1:
                        mm.then_inc(sem(L + "down"), 1)
                    if last and n == KT + 4:
                        pe_sums(pe, next_norm, 0, sq)

            def pair(t, tm, g, last=False):
                for gv in range(2):
                    up(t + gv, (tm + gv) % RING, g * 2 + 1, gv)
                if not last:
                    for gv in range(2):
                        up(t + 2 + gv, (tm + 2 + gv) % RING, g * 2 + 2, gv)
                d = 2 if last else 4
                down(t + d, ((tm + d) % RING, (tm + d + 1) % RING), g, last)

            normed_tiles(pe, t0, L + "n")
            with pe.Fori(0, (FG - 1) // 2) as i:
                for j in range(2):
                    pair(i * 12 + (t0 + 2 + 6 * j), (t0 + 2 + 6 * j) % RING, i * 2 + j)
            pair(t0 + 2 + 6 * (FG - 1), (t0 + 2 + 6 * (FG - 1)) % RING, FG - 1, last=True)
            pe_spread(pe, next_norm, 0, diag)
            pe_sums(pe, next_norm, 1, sq)

        def half_base(t):
            n = t
            for a, b in ((T_L1_V, T_L1_V + 8),):
                n -= max(0, min(t, b) - a)
            for f in (T_FFN0, T_FFN1):
                if t >= f + 3 * FT:
                    n -= FT
            return n

        def act_mlp(act, ch, L, t0):
            hb = half_base(t0)

            def evac(n, t, gv, first=False):
                buf = upg if gv == 0 else upv
                if not first:
                    act.wait_ge(sem(L + "conv"), n * 2 + gv - 1)
                for s in range(2):
                    if s == 0:
                        act.wait_ge(half_done, n * 2 + (hb + gv + 1))
                    else:
                        act.wait_ge(w_used, t + gv + 1)
                    nc.scalar.copy(buf[:, 2 + s * HALF:2 + (s + 1) * HALF],
                                   ps[:, 2 * gv + s, :]).then_inc(sem(L + "up_read"), 1)

            def finish(n, j, down=None):
                act.wait_ge(sem(L + "conv"), n * 2 + 2)
                nc.scalar.activation(cvg[:, :], cvg[:, :], ACT.Silu).then_inc(sem(L + "silu"), 1)
                act.wait_ge(sem(L + "prod"), n + 1)
                if down is not None:
                    act.wait_ge(w_used, down)
                nc.scalar.copy(hid_hi[:, j, :], cvv[:, :]).then_inc(sem(L + "hid_hi"), 1)

            def pair(t, g, last=False):
                for gv in range(2):
                    evac(g * 2 + 1, t, gv)
                    if last and gv == 0:
                        n = g * 2 + 1
                        act.wait_ge(sem(L + "conv"), n * 2 + 1)
                        nc.scalar.activation(cvg[:, :], cvg[:, :], ACT.Silu).then_inc(sem(L + "silu"), 1)
                if last:
                    for s in range(2):
                        act.wait_ge(sem(L + "prod"), n + 1 + s)
                        nc.scalar.copy(hid_hi[:, 1, halves[s]], cvv[:, halves[s]]
                                       ).then_inc(sem(L + "hid_hi"), 1)
                else:
                    finish(g * 2 + 1, 1)
                if not last:
                    for gv in range(2):
                        evac(g * 2 + 2, t + 2, gv)
                    finish(g * 2 + 2, 0, down=t + 6)

            for gv in range(2):
                evac(0, t0, gv, first=True)
            finish(0, 0)
            with act.Fori(0, FG - 1) as g:
                pair(g * 6 + (t0 + 2), g)
            pair(t0 + 2 + 6 * (FG - 1), FG - 1, last=True)

        def dve_mlp(dve, ch, L, t0, layer, next_norm):
            col = _cols[f"conv{layer}"]

            def conv_step(n, gv, i):
                def w(i):
                    return pars[:, bass.ds(n * 8 + (col + gv * 4 + i), 1)]
                src, dst = (upg, cvg) if gv == 0 else (upv, cvv)
                if i == 0:
                    dve.wait_ge(sem(L + "up_read"), n * 4 + 2 * gv + 2)
                    ch.link(nc.vector.tensor_scalar(dst[:, :], src[:, 0:S], w(0), w(3), ALU.mult, ALU.add))
                elif i == 1:
                    ch.link(nc.vector.scalar_tensor_tensor(out=dst[:, :], in0=src[:, 1:S + 1], scalar=w(1),
                                                           in1=dst[:, :], op0=ALU.mult, op1=ALU.add))
                else:
                    nc.vector.scalar_tensor_tensor(out=dst[:, :], in0=src[:, 2:S + 2], scalar=w(2), in1=dst[:, :],
                                                   op0=ALU.mult, op1=ALU.add).then_inc(sem(L + "conv"), 1)

            def conv(n, gv):
                for i in range(3):
                    conv_step(n, gv, i)

            def prod(n):
                dve.wait_ge(sem(L + "silu"), n + 1)
                nc.vector.tensor_tensor(cvv[:, :], cvg[:, :], cvv[:, :], ALU.mult).then_inc(sem(L + "prod"), 1)

            def lo(n, j):
                dve.wait_ge(sem(L + "hid_hi"), n + 1)
                nc.vector.tensor_tensor(hid_lo[:, j, :], cvv[:, :], hid_hi[:, j, :].bitcast(F32),
                                        ALU.subtract).then_inc(sem(L + "hid"), 1)
                dve.wait_ge(sem(L + "hid"), n + 1)

            def last_half(n, s):
                tok, w = halves[s], [pars[:, n * 8 + col + 4 + i:n * 8 + col + 5 + i] for i in range(4)]
                dve.wait_ge(sem(L + "up_read"), n * 4 + 3 + s)
                dst = cvv[:, tok]
                ch.link(nc.vector.tensor_scalar(dst, upv[:, tok], w[0], w[3], ALU.mult, ALU.add))
                for i in (1, 2):
                    ch.link(nc.vector.scalar_tensor_tensor(out=dst, in0=upv[:, tok.start + i:tok.stop + i], scalar=w[i],
                                                           in1=dst, op0=ALU.mult, op1=ALU.add))
                dve.wait_ge(sem(L + "silu"), n + 1)
                nc.vector.tensor_tensor(dst, cvg[:, tok], dst, ALU.mult).then_inc(sem(L + "prod"), 1)
                dve.wait_ge(sem(L + "hid_hi"), n + 1 + s)
                nc.vector.tensor_tensor(hid_lo[:, 1, tok], dst, hid_hi[:, 1, tok].bitcast(F32),
                                        ALU.subtract).then_inc(sem(L + "hid"), 1)

            def add(g, t_last, last, between):
                for n in range(2 * KT):
                    m, s = (n % KT, n // KT) if last else (n // 2, n % 2)
                    if n < 2 * KT - 1:
                        dve.wait_ge(sem(L + "down"), g * (2 * KT - 1) + (n + 1))
                    else:
                        dve.wait_ge(w_used, t_last + 1)
                    h = hT[:, m, s * HALF:(s + 1) * HALF]
                    nc.vector.tensor_tensor(h, h, ps[:, 4 + n % 4, :], ALU.add).then_inc(sem(L + "added"), 1)
                    if n in between:
                        between[n]()
                    if last and m >= 2:
                        dve_accumulate(dve, next_norm, m - 1, s)
                    if last and n == KT + 6:
                        dve_diagonal(dve, ch, next_norm, 0, diag)

            def pair(t, g, last=False):
                if last:
                    conv(g * 2 + 1, 0)
                    for s in range(2):
                        last_half(g * 2 + 1, s)
                else:
                    for gv in range(2):
                        conv(g * 2 + 1, gv)
                    prod(g * 2 + 1)
                    lo(g * 2 + 1, 1)
                between = {}
                if not last:
                    conv(g * 2 + 2, 0)
                    between = {n + 1: lambda n=n: conv_step(g * 2 + 2, 1, n) for n in range(3)}
                    between[7] = lambda: prod(g * 2 + 2)
                add(g, t + (3 if last else 5), last, between)
                if not last:
                    lo(g * 2 + 2, 0)

            dve.sem_inc(sem(L + "added"), 4)
            nc.vector.memset(upg[:, 0:2], 0.0)
            ch.link(nc.vector.memset(upv[:, 0:2], 0.0))
            for gv in range(2):
                conv(0, gv)
            prod(0)
            lo(0, 0)
            with dve.Fori(0, FG - 1) as g:
                ch.enter(g, 8)
                pair(g * 6 + (t0 + 2), g)
            ch.leave(FG - 1)
            pair(t0 + 2 + 6 * (FG - 1), FG - 1, last=True)

        def m_tiles(pe, t0, count, read, ready):
            with pe.Fori(0, count // 4) as i:
                for b in range(4):
                    m_tile(pe, i * 4 + (t0 + b), (t0 + b) % RING, (2 * (b % 2), 2 * (b % 2) + 1),
                           lambda s: pe.wait_ge(read, i * 8 + (2 * b + s + 1)),
                           ready if b == 0 else None)

        def dve_out(dve, ch, L, t0, x_count, next_norm):
            hb = half_base(t0)
            for m in range(KT):
                dve.wait_ge(x_in[m], x_count)
                for s in range(2):
                    if s == 0:
                        dve.wait_ge(half_done, hb + m + 1)
                    else:
                        dve.wait_ge(w_used, t0 + m + 1)
                    h = hT[:, m, s * HALF:(s + 1) * HALF]
                    nc.vector.tensor_tensor(h, h, ps[:, 2 * (m % 2) + s, :], ALU.add).then_inc(sem(L + "res"), 1)
                    if m >= 2:
                        dve_accumulate(dve, next_norm, m - 1, s)
            dve_diagonal(dve, ch, next_norm, 0, diag)

        @block.tensor
        def _(pe):
            for name in ("lru_pre", "yt"):
                pe.sem_inc(sem(name), 1)
            pe.sem_inc(sem("o"), 2)
            pe.wait_ge(sem("const_in"), 32)
            pe_sums(pe, "n0", 0, sq)
            pe_spread(pe, "n0", 0, diag)
            pe_sums(pe, "n0", 1, sq)
            pe_spread(pe, "n0", 1, diag)
            with pe.Fori(0, LRU_T // 2) as i:
                for jj in range(2):
                    j = i * 2 + jj
                    t = i * 4 + 2 * jj
                    m_tile(pe, t, 2 * jj, (0, 1), lambda s: pe.wait_ge(sem("xr_read"), j * 2 + 1),
                           lambda k, s: pe.wait_ge(sem("norm_ready"), s * KT + k + 1))
                    m_tile(pe, t + 1, 2 * jj + 1, (2, 3), lambda s: pe.wait_ge(sem("gelu"), j + 1))
                    pe.wait_ge(sem("xc_ready"), j + 2)
                    pe.wait_ge(sem("wlfix_in"), j + 1)
                    pe.wait_ge(sem("lru_r"), j + 1)
                    pe.wait_ge(sem("lru_i"), j + 1)
                    for g in range(2):
                        for s in range(2):
                            nc.tensor.matmul(ps[:, 4 + 2 * g + s, :], wlfix[:, jj, g * P:(g + 1) * P],
                                             xc[:, s * HALF:(s + 1) * HALF], start=True, stop=True
                                             ).then_inc(sem("lru_pre"), 1)
            t = 2 * LRU_T
            pe.wait_ge(sem("xr_read"), 2 * LRU_T + 1)
            m_tile(pe, t, t % RING, (0, 1))
            pe.wait_ge(sem("gelu"), LRU_T + 1)
            m_tile(pe, t + 1, (t + 1) % RING, (2, 3))
            for s in range(2):
                pe_sums(pe, "nk", s, sqb)
            for s in range(2):
                pe_spread(pe, "nk", s, diagb)
            pe.wait_ge(sem("lru_r"), LRU_T + 1)
            m_tile(pe, t + 2, (t + 2) % RING, (4, 5))
            pe.wait_ge(sem("lru_i"), LRU_T + 1)
            m_tile(pe, t + 3, (t + 3) % RING, (6, 7))
            for s in range(2):
                pe_sums(pe, "nq", s, sqb)
            for s in range(2):
                pe_spread(pe, "nq", s, diagb)
            pe.wait_ge(sem("wb_in"), 32)
            pe.wait_ge(sem("kv_normed"), 1)
            wv = wkvb_s[:, :].rearrange("p (h e) -> p h e", h=HEADS)[:, :, NOPE:NOPE + VH]
            for c in range(TT):
                if c >= 2:
                    pe.wait_ge(sem("v_read"), c - 1)
                nc.tensor.matmul(ps[:, 2 + c % 2, :], lat[:, 2, c * P:(c + 1) * P], wv,
                                 start=True, stop=True).then_inc(sem("v_mm"), 1)

            def project(h, par, part, bank=0):
                if part == 0:
                    pe.wait_ge(sem("wh_in"), h * 3 + 3)
                if bank == 0 and not (isinstance(h, int) and h == 0):
                    pe.wait_ge(sem("proj_read"), h * 4 + part)
                s = part % 2
                tok = halves[s]
                if part < 2:
                    for k in range(2):
                        mm = nc.tensor.matmul(ps[:, bank, :], wh[:, par, k * P:(k + 1) * P], lat[:, k, tok],
                                              start=(k == 0), stop=(k == 1))
                else:
                    mm = nc.tensor.matmul(ps[0:NOPE, bank, :], wh[:, par, 2 * P:2 * P + NOPE], lat[:, 2, tok],
                                          start=True, stop=True)
                mm.then_inc(sem("proj"), 1)

            def scores(h, par, k, step):
                qt = order[k]
                if k == 0:
                    pe.wait_ge(sem("proj_read"), h * 4 + 4)
                if not isinstance(step, int) or step >= 2:
                    pe.wait_ge(sem("probs"), step)
                b = 1 + 2 * (k % 2)
                n = (qt + 1) * P
                for a in range(0, n, HALF):
                    w = min(HALF, n - a)
                    mm = nc.tensor.matmul(ps[:, b + a // HALF, 0:w], qh[0:QK, par, qt * P:(qt + 1) * P],
                                          kh[0:QK, par, a:a + w], start=True, stop=True)
                mm.then_inc(sem("scores"), 1)

            def transpose(k, step, grp):
                pe.wait_ge(sem("probs"), step + 2)
                for n, (a, w) in enumerate(groups_of(order[k])):
                    pe.wait_ge(sem("pt_read"), grp + n + 1)
                    for kb in range(a, a + w):
                        mm = nc.tensor.transpose(ps[:, 5 + (group_parity[k] + n) % 2, (kb - a) * P:(kb - a + 1) * P],
                                                 pbuf[:, k % 2, kb * P:(kb + 1) * P], ident)
                    mm.then_inc(sem("pt"), 1)

            def weigh(h, k, step, grp):
                pe.wait_ge(sem("o_read"), step + 1)
                qt = order[k]
                o = ps[:, 7, 0:VH]
                for n, (a, w) in enumerate(groups_of(qt)):
                    pe.wait_ge(sem("pt_read"), grp + n + 3)
                    for kb in range(a, a + w):
                        mm = nc.tensor.matmul(o, ptb[:, k % 2, kb * P:(kb + 1) * P],
                                              vtok[:, kb, bass.ds(h * VH, VH)], start=(kb == 0), stop=(kb == qt),
                                              skip_group_check=True)
                mm.then_inc(sem("o"), 1)

            def turn(p, n, last):
                _, first, blocks = turns[n]
                done = max(order.index(b) for b in range(first, first + blocks))
                pe.wait_ge(sem("o_read"), (p * 16 + (8 + done + 1)) + 1)
                if n == 0:
                    pe.wait_ge(sem("proj_read"), p * 8 + (8 if last else 12))
                else:
                    pe.wait_ge(sem("y_read"), p * 3 + n + 1)
                for b in range(blocks):
                    mm = nc.tensor.transpose(ps[:, 0, b * P:(b + 1) * P], opair[:, first + b, :], ident)
                mm.then_inc(sem("yt"), 1)

            def head_pair(p, last=False):
                for i in range(16):
                    par, k = i // 8, i % 8
                    step = p * 16 + i
                    grp = p * 24 + (12 * par + groups_before[k])
                    transpose(k, step, grp)
                    j = i + 2
                    if not (last and j >= 16):
                        scores(p * 2 + j // 8, (j // 8) % 2, j % 8, p * 16 + j)
                    if i == 0:
                        pe.wait_ge(sem("y_read"), p * 3 + 1)
                    if k < 4 and not (last and par == 1):
                        project(p * 2 + par + 1, 1 - par, k)
                    weigh(p * 2 + par, k, step, grp)
                    for n, (slot, _, _) in enumerate(turns):
                        if par == 1 and slot == k:
                            turn(p, n, last)

            pe.wait_ge(sem("v_read"), TT)
            pe.wait_ge(sem("q_normed"), 2)
            pe.wait_ge(sem("kpe_ready"), 1)
            for part in range(4):
                project(0, 0, part, first_banks[part])
            for i in range(2):
                scores(0, 0, i, i)
            with pe.Fori(0, HEADS // 2 - 1) as p:
                head_pair(p)
            head_pair(HEADS // 2 - 1, last=True)
            pe.wait_ge(sem("lru_split"), LRU_T)
            pe.wait_ge(sem("y_read"), len(turns) * (HEADS // 2) + 1)
            m_tiles(pe, T_L0_OUT, KT, sem("L0res"), None)
            for s in range(2):
                pe_sums(pe, "F0n", s, sq)
            pe_spread(pe, "F0n", 0, diag)
            pe_mlp(pe, "F0", T_FFN0, "n1")


            def gate_product():
                pe.wait_ge(sem("wg_split"), 1)
                for s in range(2):
                    for k in range(KT):
                        wk, tok = slice(k * P, (k + 1) * P), halves[s]
                        nc.tensor.matmul(ps[:, 4 + s, :], wghi[:, wk], ahi[:, k, tok], start=(k == 0), stop=False)
                        nc.tensor.matmul(ps[:, 4 + s, :], wghi[:, wk], alo[:, k, tok], start=False, stop=False)
                        mm = nc.tensor.matmul(ps[:, 4 + s, :], wglo[:, wk], ahi[:, k, tok], start=False,
                                              stop=(k == KT - 1))
                    mm.then_inc(sem("g_mm"), 1)

            def gates_turn():
                pe.wait_ge(sem("g_in"), 1)
                for c in range(TT):
                    mm = nc.tensor.transpose(ps[:, 6, c * 8:(c + 1) * 8], grow[:, c * P:(c + 1) * P], ident[0:8, 0:8])
                mm.then_inc(sem("g_pre"), 1)

            def gates_sum():
                pe.wait_ge(sem("g_sp"), 1)
                nc.tensor.matmul(ps[:, 5, 0:TT * MH], tri, gsp, start=True, stop=True
                                 ).then_inc(sem("g_cum"), 1)

            def gates_rows():
                pe.wait_ge(sem("g_a"), 2)
                nc.tensor.transpose(ps[0:32, 6, 0:P], ga, ident)
                nc.tensor.transpose(ps[0:32, 6, P:2 * P], gnb, ident).then_inc(sem("g_turned"), 1)

            def gates_ends():
                pe.wait_ge(sem("g_max"), 2)
                nc.tensor.matmul(ps[0:1, 7, 0:32], gAT[0:32, P - 1:P], ident[0:32, 0:32], start=True, stop=True)
                nc.tensor.matmul(ps[0:1, 7, 32:64], g_last, ident[0:32, 0:32], start=True, stop=True
                                 ).then_inc(sem("g_rows"), 1)

            def gates_spread():
                pe.wait_ge(sem("g_m"), 1)
                nc.tensor.matmul(ps[0:32, 7, 64:65], m_row, ones[0:1, 0:1], start=True, stop=True)
                nc.tensor.matmul(ps[:, 7, 128:160], ones[0:1, :], m_row, start=True, stop=True)
                nc.tensor.matmul(ps[:, 7, 160:192], ones[0:1, :], ml_row, start=True, stop=True
                                 ).then_inc(sem("g_spread"), 1)

            def gates_stabilisers():
                pe.wait_ge(sem("g_MT"), 1)
                nc.tensor.transpose(ps[:, 7, 256:288], gMT[0:32, :], ident[0:32, 0:32]).then_inc(sem("g_M"), 1)

            behind = [None, None, gates_turn, gates_sum, gates_rows, gates_ends, gates_spread,
                      gates_stabilisers]
            normed_tiles(pe, T_L1, "n1")
            gate_product()
            for h in range(1, MH):
                for qk in range(2):
                    t = T_L1 + 2 * h + qk
                    m_tile(pe, t, t % RING, (2 * qk, 2 * qk + 1),
                           lambda s: pe.wait_ge(sem("l1_read"), 4 * h + 2 * qk + s - 3))
                    behind[2 * h + qk]()

            pe.wait_ge(sem("l1_read"), 4 * MH)
            pe.wait_ge(sem("g_e"), 1)

            with pe.Fori(0, 2) as n:
                for j in range(4):
                    slot = (T_L1_V + j) % RING
                    pe.wait_ge(w_ready, n * 4 + (T_L1_V + j + 1))
                    for c in range(TT):
                        if j == 0:
                            pe.wait_ge(sem("l1_read"), n * 8 + (4 * MH + c + 1 - TT))
                        for kk in range(2):
                            k = 2 * j + kk
                            tok = slice(c * P, (c + 1) * P)
                            cols = slice(kk * HALF, (kk + 1) * HALF)
                            nc.tensor.matmul(ps[:, c, :], ahi[:, k, tok], whi[:, slot, cols], start=(k == 0),
                                             stop=False)
                            nc.tensor.matmul(ps[:, c, :], alo[:, k, tok], whi[:, slot, cols], start=False,
                                             stop=False)
                            mm = nc.tensor.matmul(ps[:, c, :], ahi[:, k, tok], wlo[:, slot, cols], start=False,
                                                  stop=(k == KT - 1))
                        if c == TT - 1:
                            mm.then_inc(w_used, 1)
                        elif j == 3:
                            mm.then_inc(sem("v1_mm"), 1)
            pe.wait_ge(sem("l1_read"), 4 * MH + 2 * TT)

            def chunk_scores(c):
                tok = slice(c * P, (c + 1) * P)
                pe.wait_ge(sem("mtx"), c + 1)
                if c >= 1:
                    pe.wait_ge(sem("mw"), 4 * c)
                nc.tensor.matmul(ps[:, 0, :], ones[0:32, :], mtx[0:32, :], start=True, stop=False,
                                 skip_group_check=True)
                for h in range(MH):
                    mm = nc.tensor.matmul(ps[:, 0, h * P:(h + 1) * P], ident, masks, start=False, stop=(h == 3),
                                          skip_group_check=True)
                mm.then_inc(sem("m_bc"), 1)
                if c >= 1:
                    pe.wait_ge(sem("msw"), c)
                    pe.wait_ge(sem("mkw"), 4 * c)
                for h in range(MH):
                    mm = nc.tensor.matmul(ps[:, 1, h * P:(h + 1) * P], kT[:, h, tok], qT[:, h, tok],
                                          start=(h == 0), stop=(h == MH - 1), skip_group_check=True)
                mm.then_inc(sem("m_qk"), 1)
                for h in range(MH):
                    mm = nc.tensor.transpose(ps[:, 2, h * P:(h + 1) * P], kT[:, h, tok], ident)
                mm.then_inc(sem("m_kt"), 1)

            def chunk_head(c, h):
                tok = slice(c * P, (c + 1) * P)
                n = 4 * c + h
                if n >= 1:
                    pe.wait_ge(sem("m_inter_read"), n)
                    if c >= 1:
                        pe.wait_ge(sem("m_state"), n - 3)
                nc.tensor.matmul(ps[:, 5, 0:MV + 1], qT[:, h, tok], cst[:, h, 0:MV + 1],
                                 start=True, stop=True).then_inc(sem("m_inter"), 1)
                if n >= 2:
                    pe.wait_ge(sem("m_num_read"), n - 1)
                pe.wait_ge(sem("msw"), c + 1)
                nc.tensor.matmul(ps[:, 3 + h % 2, 0:MV + 1], msw[:, c % 2, h * P:(h + 1) * P],
                                 vaug[:, c, h, 0:MV + 1], start=True, stop=True).then_inc(sem("m_num"), 1)
                if n >= 1:
                    pe.wait_ge(sem("m_state"), n)
                pe.wait_ge(sem("mkw"), 4 * c + h + 1)
                nc.tensor.matmul(ps[:, 6, 0:MV + 1], mkw[:, c % 2, h * P:(h + 1) * P],
                                 vaug[:, c, h, 0:MV + 1], start=True, stop=True).then_inc(sem("m_kv"), 1)

            def chunk_turn(c, blocks):
                for b in blocks:
                    n = 2 * c + b
                    pe.wait_ge(sem("m_hn"), c + 1)
                    if n >= 1:
                        pe.wait_ge(sem("m_y"), 4 * n)
                    for i in range(4):
                        h, e = 2 * b + i // 2, i % 2
                        mm = nc.tensor.transpose(ps[:, 7, i * P:(i + 1) * P], mhn[:, h, e * P:(e + 1) * P], ident)
                    mm.then_inc(sem("m_turned"), 1)

            pe.wait_ge(sem("cst0"), 1)
            chunk_scores(0)
            for c in range(TT):
                if c + 1 < TT:
                    chunk_scores(c + 1)
                for h in range(MH):
                    chunk_head(c, h)
                    if c >= 1 and h % 2:
                        chunk_turn(c - 1, (h // 2,))
            chunk_turn(TT - 1, range(2))

            pe.wait_ge(sem("m_y"), 8 * TT)

            m_tiles(pe, T_L1_O, KT, sem("sigo"), None)
            m_tiles(pe, T_L1_OUT, KT, sem("L1res"), lambda k, s: pe.wait_ge(sem("L1mix"), k + 1))
            for s in range(2):
                pe_sums(pe, "F1n", s, sq)
            pe_spread(pe, "F1n", 0, diag)
            pe_mlp(pe, "F1", T_FFN1, "nf")
            pe_spread(pe, "nf", 1, diag)

        @block.scalar
        def _(act):
            ch = Chain(act, sem("act_chain"))
            for name in ("xr_read", "gelu", "lru_r", "lru_i", "probs"):
                act.sem_inc(sem(name), 1)
            act.sem_inc(sem("pt_read"), 2)
            act.dma_start(wlru_s[:], wlru).then_inc(sem("wlru_in"), 16)
            act.dma_start(wkvb_s[:], wkvb).then_inc(sem("wb_in"), 16)
            act.wait_ge(sem("const_in"), 32)
            act.wait_ge(sem("eps_set"), 1)
            act.wait_ge(sem("lam_abs"), 1)
            nc.scalar.activation(l1, l0, ACT.Exp).then_inc(sem("lam_exp"), 1)
            act_squares(act, "n0", lambda k, s: act.wait_ge((x_in, x_second)[s][k], 16), KT + 1)
            act_round(act, "n0")
            def lru_par(j, n):
                return pars[:, bass.ds(j * 8 + (_cols["lru"] + n), 1)]

            act.wait_ge(sem("wlru_in"), 16)
            act.wait_ge(sem("lcoef"), 1)
            with act.Fori(0, LRU_T // 2) as i:
                for jj in range(2):
                    j = i * 2 + jj
                    t = i * 4 + 2 * jj
                    act.wait_ge(sem("lru_pre"), j * 4 + 1)
                    nc.scalar.copy(wlfix[:, jj, :], wlru_s[:, bass.ds(j, 1), :].rearrange("p a b -> p (a b)")
                                   ).then_inc(sem("wlfix_in"), 1)
                    act.wait_ge(sem("xc_ready"), j + 1)
                    act.wait_ge(half_done, t + 1)
                    nc.scalar.copy(xrp[:, 3:3 + HALF], ps[:, 0, :]).then_inc(sem("xr_read"), 1)
                    act.wait_ge(w_used, t + 1)
                    nc.scalar.copy(xrp[:, 3 + HALF:3 + S], ps[:, 1, :]).then_inc(sem("xr_read"), 1)
                    act.wait_ge(sem("ylru"), j + 1)
                    act.wait_ge(w_used, t + 2)
                    nc.scalar.activation(lg[:, :], spread_banks(2), ACT.Gelu_apprx_tanh).then_inc(sem("gelu"), 1)
                    act.wait_ge(sem("lru_pre"), j * 4 + 2 + 1)
                    nc.scalar.activation(lr[:, :], spread_banks(4), ACT.Sigmoid,
                                         bias=lru_par(j, 5)).then_inc(sem("lru_r"), 1)
                    act.wait_ge(sem("lru_pre"), j * 4 + 4 + 1)
                    nc.scalar.activation(li[:, :], spread_banks(6), ACT.Sigmoid,
                                         bias=lru_par(j, 6)).then_inc(sem("lru_i"), 1)
                    act.wait_ge(sem("lru_r"), j + 2)
                    nc.scalar.activation(lc[:, :], lr[:, :], ACT.Exp,
                                         scale=small[:, bass.ds(j + 80, 1)]).then_inc(sem("lru_a"), 1)
                    act.wait_ge(sem("lru_a"), j + 1)
                    nc.scalar.activation(lr[:, :], lr[:, :], ACT.Tanh,
                                         scale=small[:, bass.ds(j + 20, 1)]).then_inc(sem("lru_u"), 1)
                    act.wait_ge(sem("lru_u"), j + 1)
                    nc.scalar.activation(ls[:, :], lr[:, :], ACT.Sqrt).then_inc(sem("lru_sq"), 1)
            t = 2 * LRU_T
            act.wait_ge(sem("lru_pre"), 4 * LRU_T + 1)
            act.dma_start(wqb_s[:], wqb).then_inc(sem("wb_in"), 16)
            act.wait_ge(sem("angles"), 1)
            nc.scalar.activation(tab[64:128, :], lat[64:128, 1, :], ACT.Sin,
                                 scale=cons[64:128, C_ROPE + 3:C_ROPE + 4]).then_inc(sem("tab_ready"), 1)
            act.wait_ge(sem("tab_ready"), 1)

            def latent(n, t, banks):
                act.wait_ge(w_used, t + 1)
                nc.scalar.copy(lat[:, n, :], spread_banks(banks)).then_inc(sem("lat_in"), 1)

            latent(2, t, 0)
            act.wait_ge(sem("lat_in"), 1)
            for s in range(2):
                act_square(act, "nk", 0, s, lat[:, 2, :], sqb)
            latent(0, t + 1, 2)
            for s in range(2):
                act_std(act, "nk", s)
            latent(1, t + 2, 4)
            for k in range(2):
                act.wait_ge(sem("lat_in"), k + 2)
                for s in range(2):
                    act_square(act, "nq", k, s, lat[:, k, :], sqb)
            for s in range(2):
                act_std(act, "nq", s)
            act.wait_ge(w_used, T_L0_OUT)
            for j in range(LRU_T):
                act.wait_ge(sem("ylru"), j + 2)
                nc.scalar.copy(ahi[:, j, :], ylru[:, j, :]).then_inc(sem("lru_hi"), 1)
            for c in range(TT):
                act.wait_ge(sem("v_mm"), c + 1)
                nc.scalar.copy(vtok[:, c, :], ps[:, 2 + c % 2, :]).then_inc(sem("v_read"), 1)

            act.wait_ge(sem("wb_in"), 32)

            def head_weights(h, par):
                if not isinstance(h, int) or h >= 2:
                    act.wait_ge(sem("proj"), h * 4 - 4)
                for n in range(2):
                    nc.scalar.copy(wh[:, par, n * P:(n + 1) * P],
                                   wqb_s[:, n, bass.ds(h * P, P)]).then_inc(sem("wh_in"), 1)
                nc.scalar.copy(wh[:, par, 2 * P:3 * P], wkvb_s[:, bass.ds(h * P, P)]).then_inc(sem("wh_in"), 1)

            def nope(h, par, part, bank=0):
                s = part % 2
                tok = halves[s]
                act.wait_ge(sem("proj"), h * 4 + (part + 1))
                if part < 2:
                    nc.scalar.mul(qh[0:NOPE, par, tok], ps[0:NOPE, bank, :], QK_SCALE).then_inc(sem("q_nope"), 1)
                else:
                    nc.scalar.copy(kh[0:NOPE, par, tok], ps[0:NOPE, bank, :]).then_inc(sem("proj_read"), 1)

            def exps(k, step):
                n = (order[k] + 1) * P
                act.wait_ge(sem("nmax"), step + 1)
                b = 1 + 2 * (k % 2)
                sc = ps[:, b:b + 2, :].rearrange("p a b -> p (a b)")[:, 0:n]
                nc.scalar.activation(pbuf[:, k % 2, 0:n], sc, ACT.Exp, bias=nmax[:, k % 2:k % 2 + 1],
                                     accum_out=rsum[:, k % 4:k % 4 + 1]).then_inc(sem("probs"), 1)

            def turned(k, step, grp):
                act.wait_ge(sem("o"), step + 1)
                for n, (a, w) in enumerate(groups_of(order[k])):
                    act.wait_ge(sem("pt"), grp + (n + 1))
                    nc.scalar.copy(ptb[:, k % 2, a * P:(a + w) * P],
                                   ps[:, 5 + (group_parity[k] + n) % 2, 0:w * P]).then_inc(sem("pt_read"), 1)

            def y_hi(p, n):
                _, first, blocks = turns[n]
                act.wait_ge(sem("yt"), (p * 3 + (n + 1)) + 1)
                hi = ahi[:, bass.ds(p + LRU_T, 1), first * P:(first + blocks) * P]
                nc.scalar.copy(hi.rearrange("p a b -> p (a b)"),
                               ps[:, 0, 0:blocks * P]).then_inc(sem("y_hi"), 1)

            def head_pair(p, last=False):
                for i in range(16):
                    par, k = i // 8, i % 8
                    if not (last and i == 15):
                        exps((i + 1) % 8, p * 16 + (i + 1))
                    turned(k, p * 16 + i, p * 24 + (12 * par + groups_before[k]))
                    for n, (slot, _, _) in enumerate(turns):
                        if par == 1 and k == min(slot + 1, 7):
                            y_hi(p, n)
                    if k < 4 and not (last and par == 1):
                        nope(p * 2 + par + 1, 1 - par, k)
                    if k == 4 and not last:
                        head_weights(p * 2 + par + 2, par)

            act.wait_ge(sem("kpe_in"), 2)
            act.wait_ge(sem("ylru"), LRU_T + 1)
            head_weights(0, 0)
            head_weights(1, 1)
            for part in range(4):
                nope(0, 0, part, first_banks[part])
            exps(0, 0)
            with act.Fori(0, HEADS // 2 - 1) as p:
                head_pair(p)
            head_pair(HEADS // 2 - 1, last=True)
            act.wait_ge(sem("o"), 8 * HEADS + 2)
            for k in range(KT):
                act.dma_start(hT[:, k, :], xt[k * P:(k + 1) * P, :]).then_inc(x_in[k], 16)
            act_squares(act, "F0n", lambda k, s: act.wait_ge(sem("L0res"), 2 * k + s + 5))
            act_round(act, "F0n", std_0=True)
            act_mlp(act, ch, "F0", T_FFN0)

            last_added = 2 * KT * (FG - 1) + 4
            act_squares(act, "n1", lambda k, s: act.wait_ge(sem("F0added"), last_added + KT * s + k + 1), KT + 5)
            act.dma_start(spill, hT[:, :, :].rearrange("p a b -> p (a b)")).then_inc(sem("spilled"), 16)
            act.dma_start(wgs[:], wg).then_inc(sem("wg_in"), 16)
            act_round(act, "n1")
            act.wait_ge(sem("wg_in"), 16)
            nc.scalar.copy(wghi[:], wgs[:]).then_inc(sem("wg_hi"), 1)

            hb = half_base(T_L1)

            def head_part(h, qk):
                for s in range(2):
                    if s == 0:
                        act.wait_ge(half_done, hb + 2 * h + qk + 1)
                    else:
                        act.wait_ge(w_used, T_L1 + 2 * h + qk + 1)
                    tok = halves[s]
                    if qk == 0:
                        ins = nc.scalar.mul(qT[:, h, tok], ps[:, s, :], float(MQK) ** -0.5)
                    else:
                        ins = nc.scalar.copy(kT[:, h, tok], ps[:, 2 + s, :])
                    ins.then_inc(sem("l1_read"), 1)

            head_part(0, 0)
            head_part(0, 1)
            act.wait_ge(sem("g_mm"), 2)
            nc.scalar.copy(grow, spread_banks(4)[0:8, :]).then_inc(sem("g_in"), 1)
            head_part(1, 0)
            tv = gt.rearrange("p (c g) -> p c g", c=TT)
            act.wait_ge(sem("g_z"), 1)
            nc.scalar.activation(gt, gz, ACT.Tanh, scale=1.0 / GATE_CAP).then_inc(sem("g_tanh"), 1)
            act.wait_ge(sem("g_tanh"), 1)
            ch.link(nc.scalar.activation(gex.rearrange("p (c g) -> p c g", c=TT), tv[:, :, MH:2 * MH], ACT.Exp,
                                         scale=-GATE_CAP))
            nc.scalar.activation(gsp, gex, ACT.Ln, bias=one_col).then_inc(sem("g_sp"), 1)
            head_part(1, 1)
            for h in range(2, MH):
                head_part(h, 0)
                head_part(h, 1)
            act.wait_ge(sem("g_E"), 1)
            nc.scalar.activation(g_exp, g_exp, ACT.Exp).then_inc(sem("g_e"), 1)
            act.wait_ge(sem("spilled"), 16)
            with act.Fori(0, 2) as n:
                for c in range(TT):
                    if c < TT - 1:
                        act.wait_ge(sem("v1_mm"), n * (TT - 1) + (c + 1))
                    else:
                        act.wait_ge(w_used, n * 4 + (T_L1_V + 4))
                    nc.scalar.copy(vaug[:, c, bass.ds(n * 2, 2), 0:MV],
                                   ps[:, c, :].rearrange("p (h e) -> p h e", h=2)).then_inc(sem("l1_read"), 1)

            def stab(c):
                act.wait_ge(sem("m_bc"), c + 1)
                if c >= 2:
                    act.wait_ge(sem("msw"), c - 1)
                for h in range(MH):
                    nc.scalar.activation(mw[:, c % 2, h * P:(h + 1) * P], ps[:, 0, h * P:(h + 1) * P], ACT.Exp,
                                         bias=ga[:, 4 * c + h:4 * c + h + 1], scale=-1.0).then_inc(sem("mw"), 1)

            def squares(c, h):
                act.wait_ge(sem("m_num_read"), 4 * c + h + 1)
                if c + h >= 1:
                    act.wait_ge(sem("m_sq"), 4 * c + h)
                nc.scalar.activation(junk[:], mnum[:, h, 0:MV], ACT.Square,
                                     accum_out=mss[:, h:h + 1]).then_inc(sem("m_sq"), 1)

            act.wait_ge(sem("g_e"), 1)
            stab(0)
            stab(1)
            for c in range(TT):
                for h in range(MH):
                    n = 4 * c + h
                    act.wait_ge(sem("m_inter"), n + 1)
                    if n >= 1:
                        act.wait_ge(sem("m_num_read"), n)
                    nc.scalar.mul(mtmp[:, 0:MV + 1], ps[:, 5, 0:MV + 1],
                                  g_exp[:, n:n + 1]).then_inc(sem("m_inter_read"), 1)
                    if h >= 1:
                        squares(c, h - 1)
                squares(c, MH - 1)
                if c + 2 < TT:
                    stab(c + 2)
                act.wait_ge(sem("m_v"), c + 1)
                nc.scalar.activation(msd, mt2, ACT.Sqrt, bias=eps, scale=1.0 / MV).then_inc(sem("m_sd"), 1)
            hb = half_base(T_L1_O)
            for m in range(KT):
                for s in range(2):
                    n = 2 * m + s
                    if s == 0:
                        act.wait_ge(half_done, hb + m + 1)
                    else:
                        act.wait_ge(w_used, T_L1_O + m + 1)
                    if n >= 2:
                        act.wait_ge(sem("y_gated"), n - 1)
                    nc.scalar.activation(sigo[:, s, :], ps[:, 2 * (m % 2) + s, :],
                                         ACT.Sigmoid).then_inc(sem("sigo"), 1)
            act.wait_ge(w_used, T_L1_OUT)
            for m in range(KT):
                act.wait_ge(sem("y_gated"), 2 * m + 2)
                nc.scalar.copy(ahi[:, m, :].rearrange("p (c t) -> p c t", c=TT),
                               vaug[:, :, m // 2, (m % 2) * P:(m % 2 + 1) * P]).then_inc(sem("L1hi"), 1)
            act.wait_ge(sem("L1mix"), KT)
            for k in range(KT):
                act.dma_start(hT[:, k, :], spill[:, k * S:(k + 1) * S]).then_inc(x_in[k], 16)
            act_squares(act, "F1n", lambda k, s: act.wait_ge(sem("L1res"), 2 * k + s + 5))
            act_round(act, "F1n", std_0=True)
            act_mlp(act, ch, "F1", T_FFN1)
            act_squares(act, "nf", lambda k, s: act.wait_ge(sem("F1added"), last_added + KT * s + k + 1), KT + 5)
            act_std(act, "nf", 1)

        @block.vector
        def _(dve):
            ch = Chain(dve, sem("dve_chain"))
            for name in ("ylru", "xc_ready", "y_read", "o_read"):
                dve.sem_inc(sem(name), 1)
            nc.vector.memset(eps, EPS).then_inc(sem("eps_set"), 1)
            dve.sem_inc(sem("L0res"), 4)
            dve.wait_ge(sem("const_in"), 32)
            lam = pars[:, _cols["lru"]:_cols["lru"] + 8 * LRU_T].rearrange("p (j n) -> p j n", n=8)[:, :, 7]
            nc.vector.scalar_tensor_tensor(out=l0, in0=lam, scalar=-1.0, in1=lam, op0=ALU.mult,
                                           op1=ALU.min).then_inc(sem("lam_abs"), 1)
            dve.wait_ge(sem("lam_exp"), 1)
            ch.link(nc.vector.tensor_scalar(l2, l1, 2.0, None, ALU.add))
            ch.link(nc.vector.reciprocal(l2, l2))
            ch.link(nc.vector.tensor_tensor(l1, l1, l2, ALU.mult))
            ch.link(nc.vector.tensor_tensor(l2, l1, l1, ALU.mult))
            ch.link(nc.vector.tensor_scalar(l3, l2, 1.0 / 17, 1.0 / 15, ALU.mult, ALU.add))
            for n in (13, 11, 9, 7, 5, 3, 1):
                ch.link(nc.vector.tensor_tensor(l3, l3, l2, ALU.mult))
                ch.link(nc.vector.tensor_scalar(l3, l3, 1.0 / n, None, ALU.add))
            ch.link(nc.vector.tensor_tensor(l3, l3, l1, ALU.mult))
            ch.link(nc.vector.tensor_scalar(l0, lam, -1.0, 0.0, ALU.mult, ALU.max))
            ch.link(nc.vector.tensor_scalar(l3, l3, 8.0, None, ALU.mult))
            ch.link(nc.vector.scalar_tensor_tensor(out=lcoef, in0=l0, scalar=4.0, in1=l3, op0=ALU.mult,
                                                   op1=ALU.add))
            nc.vector.tensor_scalar(lexp, lcoef, -2.0, None, ALU.mult).then_inc(sem("lcoef"), 1)
            for k in range(1, KT - 1):
                dve_accumulate(dve, "n0", k, 0)
            for k in range(1, KT - 1):
                dve_accumulate(dve, "n0", k, 1)
                if k == 2:
                    dve_diagonal(dve, ch, "n0", 0, diag)
            dve_norm(dve, ch, "n0", "e_g")
            ch.link(nc.vector.memset(xrp[:, 0:3], 0.0))
            with dve.Fori(0, LRU_T // 2) as i:
                ch.enter(i, 2 * 7)
                for jj in range(2):
                    j = i * 2 + jj

                    def w(n):
                        return pars[:, bass.ds(j * 8 + (_cols["lru"] + n), 1)]

                    dve.wait_ge(sem("xr_read"), j * 2 + 2 + 1)
                    dve.wait_ge(sem("lru_pre"), j * 4 + 1)
                    ch.link(nc.vector.tensor_scalar(xc[:, :], xrp[:, 0:S], w(0), w(4), ALU.mult, ALU.add))
                    for n in (1, 2):
                        ch.link(nc.vector.scalar_tensor_tensor(out=xc[:, :], in0=xrp[:, n:n + S], scalar=w(n),
                                                               in1=xc[:, :], op0=ALU.mult, op1=ALU.add))
                    nc.vector.scalar_tensor_tensor(out=xc[:, :], in0=xrp[:, 3:3 + S], scalar=w(3), in1=xc[:, :],
                                                   op0=ALU.mult, op1=ALU.add).then_inc(sem("xc_ready"), 1)
                    dve.wait_ge(sem("lru_i"), j + 2)
                    dve.wait_ge(sem("xc_ready"), j + 2)
                    ch.link(nc.vector.tensor_tensor(li[:, :], li[:, :], xc[:, :], ALU.mult))
                    dve.wait_ge(sem("lru_sq"), j + 1)
                    ch.link(nc.vector.scalar_tensor_tensor(out=ls[:, :], in0=lc[:, :], scalar=1.0, in1=ls[:, :],
                                                           op0=ALU.add, op1=ALU.mult))
                    ch.link(nc.vector.tensor_tensor(ls[:, :], ls[:, :], li[:, :], ALU.mult))
                    y = ylru[:, bass.ds(j, 1), :].rearrange("p a b -> p (a b)")
                    ch.link(nc.vector.tensor_tensor_scan(y, lc[:, :], ls[:, :], 0.0, ALU.mult, ALU.add))
                    dve.wait_ge(sem("gelu"), j + 2)
                    nc.vector.tensor_tensor(y, y, lg[:, :], ALU.mult).then_inc(sem("ylru"), 1)
            ch.leave(LRU_T // 2)

            dve.wait_ge(sem("lat_in"), 1)
            for s in range(2):
                dve_diagonal(dve, ch, "nk", s, diagb)
            dve.wait_ge(sem("norm_bc"), nbase("nk", "half") + 2)
            nc.vector.scalar_tensor_tensor(out=lat[:, 2, :], in0=lat[:, 2, :], scalar=pcol("kv_g", 0),
                                           in1=spread_banks(0), op0=ALU.mult, op1=ALU.mult
                                           ).then_inc(sem("kv_normed"), 1)
            dve.wait_ge(w_used, T_L0_OUT)
            dve.wait_ge(sem("tab_ready"), 1)
            a32, b32 = slice(NOPE, QK), slice(QK, P)
            kr = spread_banks(6)
            nc.vector.tensor_tensor(rt1[a32, :], kr[a32, :], tab[a32, :], ALU.mult)
            ch.link(nc.vector.tensor_tensor(rt2[a32, :], kr[b32, :], tab[b32, :], ALU.mult))
            nc.vector.tensor_tensor(kpe[a32, :], rt1[a32, :], rt2[a32, :], ALU.add).then_inc(sem("kpe_ready"), 1)
            for s in range(2):
                dve_diagonal(dve, ch, "nq", s, diagb)
            dve.wait_ge(sem("norm_bc"), nbase("nq", "half") + 2)
            for k in range(2):
                nc.vector.scalar_tensor_tensor(out=lat[:, k, :], in0=lat[:, k, :], scalar=pcol("q_g", k),
                                               in1=spread_banks(4), op0=ALU.mult, op1=ALU.mult
                                               ).then_inc(sem("q_normed"), 1)
            for j in range(LRU_T):
                dve.wait_ge(sem("lru_hi"), j + 1)
                nc.vector.tensor_tensor(alo[:, j, :], ylru[:, j, :], ahi[:, j, :].bitcast(F32),
                                        ALU.subtract).then_inc(sem("lru_split"), 1)
            dve.wait_ge(sem("kpe_ready"), 1)
            dve.wait_ge(sem("lru_split"), LRU_T)
            for par in range(2):
                nc.vector.tensor_copy(kh[a32, par, :], kpe[a32, :]).then_inc(sem("kpe_in"), 1)

            def rotate(h, par, part, bank=0):
                tok = slice(part * HALF, (part + 1) * HALF)
                dve.wait_ge(sem("q_nope"), h * 2 + (part + 1))
                nc.vector.scalar_tensor_tensor(out=rt1[a32, tok], in0=ps[a32, bank, :], scalar=QK_SCALE,
                                               in1=tab[a32, tok], op0=ALU.mult, op1=ALU.mult)
                ch.link(nc.vector.scalar_tensor_tensor(out=rt2[a32, tok], in0=ps[b32, bank, :], scalar=QK_SCALE,
                                                       in1=tab[b32, tok], op0=ALU.mult, op1=ALU.mult))
                nc.vector.tensor_tensor(qh[a32, par, tok], rt1[a32, tok], rt2[a32, tok], ALU.add
                                        ).then_inc(sem("proj_read"), 1)

            def maxima(k, step):
                n = (order[k] + 1) * P
                b = 1 + 2 * (k % 2)
                sc = ps[:, b:b + 2, :].rearrange("p a b -> p (a b)")
                dve.wait_ge(sem("scores"), step + 1)
                if not isinstance(step, int) or step >= 1:
                    dve.wait_ge(sem("probs"), step)
                ch.link(nc.vector.tensor_tensor(sc[:, n - P:n], sc[:, n - P:n], maskq, ALU.add))
                nc.vector.tensor_reduce(nmax[:, k % 2:k % 2 + 1], sc[:, 0:n], AX_X, ALU.max,
                                        negate=True).then_inc(sem("nmax"), 1)

            def outputs(p, par, k, step):
                dve.wait_ge(sem("probs"), step + 2)
                ch.link(nc.vector.reciprocal(rinv[:, k % 2:k % 2 + 1], rsum[:, k % 4:k % 4 + 1]))
                dve.wait_ge(sem("o"), step + 3)
                if par == 0:
                    dve.wait_ge(sem("yt"), p * 3 + 1)
                nc.vector.tensor_scalar(opair[:, order[k], par * VH:(par + 1) * VH],
                                        ps[:, 7, 0:VH],
                                        rinv[:, k % 2:k % 2 + 1], None, ALU.mult).then_inc(sem("o_read"), 1)

            def y_lo(p, n):
                _, first, blocks = turns[n]
                tok = slice(first * P, (first + blocks) * P)
                dve.wait_ge(sem("y_hi"), p * 3 + (n + 1))
                hi = ahi[:, bass.ds(p + LRU_T, 1), tok].rearrange("p a b -> p (a b)")
                lo = alo[:, bass.ds(p + LRU_T, 1), tok].rearrange("p a b -> p (a b)")
                nc.vector.tensor_tensor(lo, ps[:, 0, 0:blocks * P], hi.bitcast(F32), ALU.subtract
                                        ).then_inc(sem("y_read"), 1)

            def head_pair(p, last=False):
                for i in range(16):
                    par, k = i // 8, i % 8
                    if not (last and i >= 14):
                        maxima((i + 2) % 8, p * 16 + (i + 2))
                    if k < 2 and not (last and par == 1):
                        rotate(p * 2 + par + 1, 1 - par, k)
                    outputs(p, par, k, p * 16 + i)
                    for n, (slot, _, _) in enumerate(turns):
                        if par == 1 and k == min(slot + 1, 7):
                            y_lo(p, n)

            for part in range(2):
                rotate(0, 0, part, first_banks[part])
            for i in range(2):
                maxima(i, i)
            with dve.Fori(0, HEADS // 2 - 1) as p:
                ch.enter(p, 36)
                head_pair(p)
            ch.leave(HEADS // 2 - 1)
            head_pair(HEADS // 2 - 1, last=True)
            dve_out(dve, ch, "L0", T_L0_OUT, 32, "F0n")
            dve_norm(dve, ch, "F0n", "f_g0")
            dve_mlp(dve, ch, "F0", T_FFN0, 0, "n1")

            dve.sem_inc(sem("sigo"), 4)
            dve.sem_inc(sem("L1res"), 4)
            dve_norm(dve, ch, "n1", "o_g")
            dve.wait_ge(sem("wg_hi"), 1)
            nc.vector.tensor_tensor(wglo[:], wgs[:], wghi[:].bitcast(F32), ALU.subtract).then_inc(sem("wg_split"), 1)
            dve.wait_ge(sem("g_pre"), 1)
            nc.vector.tensor_tensor(gz, ps[:, 6, 0:8 * TT], pcol("gate_b", 0, 8 * TT), ALU.add
                                    ).then_inc(sem("g_z"), 1)
            dve.wait_ge(sem("g_cum"), 1)
            tv = gt.rearrange("p (c g) -> p c g", c=TT)
            nc.vector.scalar_tensor_tensor(out=ga.rearrange("p (c g) -> p c g", c=TT), in0=tv[:, :, 0:MH],
                                           scalar=GATE_CAP, in1=ps[:, 5, 0:32].rearrange("p (c g) -> p c g", c=TT),
                                           op0=ALU.mult, op1=ALU.add).then_inc(sem("g_a"), 1)
            nc.vector.tensor_copy(gnb, ps[:, 5, 0:32]).then_inc(sem("g_a"), 1)
            dve.wait_ge(sem("g_turned"), 1)
            ch.link(nc.vector.tensor_copy(gaT[0:32, :], ps[0:32, 6, 0:P]))
            nc.vector.tensor_tensor_scan(gAT[0:32, :], gaT[0:32, :], gaT[0:32, :], -BIG, ALU.max, ALU.max
                                         ).then_inc(sem("g_max"), 1)
            nc.vector.tensor_copy(g_last, ps[0:32, 6, 2 * P - 1:2 * P]).then_inc(sem("g_max"), 1)
            dve.wait_ge(sem("g_rows"), 1)
            nc.vector.memset(ginfo[0:1, 256:260], 0.0)
            ch.link(nc.vector.tensor_copy(g_row, ps[0:1, 7, 0:64]))
            for h in range(MH):
                ch.add(nc.vector.tensor_tensor_scan(m_next[:, h::MH], g_row[:, h:32:MH], g_row[:, 32 + h:64:MH], 0.0,
                                                    ALU.max, ALU.subtract))
            ch.wait(ch.n)
            nc.vector.tensor_tensor(ml_row, m_row, g_row[:, 0:32], ALU.max).then_inc(sem("g_m"), 1)
            dve.wait_ge(sem("g_spread"), 1)
            ch.link(nc.vector.tensor_copy(g_mcol, ps[0:32, 7, 64:65]))
            ch.link(nc.vector.tensor_copy(gz, ps[:, 7, 128:192]))
            nc.vector.tensor_scalar(gMT[0:32, :], gAT[0:32, :], g_mcol, None, ALU.max).then_inc(sem("g_MT"), 1)
            dve.wait_ge(sem("g_M"), 1)
            m_tok = ps[:, 7, 256:288]
            nc.vector.tensor_tensor(g_exp[:, 0:32], gz[:, 0:32], m_tok, ALU.subtract)
            nc.vector.tensor_tensor(g_exp[:, 32:64], gnb, m_tok, ALU.subtract)
            nc.vector.tensor_tensor(g_exp[:, 64:96], ga, gz[:, 32:64], ALU.subtract)
            nc.vector.tensor_tensor(g_exp[:, 96:128], gz[:, 0:32], gz[:, 32:64], ALU.subtract
                                    ).then_inc(sem("g_E"), 1)
            dve.wait_ge(sem("spilled"), 16)
            ch.link(nc.vector.memset(vaug[:, :, :, MV:MVA], 1.0))
            nc.vector.memset(cst[:, :, :], 0.0).then_inc(sem("cst0"), 1)

            def stab_rows(c):
                if c == 0:
                    dve.wait_ge(sem("g_MT"), 1)
                else:
                    dve.wait_ge(sem("m_bc"), c)
                for h in range(MH):
                    ins = nc.vector.tensor_scalar(mtx[0:32, h * P:(h + 1) * P], gMT[0:32, :],
                                                  ident[0:32, 4 * c + h:4 * c + h + 1], None, ALU.mult)
                ins.then_inc(sem("mtx"), 1)

            def weights(c):
                dve.wait_ge(sem("mw"), 4 * c + 4)
                dve.wait_ge(sem("m_qk"), c + 1)
                if c >= 2:
                    dve.wait_ge(sem("m_kv"), 4 * c - 4)
                nc.vector.tensor_tensor(msw[:, c % 2, :], ps[:, 1, :], mw[:, c % 2, :], ALU.mult
                                        ).then_inc(sem("msw"), 1)
                dve.wait_ge(sem("m_kt"), c + 1)
                for h in range(MH):
                    n = 4 * c + h
                    nc.vector.tensor_scalar(mkw[:, c % 2, h * P:(h + 1) * P], ps[:, 2, h * P:(h + 1) * P],
                                            g_exp[:, 64 + n:65 + n], None, ALU.mult).then_inc(sem("mkw"), 1)

            def gather(c, blocks):
                for b in blocks:
                    dve.wait_ge(sem("m_turned"), 2 * c + b + 1)
                    for i in range(4):
                        h, e = 2 * b + i // 2, i % 2
                        nc.vector.tensor_scalar(vaug[:, c, h, e * P:(e + 1) * P], ps[:, 7, i * P:(i + 1) * P],
                                                pcol("out_g", 2 * h + e), None, ALU.mult).then_inc(sem("m_y"), 1)

            stab_rows(0)
            dve.wait_ge(sem("g_e"), 1)
            for c in range(2):
                weights(c)
                stab_rows(c + 1)
            for c in range(TT):
                if c >= 1:
                    dve.wait_ge(sem("m_hn"), c)
                for h in range(MH):
                    n = 4 * c + h
                    dve.wait_ge(sem("m_inter_read"), n + 1)
                    dve.wait_ge(sem("m_num"), n + 1)
                    nc.vector.tensor_tensor(mnum[:, h, 0:MV + 1], ps[:, 3 + h % 2, 0:MV + 1], mtmp[:, 0:MV + 1],
                                            ALU.add).then_inc(sem("m_num_read"), 1)
                    dve.wait_ge(sem("m_kv"), n + 1)
                    nc.vector.scalar_tensor_tensor(out=cst[:, h, 0:MV + 1], in0=cst[:, h, 0:MV + 1],
                                                   scalar=g_exp[:, 96 + n:97 + n], in1=ps[:, 6, 0:MV + 1],
                                                   op0=ALU.mult, op1=ALU.add).then_inc(sem("m_state"), 1)
                    if c >= 1 and h == 2:
                        gather(c - 1, (0,))
                if 1 <= c < TT - 2:
                    stab_rows(c + 2)
                if c >= 1:
                    gather(c - 1, (1,))
                dve.wait_ge(sem("m_num_read"), 4 * c + 4)
                ch.link(nc.vector.scalar_tensor_tensor(out=mden, in0=mnum[:, :, MV], scalar=-1.0,
                                                       in1=mnum[:, :, MV], op0=ALU.mult, op1=ALU.max))
                ch.link(nc.vector.tensor_tensor(mden, mden, g_exp[:, 32 + 4 * c:36 + 4 * c], ALU.max))
                ch.link(nc.vector.reciprocal(mrd, mden))
                ch.link(nc.vector.tensor_tensor(mt2, mrd, mrd, ALU.mult))
                dve.wait_ge(sem("m_sq"), 4 * c + 4)
                nc.vector.tensor_tensor(mt2, mt2, mss, ALU.mult).then_inc(sem("m_v"), 1)
                if c + 2 < TT:
                    weights(c + 2)
                dve.wait_ge(sem("m_sd"), c + 1)
                ch.link(nc.vector.reciprocal(mrs, msd))
                ch.link(nc.vector.tensor_tensor(msc, mrs, mrd, ALU.mult))
                if c >= 1:
                    dve.wait_ge(sem("m_turned"), 2 * c)
                for h in range(MH):
                    ins = nc.vector.tensor_scalar(mhn[:, h, :], mnum[:, h, 0:MV], msc[:, h:h + 1], None, ALU.mult)
                ins.then_inc(sem("m_hn"), 1)
            gather(TT - 1, range(2))
            for m in range(KT):
                for s in range(2):
                    n = 2 * m + s
                    dve.wait_ge(sem("sigo"), n + 5)
                    y = vaug[:, 4 * s:4 * s + 4, m // 2, (m % 2) * P:(m % 2 + 1) * P]
                    nc.vector.tensor_tensor(y, y, sigo[:, s, :].rearrange("p (c t) -> p c t", c=4), ALU.mult
                                            ).then_inc(sem("y_gated"), 1)
            for m in range(KT):
                dve.wait_ge(sem("L1hi"), m + 1)
                nc.vector.tensor_tensor(alo[:, m, :].rearrange("p (c t) -> p c t", c=TT),
                                        vaug[:, :, m // 2, (m % 2) * P:(m % 2 + 1) * P],
                                        ahi[:, m, :].bitcast(F32).rearrange("p (c t) -> p c t", c=TT),
                                        ALU.subtract).then_inc(sem("L1mix"), 1)
            dve_out(dve, ch, "L1", T_L1_OUT, 48, "F1n")
            dve_norm(dve, ch, "F1n", "f_g1")
            dve_mlp(dve, ch, "F1", T_FFN1, 1, "nf")
            for s in range(2):
                dve.wait_ge(sem("norm_bc"), nbase("nf", "half") + s + 1)
                for k in range(KT):
                    h = hT[:, k, halves[s]]
                    nc.vector.scalar_tensor_tensor(out=h, in0=h, scalar=pcol("fin_g", k),
                                                   in1=ps[:, norm_banks["nf"][s], :], op0=ALU.mult, op1=ALU.mult
                                                   ).then_inc(sem("fin_ready"), 1)
                    if s == 0 and k == 2:
                        dve_diagonal(dve, ch, "nf", 1, diag)


def _m_tile(w, cols):
    k = w.shape[0] // P
    return w[:, cols].reshape(k, P, P).transpose(1, 0, 2).reshape(P, k * P)


def _mlp_tiles(up, down):
    def ups(f):
        return [_m_tile(up, slice(f * P, (f + 1) * P)), _m_tile(up, slice(D_FF + f * P, D_FF + (f + 1) * P))]

    tiles = ups(0)
    for g in range(FG):
        tiles += ups(2 * g + 1)
        if g < FG - 1:
            tiles += ups(2 * g + 2)
        tiles += [down[(2 * g + j) * P:(2 * g + j + 1) * P, :] for j in range(2)]
    return tiles


def kernel(**inputs):
    import concourse.bacc as bacc
    from concourse.bass_utils import run_bass_kernel_spmd

    a = {k: np.asarray(v) for k, v in inputs.items()}
    w0, w1 = a["e_w_in"][0], a["o_w_in"][0]
    tiles = []
    for j in range(LRU_T):
        tiles += [_m_tile(w0, slice(j * P, (j + 1) * P)), _m_tile(w0, slice(LRU_W + j * P, LRU_W + (j + 1) * P))]
    q0 = 2 * LRU_W
    kv0 = q0 + Q_LORA
    r0 = kv0 + KV_LORA
    half = ROPE // 2
    tiles += [_m_tile(w0, slice(kv0, kv0 + P)), _m_tile(w0, slice(q0, q0 + P)), _m_tile(w0, slice(q0 + P, q0 + 2 * P))]
    rot = np.concatenate([np.zeros((D, NOPE), np.float32), w0[:, r0:r0 + ROPE], w0[:, r0 + half:r0 + ROPE],
                          w0[:, r0:r0 + half]], axis=1)
    tiles.append(_m_tile(rot, slice(0, P)))
    tiles += [_m_tile(a["e_w_out"][0], slice(m * P, (m + 1) * P)) for m in range(KT)]
    tiles += _mlp_tiles(a["f_w_up"][0], a["f_w_down"][0])
    c1 = MH * MQK
    for h in range(MH):
        tiles += [_m_tile(w1, slice(h * P, (h + 1) * P)), _m_tile(w1, slice(c1 + h * P, c1 + (h + 1) * P))]
    for n in range(2):
        for j in range(4):
            v = w1[2 * j * P:(2 * j + 2) * P, 2 * c1 + n * HALF:2 * c1 + (n + 1) * HALF]
            tiles.append(v.reshape(2, P, HALF).transpose(1, 0, 2).reshape(P, 2 * HALF))
    o0 = 2 * c1 + MH * MV
    tiles += [_m_tile(w1, slice(o0 + m * P, o0 + (m + 1) * P)) for m in range(KT)]
    tiles += [_m_tile(a["o_w_out"][0], slice(m * P, (m + 1) * P)) for m in range(KT)]
    tiles += _mlp_tiles(a["f_w_up"][1], a["f_w_down"][1])
    assert len(tiles) == TILES, (len(tiles), TILES)
    wt = np.ascontiguousarray(np.concatenate(tiles, axis=0))

    wg = np.zeros((P, KT, P), np.float32)
    wg[:, :, 0:8] = w1[:, o0 + MH * MV:].reshape(KT, P, 8).transpose(1, 0, 2)
    wg = wg.reshape(P, KT * P)
    qb = a["e_w_qb"][0].reshape(Q_LORA, HEADS, QK)
    qb = np.concatenate([qb, qb[:, :, NOPE + half:], qb[:, :, NOPE:NOPE + half]], axis=2)
    wqb = np.ascontiguousarray(qb.reshape(2, P, HEADS * P).transpose(1, 0, 2))
    wkvb = np.ascontiguousarray(a["e_w_kvb"][0])
    wlru = np.zeros((P, LRU_T, 2, P), np.float32)
    for g, name in enumerate(("e_lru_w_a", "e_lru_w_x")):
        for j in range(LRU_T):
            for b in range(2):
                wlru[64 * b:64 * (b + 1), j, g, 64 * b:64 * (b + 1)] = a[name][0, 2 * j + b]
    wlru = wlru.reshape(P, LRU_T, 2 * P)

    def columns(v):
        return v.reshape(-1, P).T

    par = np.zeros((P, NPAR), np.float32)

    def put(name, v):
        par[:, _cols[name]:_cols[name] + v.shape[1]] = v

    put("e_g", columns(a["e_norm_g"][0]))
    put("o_g", columns(a["o_norm_g"][0]))
    put("f_g0", columns(a["f_norm_g"][0]))
    put("f_g1", columns(a["f_norm_g"][1]))
    put("fin_g", columns(a["final_norm_g"]))
    put("q_g", columns(a["e_q_norm_g"][0]))
    put("kv_g", columns(a["e_kv_norm_g"][0]))
    put("out_g", columns(a["o_out_norm_g"][0]))
    lru = [a["e_lru_conv_w"][0, n] for n in range(4)] + [a["e_lru_conv_b"][0], a["e_lru_b_a"][0].reshape(-1),
                                                        a["e_lru_b_x"][0].reshape(-1), a["e_lru_lambda"][0]]
    put("lru", np.stack([columns(v) for v in lru], axis=2).reshape(P, -1))
    put("gate_b", np.broadcast_to(np.tile(np.concatenate([a["o_b_igate"][0], a["o_b_fgate"][0]]), TT), (P, 8 * TT)))
    for l in range(2):
        rows = [a["f_conv_w"][l, n] for n in range(3)] + [a["f_conv_b"][l]]
        parts = [columns(r[g * D_FF:(g + 1) * D_FF]) for g in range(2) for r in rows]
        put(f"conv{l}", np.stack(parts, axis=2).reshape(P, -1))

    con = np.zeros((P, NCON), np.float32)
    i = np.arange(P)
    con[:, C_ID:C_ID + P] = np.eye(P)
    con[:, C_ONE:C_ONE + P] = 1.0
    con[:, C_TRI:C_TRI + P] = i[:, None] <= i[None, :]
    con[:, C_MASKQ:C_MASKQ + P] = -BIG * (i[:, None] < i[None, :])
    con[:, C_MASKS:C_MASKS + P] = BIG * (i[:, None] > i[None, :])
    freq = (10000.0 ** (-np.arange(half) / half)).astype(np.float32)
    con[NOPE:, C_ROPE] = np.tile(freq, 4)
    con[NOPE:QK, C_ROPE + 1] = 0.25
    con[NOPE:QK, C_ROPE + 2] = np.pi / 2
    con[NOPE:, C_ROPE + 3] = 1.0
    con[QK:QK + half, C_ROPE + 3] = -1.0

    xt = np.ascontiguousarray(a["x"][0].T)
    pos = np.ascontiguousarray(np.broadcast_to(a["positions"][0][None, :], (P, S)))

    nc = bacc.Bacc("TRN2", target_bir_lowering=False, num_devices=1)
    arrays = {"wt": wt, "xt": xt, "pos": pos, "par": par, "con": con, "wqb": wqb, "wkvb": wkvb, "wlru": wlru,
              "wg": wg}
    aps = {n: nc.dram_tensor("in_" + n, v.shape, mybir.dt.from_np(v.dtype), kind="ExternalInput").ap()
           for n, v in arrays.items()}
    spill = nc.dram_tensor("spill", (P, KT * S), F32, kind="Internal").ap()
    out = nc.dram_tensor("out_0", (D, S), F32, kind="ExternalOutput").ap()
    build(nc, spill=spill, out=out, **aps)
    r = run_bass_kernel_spmd(nc, [{"in_" + n: v for n, v in arrays.items()}], core_ids=[0])
    return np.ascontiguousarray(r.results[0]["out_0"].T)[None]
```
